# Optimizing a Trainium2 kernel written in Bass

```python
import math, functools
import jax, jax.numpy as jnp
from jax import lax
import numpy as np

D_MODEL = 1024
BATCH = 1
SEQ = 512
DEPTH = 1
DEC_BATCH = 8
DEC_SEQ = 4
PAST_LEN = 1024
PAGE_SIZE = 128

EPS = 1e-6
SSD_HEAD_DIM = 64
SSD_INNER = D_MODEL
SSD_HEADS = SSD_INNER // SSD_HEAD_DIM
SSD_GROUPS = 4
SSD_HPG = SSD_HEADS // SSD_GROUPS
SSD_STATE = 128
SSD_CONV = 4
SSD_CHUNK = 128
SSD_CONV_DIM = SSD_INNER + 2 * SSD_GROUPS * SSD_STATE
ATT_HEADS = 8
ATT_HEAD_DIM = 128
ATT_KV_HEADS = 2
ATT_GROUP = ATT_HEADS // ATT_KV_HEADS
IDX_HEADS = 8
IDX_DIM = 64
TOPK_MAX = 256
Q_BLOCK = 128
N_BUCKETS = 32
MAX_DISTANCE = 128
SC_WIDTH = D_MODEL
SC_KERNEL = 3
N_EXPERT_GROUPS = 4
EXPERTS_PER_GROUP = 8
N_EXPERTS = N_EXPERT_GROUPS * EXPERTS_PER_GROUP
EXPERT_FF = 256
TOP_K_EXPERTS = 2

IN_SIZES = (SSD_INNER, SSD_CONV_DIM, SSD_HEADS,
            ATT_HEADS * ATT_HEAD_DIM, ATT_KV_HEADS * ATT_HEAD_DIM, ATT_KV_HEADS * ATT_HEAD_DIM,
            IDX_HEADS * IDX_DIM, IDX_DIM, IDX_HEADS,
            SC_WIDTH, SC_WIDTH, SC_WIDTH,
            3 * D_MODEL)
N_IN = sum(IN_SIZES)

kernel_name = "hybrid_ssd_dsa_shortconv_hmoe_step"

F32 = jnp.float32

def rms_norm(x, w):
    xf = x.astype(F32)
    y = xf * lax.rsqrt(jnp.mean(xf * xf, axis=-1, keepdims=True) + EPS)
    return (y * w.astype(F32)).astype(x.dtype)

def ada_modulation(c, w, b):
    m = jax.nn.silu(c) @ w + b
    return jnp.split(m[:, None, :], 6, axis=-1)

def causal_dwconv(u, prev, w):
    k = w.shape[0]
    n = u.shape[1]
    full = jnp.concatenate([prev.astype(u.dtype), u], axis=1)
    out = sum(full[:, i:i + n] * w[i] for i in range(k))
    return out, full[:, full.shape[1] - (k - 1):]

def t5_bucket(dist):
    n = jnp.maximum(dist, 0)
    max_exact = N_BUCKETS // 2
    large = max_exact + (jnp.log(jnp.maximum(n, 1).astype(F32) / max_exact)
                         / math.log(MAX_DISTANCE / max_exact) * (N_BUCKETS - max_exact)).astype(jnp.int32)
    large = jnp.minimum(large, N_BUCKETS - 1)
    return jnp.where(n < max_exact, n, large)

def ssd_scan(x, dt, a, bm, cm, h0, chunk):
    b, l, g, j, p = x.shape
    n = bm.shape[-1]
    c = l // chunk
    dt = dt.astype(F32)
    adt = (dt * a).reshape(b, c, chunk, g, j)
    xdt = (x.astype(F32) * dt[..., None]).reshape(b, c, chunk, g, j, p)
    bm = bm.astype(F32).reshape(b, c, chunk, g, n)
    cm = cm.astype(F32).reshape(b, c, chunk, g, n)
    cs = jnp.cumsum(adt, axis=2)
    causal = jnp.tril(jnp.ones((chunk, chunk), dtype=bool))
    seg = cs[:, :, :, None] - cs[:, :, None, :]
    decay_ls = jnp.exp(jnp.where(causal[None, None, :, :, None, None], seg, -jnp.inf))
    cb = jnp.einsum('bclgn,bcsgn->bclsg', cm, bm)
    y_diag = jnp.einsum('bclsgj,bcsgjp->bclgjp', cb[..., None] * decay_ls, xdt)
    decay_to_end = jnp.exp(cs[:, :, -1:] - cs)
    chunk_states = jnp.einsum('bcsgn,bcsgj,bcsgjp->bcgjpn', bm, decay_to_end, xdt)
    chunk_decay = jnp.exp(cs[:, :, -1])

    def step(h, inp):
        st, dec = inp
        return h * dec[..., None, None] + st, h

    h_final, h_in = lax.scan(step, h0.astype(F32),
                             (jnp.moveaxis(chunk_states, 1, 0), jnp.moveaxis(chunk_decay, 1, 0)))
    h_in = jnp.moveaxis(h_in, 0, 1)
    y_off = jnp.einsum('bclgn,bcgjpn,bclgj->bclgjp', cm, h_in, jnp.exp(cs))
    return (y_diag + y_off).reshape(b, l, g, j, p), h_final

def ssd_mixer(z, xbc, dt_raw, conv_prev, h0, conv_w, conv_b, dt_bias, a_log, d_skip, norm_w):
    b, l, _ = z.shape
    xbc, conv_new = causal_dwconv(xbc, conv_prev, conv_w)
    xbc = jax.nn.silu(xbc + conv_b)
    xs, bm, cm = jnp.split(xbc, [SSD_INNER, SSD_INNER + SSD_GROUPS * SSD_STATE], axis=-1)
    dt = jax.nn.softplus(dt_raw.astype(F32) + dt_bias.astype(F32))
    a = -jnp.exp(a_log.astype(F32))
    chunk = SSD_CHUNK if l % SSD_CHUNK == 0 else l
    xs5 = xs.reshape(b, l, SSD_GROUPS, SSD_HPG, SSD_HEAD_DIM)
    y, h_final = ssd_scan(xs5, dt.reshape(b, l, SSD_GROUPS, SSD_HPG), a.reshape(SSD_GROUPS, SSD_HPG),
                          bm.reshape(b, l, SSD_GROUPS, SSD_STATE), cm.reshape(b, l, SSD_GROUPS, SSD_STATE),
                          h0.reshape(b, SSD_GROUPS, SSD_HPG, SSD_HEAD_DIM, SSD_STATE), chunk)
    y = y + d_skip.astype(F32).reshape(SSD_GROUPS, SSD_HPG, 1) * xs5.astype(F32)
    gy = (y.reshape(b, l, SSD_INNER) * jax.nn.silu(z.astype(F32))).reshape(b, l, SSD_GROUPS, -1)
    gy = gy * lax.rsqrt(jnp.mean(gy * gy, axis=-1, keepdims=True) + EPS)
    out = (gy.reshape(b, l, SSD_INNER) * norm_w.astype(F32)).astype(z.dtype)
    return out, conv_new, h_final.reshape(b, SSD_HEADS, SSD_HEAD_DIM, SSD_STATE).astype(z.dtype)

def indexer_topk(qi, wi, ki, q_pos, k_pos, topk):
    s = jax.nn.relu(jnp.einsum('bqhd,bld->bqlh', qi, ki).astype(F32) * IDX_DIM ** -0.5)
    score = jnp.einsum('bqlh,bqh->bql', s, wi.astype(F32)) * IDX_HEADS ** -0.5
    score = jnp.where(k_pos[None, None, :] <= q_pos[None, :, None], score, -jnp.inf)
    _, idx = lax.top_k(score, topk)
    return idx

def attend_selected(q, k_sel, v_sel, key_pos, q_pos, rel_bias):
    b, nq = q.shape[:2]
    nsel = k_sel.shape[2]
    qg = q.reshape(b, nq, ATT_KV_HEADS, ATT_GROUP, ATT_HEAD_DIM)
    logits = jnp.einsum('bqhgd,bqnhd->bqhgn', qg, k_sel).astype(F32) * ATT_HEAD_DIM ** -0.5
    dist = q_pos[None, :, None] - key_pos
    bias = rel_bias[t5_bucket(dist)].astype(F32)
    bias = bias.reshape(b, nq, nsel, ATT_KV_HEADS, ATT_GROUP).transpose(0, 1, 3, 4, 2)
    valid = (dist >= 0)[:, :, None, None, :]
    p = jax.nn.softmax(jnp.where(valid, logits + bias, -jnp.inf), axis=-1).astype(v_sel.dtype)
    out = jnp.einsum('bqhgn,bqnhd->bqhgd', p, v_sel)
    return out.reshape(b, nq, ATT_HEADS * ATT_HEAD_DIM)

def dsa_prompt(q, k, v, qi, ki, wi, rel_bias):
    b, s = q.shape[:2]
    topk = min(TOPK_MAX, s // 4)
    nb = s // Q_BLOCK
    k_pos = jnp.arange(s, dtype=jnp.int32)
    take = jax.vmap(lambda arr, ix: arr[ix])

    def blk(args):
        i, qb, qib, wib = args
        q_pos = i * Q_BLOCK + jnp.arange(Q_BLOCK, dtype=jnp.int32)
        idx = indexer_topk(qib, wib, ki, q_pos, k_pos, topk)
        return attend_selected(qb, take(k, idx), take(v, idx), idx, q_pos, rel_bias)

    to_blocks = lambda a: a.reshape(b, nb, Q_BLOCK, *a.shape[2:]).swapaxes(0, 1)
    out = lax.map(blk, (jnp.arange(nb, dtype=jnp.int32), to_blocks(q), to_blocks(qi), to_blocks(wi)))
    return out.swapaxes(0, 1).reshape(b, s, ATT_HEADS * ATT_HEAD_DIM)

def dsa_sample(q, k, v, qi, ki, wi, cache_k, cache_v, cache_kidx, page_table, rel_bias):
    b, n_new = q.shape[:2]
    past = page_table.shape[1] * PAGE_SIZE
    total = past + n_new
    topk = min(TOPK_MAX, total // 4)
    q_pos = past + jnp.arange(n_new, dtype=jnp.int32)
    k_pos = jnp.arange(total, dtype=jnp.int32)
    ki_past = cache_kidx[page_table].reshape(b, past, IDX_DIM).astype(ki.dtype)
    idx = indexer_topk(qi, wi, jnp.concatenate([ki_past, ki], axis=1), q_pos, k_pos, topk)
    in_past = (idx < past)[..., None, None]
    pidx = jnp.minimum(idx, past - 1)
    phys = jax.vmap(lambda pt, ix: pt[ix])(page_table, pidx // PAGE_SIZE)
    off = pidx % PAGE_SIZE
    nidx = jnp.clip(idx - past, 0, n_new - 1)
    take = jax.vmap(lambda arr, ix: arr[ix])
    k_sel = jnp.where(in_past, cache_k[phys, off].astype(k.dtype), take(k, nidx))
    v_sel = jnp.where(in_past, cache_v[phys, off].astype(v.dtype), take(v, nidx))
    return attend_selected(q, k_sel, v_sel, idx, q_pos, rel_bias)

def hier_moe(h, wg, we, w_gate, w_up, w_down):
    b, l, _ = h.shape
    pg = jax.nn.softmax((h @ wg).astype(F32), axis=-1)
    g_sel = jnp.argmax(pg, axis=-1)
    pg_sel = jnp.max(pg, axis=-1)
    fine = (h @ we).astype(F32).reshape(b, l, N_EXPERT_GROUPS, EXPERTS_PER_GROUP)
    gidx = jnp.broadcast_to(g_sel[..., None, None], (b, l, 1, EXPERTS_PER_GROUP))
    pf = jax.nn.softmax(jnp.take_along_axis(fine, gidx, axis=2)[:, :, 0], axis=-1)
    top_p, top_i = lax.top_k(pf, TOP_K_EXPERTS)
    wts = pg_sel[..., None] * top_p / jnp.sum(top_p, axis=-1, keepdims=True)
    expert_id = g_sel[..., None] * EXPERTS_PER_GROUP + top_i
    combine = jnp.sum(jax.nn.one_hot(expert_id, N_EXPERTS, dtype=F32) * wts[..., None], axis=-2).astype(h.dtype)
    gate = jnp.einsum('bld,edf->blef', h, w_gate)
    up = jnp.einsum('bld,edf->blef', h, w_up)
    act = jax.nn.silu(gate) * up * combine[..., None]
    return jnp.einsum('blef,efd->bld', act, w_down)

def parallel_mixer(h, lw, attend, ssm_conv_prev, ssm_h0, sc_conv_prev):
    b, l, _ = h.shape
    split_at = np.cumsum(IN_SIZES)[:-1].tolist()
    (z, xbc, dt_raw, q, k, v, qi, ki, wi, gb, gc, hv, gate_logits) = jnp.split(h @ lw['w_in'], split_at, axis=-1)
    y_a, ssm_conv_new, ssm_h = ssd_mixer(z, xbc, dt_raw, ssm_conv_prev, ssm_h0, lw['ssm_conv_w'], lw['ssm_conv_b'],
                                         lw['ssm_dt_bias'], lw['ssm_a_log'], lw['ssm_d'], lw['ssm_norm_w'])
    k = k.reshape(b, l, ATT_KV_HEADS, ATT_HEAD_DIM)
    v = v.reshape(b, l, ATT_KV_HEADS, ATT_HEAD_DIM)
    y_b = attend(q.reshape(b, l, ATT_HEADS, ATT_HEAD_DIM), k, v, qi.reshape(b, l, IDX_HEADS, IDX_DIM), ki, wi)
    u, sc_conv_new = causal_dwconv(gc * hv, sc_conv_prev, lw['sc_conv_w'])
    y_c = gb * u
    g_a, g_b, g_c = jnp.split(jax.nn.sigmoid(gate_logits), 3, axis=-1)
    merged = g_a * (y_a @ lw['w_out_ssm']) + g_b * (y_b @ lw['w_out_att']) + g_c * (y_c @ lw['w_out_sc'])
    return merged @ lw['w_o'], (k, v, ki, ssm_h, ssm_conv_new, sc_conv_new)

def layer_forward(x, c, lw, attend, ssm_conv_prev, ssm_h0, sc_conv_prev):
    shift1, scale1, gate1, shift2, scale2, gate2 = ada_modulation(c, lw['ada_w'], lw['ada_b'])
    h = rms_norm(x, lw['norm1_w']) * (1 + scale1) + shift1
    mix, new_state = parallel_mixer(h, lw, attend, ssm_conv_prev, ssm_h0, sc_conv_prev)
    x = x + gate1 * mix
    h = rms_norm(x, lw['norm2_w']) * (1 + scale2) + shift2
    x = x + gate2 * hier_moe(h, lw['router_group_w'], lw['router_expert_w'], lw['exp_w_gate'], lw['exp_w_up'], lw['exp_w_down'])
    return x, new_state

def setup_inputs(seed: int = 0) -> dict:
    key = jax.random.key(seed)
    ks = iter(jax.random.split(key, 40))
    nrm = lambda shape, scale: jax.random.normal(next(ks), shape, F32) * scale
    n_pages = PAST_LEN // PAGE_SIZE
    n_pool = (DEC_BATCH * n_pages * 5) // 4
    page_table = jax.random.permutation(next(ks), n_pool)[:DEC_BATCH * n_pages].reshape(DEC_BATCH, n_pages).astype(jnp.int32)
    dt0 = jnp.exp(jax.random.uniform(next(ks), (DEPTH, SSD_HEADS)) * (math.log(0.1) - math.log(1e-3)) + math.log(1e-3))
    return {
        'x_prompt': nrm((BATCH, SEQ, D_MODEL), 1.0),
        'x_sample': nrm((DEC_BATCH, DEC_SEQ, D_MODEL), 1.0),
        'c_prompt': nrm((BATCH, D_MODEL), 1.0),
        'c_sample': nrm((DEC_BATCH, D_MODEL), 1.0),
        'cache_k': nrm((DEPTH, n_pool, PAGE_SIZE, ATT_KV_HEADS, ATT_HEAD_DIM), 1.0),
        'cache_v': nrm((DEPTH, n_pool, PAGE_SIZE, ATT_KV_HEADS, ATT_HEAD_DIM), 1.0),
        'cache_kidx': nrm((DEPTH, n_pool, PAGE_SIZE, IDX_DIM), 1.0),
        'state_ssm': nrm((DEPTH, DEC_BATCH, SSD_HEADS, SSD_HEAD_DIM, SSD_STATE), 0.3),
        'state_ssm_conv': nrm((DEPTH, DEC_BATCH, SSD_CONV - 1, SSD_CONV_DIM), 1.0),
        'state_sc_conv': nrm((DEPTH, DEC_BATCH, SC_KERNEL - 1, SC_WIDTH), 1.0),
        'page_table': page_table,
        'ada_w': nrm((DEPTH, D_MODEL, 6 * D_MODEL), 0.5 * D_MODEL ** -0.5),
        'ada_b': nrm((DEPTH, 6 * D_MODEL), 0.01),
        'norm1_w': 1.0 + nrm((DEPTH, D_MODEL), 0.01),
        'norm2_w': 1.0 + nrm((DEPTH, D_MODEL), 0.01),
        'w_in': nrm((DEPTH, D_MODEL, N_IN), D_MODEL ** -0.5),
        'ssm_conv_w': nrm((DEPTH, SSD_CONV, SSD_CONV_DIM), SSD_CONV ** -0.5),
        'ssm_conv_b': nrm((DEPTH, SSD_CONV_DIM), 0.01),
        'ssm_dt_bias': dt0 + jnp.log(-jnp.expm1(-dt0)),
        'ssm_a_log': jnp.log(jax.random.uniform(next(ks), (DEPTH, SSD_HEADS), minval=1.0, maxval=16.0)),
        'ssm_d': 1.0 + nrm((DEPTH, SSD_HEADS), 0.1),
        'ssm_norm_w': 1.0 + nrm((DEPTH, SSD_INNER), 0.01),
        'sc_conv_w': nrm((DEPTH, SC_KERNEL, SC_WIDTH), SC_KERNEL ** -0.5),
        'rel_bias': nrm((N_BUCKETS, ATT_HEADS), 0.5),
        'w_out_ssm': nrm((DEPTH, SSD_INNER, D_MODEL), SSD_INNER ** -0.5),
        'w_out_att': nrm((DEPTH, ATT_HEADS * ATT_HEAD_DIM, D_MODEL), (ATT_HEADS * ATT_HEAD_DIM) ** -0.5),
        'w_out_sc': nrm((DEPTH, SC_WIDTH, D_MODEL), SC_WIDTH ** -0.5),
        'w_o': nrm((DEPTH, D_MODEL, D_MODEL), D_MODEL ** -0.5),
        'router_group_w': nrm((DEPTH, D_MODEL, N_EXPERT_GROUPS), D_MODEL ** -0.5),
        'router_expert_w': nrm((DEPTH, D_MODEL, N_EXPERTS), D_MODEL ** -0.5),
        'exp_w_gate': nrm((DEPTH, N_EXPERTS, D_MODEL, EXPERT_FF), D_MODEL ** -0.5),
        'exp_w_up': nrm((DEPTH, N_EXPERTS, D_MODEL, EXPERT_FF), D_MODEL ** -0.5),
        'exp_w_down': nrm((DEPTH, N_EXPERTS, EXPERT_FF, D_MODEL), EXPERT_FF ** -0.5),
        'final_norm_w': 1.0 + nrm((D_MODEL,), 0.01),
    }

def reference(x_prompt, x_sample, c_prompt, c_sample, cache_k, cache_v, cache_kidx, state_ssm, state_ssm_conv,
              state_sc_conv, page_table, ada_w, ada_b, norm1_w, norm2_w, w_in, ssm_conv_w, ssm_conv_b, ssm_dt_bias,
              ssm_a_log, ssm_d, ssm_norm_w, sc_conv_w, rel_bias, w_out_ssm, w_out_att, w_out_sc, w_o,
              router_group_w, router_expert_w, exp_w_gate, exp_w_up, exp_w_down, final_norm_w):
    xp, xs = x_prompt, x_sample
    bp = xp.shape[0]
    prompt_rows = [[] for _ in range(6)]
    sample_rows = [[] for _ in range(6)]
    prompt_attn = functools.partial(dsa_prompt, rel_bias=rel_bias)
    for l in range(DEPTH):
        lw = {'ada_w': ada_w[l], 'ada_b': ada_b[l], 'norm1_w': norm1_w[l], 'norm2_w': norm2_w[l], 'w_in': w_in[l],
              'ssm_conv_w': ssm_conv_w[l], 'ssm_conv_b': ssm_conv_b[l], 'ssm_dt_bias': ssm_dt_bias[l],
              'ssm_a_log': ssm_a_log[l], 'ssm_d': ssm_d[l], 'ssm_norm_w': ssm_norm_w[l], 'sc_conv_w': sc_conv_w[l],
              'w_out_ssm': w_out_ssm[l], 'w_out_att': w_out_att[l], 'w_out_sc': w_out_sc[l], 'w_o': w_o[l],
              'router_group_w': router_group_w[l], 'router_expert_w': router_expert_w[l],
              'exp_w_gate': exp_w_gate[l], 'exp_w_up': exp_w_up[l], 'exp_w_down': exp_w_down[l]}
        xp, st_p = layer_forward(
            xp, c_prompt, lw, prompt_attn,
            jnp.zeros((bp, SSD_CONV - 1, SSD_CONV_DIM), xp.dtype),
            jnp.zeros((bp, SSD_HEADS, SSD_HEAD_DIM, SSD_STATE), xp.dtype),
            jnp.zeros((bp, SC_KERNEL - 1, SC_WIDTH), xp.dtype))
        sample_attn = functools.partial(dsa_sample, cache_k=cache_k[l], cache_v=cache_v[l], cache_kidx=cache_kidx[l],
                                        page_table=page_table, rel_bias=rel_bias)
        xs, st_s = layer_forward(xs, c_sample, lw, sample_attn, state_ssm_conv[l], state_ssm[l], state_sc_conv[l])
        for i in range(6):
            prompt_rows[i].append(st_p[i])
            sample_rows[i].append(st_s[i])
    y_prompt = rms_norm(xp, final_norm_w)
    y_sample = rms_norm(xs, final_norm_w)
    k_p, v_p, kidx_p, ssm_p, ssm_conv_p, sc_conv_p = [jnp.stack(r) for r in prompt_rows]
    k_s, v_s, kidx_s, ssm_s, ssm_conv_s, sc_conv_s = [jnp.stack(r) for r in sample_rows]
    return (y_prompt, y_sample, k_p, v_p, kidx_p, ssm_p, ssm_conv_p, sc_conv_p,
            k_s, v_s, kidx_s, ssm_s, ssm_conv_s, sc_conv_s)


_drawn_inputs = setup_inputs


def setup_inputs(seed=0):
    import zlib

    import numpy as np

    out = dict(_drawn_inputs(seed))
    spreads = {}
    factors = {'cache_k': 8.15,
     'cache_kidx': 3.376,
     'norm1_w': 4.181,
     'norm2_w': 7.771,
     'ssm_conv_b': 11.56,
     'ssm_d': 5.34,
     'ssm_norm_w': 21.919,
     'rel_bias': 3.667,
     'final_norm_w': 175.109}
    for name, (base, spread) in spreads.items():
        noise = np.random.default_rng([zlib.crc32(name.encode()), seed]).standard_normal(out[name].shape)
        drawn = base * np.exp(spread * noise) if base else spread * noise
        out[name] = __import__('jax').numpy.asarray(drawn.astype(out[name].dtype))
    for name, factor in factors.items():
        out[name] = (out[name] * factor).astype(out[name].dtype)
    return out
```

```python
from contextlib import ExitStack

import numpy as np

import concourse.bass as bass
from concourse import mybir

F32 = mybir.dt.float32
I32 = mybir.dt.int32
U32 = mybir.dt.uint32
ACT = mybir.ActivationFunctionType
ALU = mybir.AluOpType
AX = mybir.AxisListType.X

P = 128
D = 1024
DC = D // P
SEQ = 512
QT = SEQ // P
NB, NS = 8, 4
NEW = NB * NS
NT = SEQ + NEW
HALF = NT // 2
NSEQ = 1 + NB
PAGE = 128
PAGES = 8
PAST = PAGE * PAGES
POOL = 80
KEYS = PAST + NEW
H_ATT, DH, KV = 8, 128, 2
GRP = H_ATT // KV
H_IDX, D_IDX = 8, 64
TOPK_P, TOPK_S = min(256, SEQ // 4), min(256, (PAST + NS) // 4)
H_SSD, P_SSD, N_SSD, G_SSD = 16, 64, 128, 4
HPG = H_SSD // G_SSD
XBC = 16
K_SSD, K_SC = 4, 3
SEG_P, SEG_S = K_SSD - 1 + SEQ, K_SSD - 1 + NS
W_XB = SEG_P + NB * SEG_S
SSEG_P, SSEG_S = K_SC - 1 + SEQ, K_SC - 1 + NS
W_SC = SSEG_P + NB * SSEG_S
NE, FF = 32, 256
NG, EPG = 4, 8
EPS = 1e-6
NEG_ADD = -1e30
NOT_KEY = -1e38
CHOSEN = -3e38
REL = 384
REL_TOP = 255
RING = 8

T_ADA = 0
T_KI = 16
T_QI = T_KI + 1
T_SMALL = T_QI + 4
T_K = T_SMALL + 1
T_V = T_K + 2
T_Q = T_V + 2
T_Z = T_Q + 8
T_XBC = T_Z + 8
T_SC = T_XBC + 16
T_ADA2 = T_SC + 24
T_MERGE = T_ADA2 + 32
T_O = T_MERGE + 48
T_END = T_O + 8

O_Z, O_XBC, O_DT, O_Q, O_K, O_V, O_QI, O_KI, O_WI, O_GB, O_GC, O_HV, O_GATE = (
    0, 1024, 3072, 3088, 4112, 4368, 4624, 5136, 5200, 5208, 6232, 7256, 8280)


def t5_bucket_of(dist):
    n = np.maximum(dist, 0)
    large = 16 + np.floor(np.log(np.maximum(n, 1) / 16.0) / np.log(8.0) * 16 + 1e-9).astype(np.int64)
    return np.where(n < 16, n, np.minimum(large, 31))


def shape_constants():
    i = np.arange(P)
    row_b, row_h, row_t = i // 32, (i // 4) % 8, i % 4
    new_b, new_t = np.arange(NEW) // NS, np.arange(NEW) % NS
    same = new_b[:, None] == new_b[None, :]
    parts = {}

    def put(name, a):
        full = np.zeros((P,) + a.shape[1:], np.float32)
        full[:a.shape[0]] = a
        parts[name] = full.reshape(P, -1)

    put("ident", np.eye(P))
    put("ones", np.ones((P, P)))
    put("upto", (i[:, None] <= i[None, :]))
    put("after", (i[:, None] > i[None, :]))
    put("future", np.where(i[None, :] > i[:, None], NOT_KEY, 0.0))
    put("future_add", np.where(i[None, :] > i[:, None], NEG_ADD, 0.0))
    put("upto_new", same & (new_t[:, None] <= new_t[None, :]))
    put("after_new", same & (new_t[:, None] > new_t[None, :]))
    put("new_keys", np.where(same & (new_t[None, :] <= new_t[:, None]), 0.0, NOT_KEY))
    put("head_rows", (np.arange(8)[:, None] == row_h[None, :]))
    sel = np.stack([((row_b[:, None] + 4 * a) == new_b[None, :]) & (row_t[:, None] == new_t[None, :])
                    for a in range(2)], 1)
    put("row_token", sel.reshape(P, -1))
    put("token_row", np.transpose(sel, (2, 1, 0)).reshape(NEW, -1))
    put("in_seq", (new_b[:, None] == np.arange(NB)[None, :]))
    dist = REL_TOP - np.arange(REL)
    onehot = (t5_bucket_of(dist)[None, :] == np.arange(32)[:, None]).astype(np.float32)
    onehot[31] -= 1.0
    put("rel_cols", onehot)
    put("iota8", np.broadcast_to(np.arange(8), (P, 8)))
    put("iota32", np.broadcast_to(np.arange(NE), (P, NE)))
    token = np.arange(5)[None, None, :] * P + i[:, None, None]
    put("row_values", 2 * token + np.arange(2)[None, :, None])
    return parts


CONST_AT = {}
_at = 0
for _name, _a in shape_constants().items():
    CONST_AT[_name] = (_at, _a.shape[1])
    _at += _a.shape[1]
CONST_W = _at

PARAM_AT = {}
_at = 0
for _name, _w in (("ada_b", 48), ("norm1", 8), ("norm2", 8), ("final", 8), ("conv_w", XBC * K_SSD),
                  ("conv_b", XBC), ("sc_w", 8 * K_SC), ("dt_bias", H_SSD), ("a_log", H_SSD), ("d_skip", 8),
                  ("ssm_norm", 8), ("rel_bias", H_ATT), ("c", DC * NSEQ), ("router", DC * 36),
                  ("conv_prev", XBC * NB * (K_SSD - 1)), ("sc_prev", 8 * NB * (K_SC - 1))):
    PARAM_AT[_name] = (_at, _w)
    _at += _w
PARAM_W = _at


class Link:

    def __init__(self, eng, sem):
        self.eng, self.sem, self.n = eng, sem, 0

    def __call__(self, ins):
        ins.then_inc(self.sem, 1)
        self.n += 1
        self.eng.wait_ge(self.sem, self.n)


class Arena:

    def __init__(self, tensor, size):
        self.t, self.size = tensor, size

    def at(self, start, *dims, parts=P, base=0):
        n = int(np.prod(dims))
        assert start + n <= self.size, (start, dims, self.size)
        v = self.t[base:base + parts, start:start + n]
        if len(dims) == 2:
            v = v.rearrange("p (a b) -> p a b", b=dims[1])
        if len(dims) == 3:
            v = v.rearrange("p (a b c) -> p a b c", b=dims[1], c=dims[2])
        return v


def build(nc, ins, outs):
    ctx = ExitStack()
    with ctx:
        in_use = []

        def sem(name):
            in_use.append(nc.alloc_semaphore(name=name))
            return in_use[-1]

        def retire(keep):
            nc.clear_and_free_semaphores([s for s in in_use if s not in keep])
            in_use[:] = list(keep)
            nc.all_engine_barrier()

        size = 53120
        A = Arena(ctx.enter_context(nc.sbuf_tensor("arena", [P, size], F32)), size)
        top = [0]

        def take(n):
            top[0] += n
            return top[0] - n

        a_const, a_param = take(CONST_W), take(PARAM_W)

        def const(name, parts=P):
            at, w = CONST_AT[name]
            return A.at(a_const + at, w, parts=parts)

        def param(name, parts=P):
            at, w = PARAM_AT[name]
            return A.at(a_param + at, w, parts=parts)

        mods = A.at(take(48 * NSEQ), 48, NSEQ)
        gain = A.at(take(2 * DC * NSEQ), 2, DC, NSEQ)
        c_silu = A.at(take(DC * NSEQ), DC, NSEQ)
        eps_col = A.at(take(2), 2)
        small = A.at(take(5 * 24), 5, 24)
        a_ring = take(RING * 1024)
        ring = A.at(a_ring, RING, DC * P)
        a_h = take(DC * NT)
        hT = A.at(a_h, DC, NT)
        a_x = take(DC * NT)
        xT = A.at(a_x, DC, NT)
        a_q = take(15 * NT)
        qT, kT, qiT, kiT = (A.at(a_q, 8, NT), A.at(a_q + 8 * NT, 2, NT), A.at(a_q + 10 * NT, 4, NT),
                            A.at(a_q + 14 * NT, NT))
        v_tok = A.at(take(5 * 256), 5, 256)
        a_z = take(8 * NT)
        zT = A.at(a_z, 8, NT)
        a_xb = take(XBC * W_XB)
        xb = A.at(a_xb, XBC, W_XB)
        kidx = A.at(a_xb, NB, PAST, parts=D_IDX)
        a_sc = take(256 + 384 + 512)
        score_at = [None, (a_sc, 256), (a_sc + 256, 384), (a_sc + 640, 512)]
        score_p = [None] + [A.at(*score_at[i]) for i in (1, 2, 3)]
        a_ss = take(KEYS)
        score_s = A.at(a_ss, KEYS, parts=NEW)
        best8 = A.at(take(32), 4, 8)
        a_tmp = top[0]
        assert size - a_tmp > 7300, (size - a_tmp)

        psum = ctx.enter_context(nc.psum_tensor("psum", [P, 8, 512], F32))
        pair = [psum[:, 2 * i:2 * i + 2, 0:HALF] for i in range(4)]

        def halves(ap):
            return ap.rearrange("p (h n) -> p h n", h=2)

        rel_dram = nc.dram_tensor("rel_dram", [H_ATT, P, REL + 1], F32).ap()

        def slid(q0, nq, k0, nk, h0=0, nh=H_ATT):
            return bass.AP(tensor=rel_dram.tensor, offset=rel_dram.offset + h0 * P * (REL + 1) + q0 * REL + P - 1 + k0,
                           ap=[[P * (REL + 1), nh], [REL, nq], [1, nk]])

        w_full = [sem(f"w_full{i}") for i in range(RING)]
        w_used = sem("w_used")

        loaded = [0]

        def load_tile(sp, n):
            if n >= RING:
                sp.wait_ge(w_used, n - RING + 1)
            sp.dma_start(ring[:, n % RING, :], ins["weights"][n]).then_inc(w_full[n % RING], 16)

        def load_tiles(sp, a, b):
            b = min(b, T_END)
            loaded[0] = b
            while a < b and (a % RING or b - a < RING):
                load_tile(sp, a)
                a += 1
            if a < b:
                with sp.Fori(a // RING, b // RING) as r:
                    for s in range(RING):
                        if a > 0:
                            sp.wait_ge(w_used, r * RING + (s - RING + 1))
                        sp.dma_start(ring[:, s, :], ins["weights"][bass.ds(r * RING + s, 1)].rearrange(
                            "a p n -> (a p) n")).then_inc(w_full[s], 16)
                for n in range(b // RING * RING, b):
                    load_tile(sp, n)

        def tile_ready(pe, n):
            pe.wait_ge(w_full[n % RING], 16 * (n // RING + 1))

        def w_of(n, c, a=0, b=P):
            return ring[:, n % RING, c * P + a:c * P + b]

        def gain_of(dve, link, k, name):
            link(dve.tensor_scalar(gain[:, k], mods[:, 24 * k + 8:24 * k + 16, :], 1.0, None, ALU.add))
            link(dve.tensor_tensor(gain[:, k], gain[:, k],
                                   param(name).unsqueeze(2).to_broadcast([P, DC, NSEQ]), ALU.mult))

        def project(pe, n, out, act):
            for c in range(DC):
                for h in range(2):
                    mm = pe.matmul(out[:, h, :], lhsT=w_of(n, c), rhs=act[:, c, h * HALF:(h + 1) * HALF],
                                   start=(c == 0), stop=(c == DC - 1))
            return mm

        s_in, s_x, s_csilu, s_modps, s_mods, s_gain = (sem(n) for n in (
            "in_loaded", "x_loaded", "c_silu_ready", "mods_in_psum", "mods_ready", "gain_ready"))
        s_sq, s_ss, s_std, s_rstd, s_xn, s_h, s_hs, v_link1, a_link1 = (sem(n) for n in (
            "squares_ready", "square_sums", "std_ready", "rstd_ready", "x_normed", "h_prompt", "h_sample",
            "dve_link1", "act_link1"))
        s_eps = sem("eps_ready")
        s_out = sem("out_written")
        outs_written = [0]

        def write(eng, dst, src):
            eng.dma_start(dst, src).then_inc(s_out, 16)
            outs_written[0] += 16

        a_sq, a_rstd = a_q, a_q + DC * NT
        sqT, rstd = A.at(a_sq, DC, NT), A.at(a_rstd, NT)

        with nc.Block() as block:
            @block.sync
            def _(sp):
                sp.dma_start(A.at(a_param, PARAM_W), ins["params"]).then_inc(s_in, 16)
                sp.dma_start(A.at(a_const, CONST_W), ins["consts"]).then_inc(s_in, 16)
                sp.dma_start(xT, ins["x"]).then_inc(s_x, 16)
                for n in range(RING):
                    load_tile(sp, n)
                load_tiles(sp, RING, T_KI + RING)

            @block.scalar
            def _(act):
                act.wait_ge(s_in, 32)
                act.activation(c_silu, param("c").rearrange("p (c n) -> p c n", n=NSEQ),
                               ACT.Silu).then_inc(s_csilu, 1)
                act.wait_ge(s_x, 16)
                for c in range(DC):
                    act.activation(sqT[:, c, :], xT[:, c, :], ACT.Square).then_inc(s_sq, 1)
                act.wait_ge(s_ss, 1)
                act.wait_ge(s_eps, 1)
                act.activation(halves(rstd), pair[0], ACT.Sqrt, bias=eps_col[:, 0:1],
                               scale=1.0 / D).then_inc(s_std, 1)
                act.wait_ge(s_gain, 1)
                for c in range(DC):
                    act.wait_ge(s_xn, c + 1)
                    act.activation(hT[:, c, 0:SEQ], sqT[:, c, 0:SEQ], ACT.Identity,
                                   bias=mods[:, c, 0:1], scale=gain[:, 0, c, 0:1]).then_inc(s_h, 1)

            @block.tensor
            def _(pe):
                pe.wait_ge(s_in, 32)
                for c in range(DC):
                    pe.wait_ge(s_sq, c + 1)
                    for h in range(2):
                        mm = pe.matmul(pair[0][:, h, :], lhsT=const("ones"),
                                       rhs=sqT[:, c, h * HALF:(h + 1) * HALF],
                                       start=(c == 0), stop=(c == DC - 1))
                mm.then_inc(s_ss, 1)
                pe.wait_ge(s_csilu, 1)
                with pe.Fori(0, T_KI // RING) as r:
                    for s in range(RING):
                        pe.wait_ge(w_full[s], r * 16 + 16)
                        for c in range(DC):
                            mm = pe.matmul(psum[:, 7, bass.ds(r * (RING * NSEQ) + s * NSEQ, NSEQ)],
                                           lhsT=w_of(s, c), rhs=c_silu[:, c, :],
                                           start=(c == 0), stop=(c == DC - 1))
                        mm.then_inc(w_used, 1)

            @block.vector
            def _(dve):
                link = Link(dve, v_link1)
                dve.memset(small[:, 4, :], 0.0)
                dve.memset(eps_col, EPS).then_inc(s_eps, 1)
                dve.wait_ge(s_std, 1)
                link(dve.reciprocal(rstd, rstd))
                for c in range(DC):
                    dve.tensor_tensor(sqT[:, c, :], xT[:, c, :], rstd, ALU.mult).then_inc(s_xn, 1)
                dve.wait_ge(w_used, T_KI)
                link(dve.tensor_tensor(
                    mods[:, 0:T_KI, :], psum[:, 7, 0:T_KI * NSEQ].rearrange("p (m n) -> p m n", n=NSEQ),
                    param("ada_b")[:, 0:T_KI].unsqueeze(2).to_broadcast([P, T_KI, NSEQ]), ALU.add))
                gain_of(dve, link, 0, "norm1")
                dve.sem_inc(s_gain, 1)
                dve.wait_ge(s_xn, DC)
                for c in range(DC):
                    new = sqT[:, c, SEQ:NT].rearrange("p (b t) -> p b t", t=NS)
                    link(dve.tensor_tensor(new, new, gain[:, 0, c, 1:NSEQ].unsqueeze(2).to_broadcast(
                        [P, NB, NS]), ALU.mult))
                    dve.tensor_tensor(hT[:, c, SEQ:NT].rearrange("p (b t) -> p b t", t=NS), new,
                                      mods[:, c, 1:NSEQ].unsqueeze(2).to_broadcast([P, NB, NS]),
                                      ALU.add).then_inc(s_hs, 1)

        s_pt, s_kidx, s_ev2, s_relu, s_acc, s_pl, s_qs = (sem(n) for n in (
            "page_table_loaded", "kidx_loaded", "att_tile_out", "relu_ready", "relu_used", "index_logits", "qs_ready"))
        s_wisel, s_wi, s_sl, s_srelu, s_sscore, s_scopy = (sem(n) for n in (
            "wi_spread", "wi_ready", "new_index_logits", "new_relu_ready", "new_score_summed", "new_score_out"))
        v_link2 = sem("dve_link2")
        relu_scale = D_IDX ** -0.5 * H_IDX ** -0.5
        page_tab = ctx.enter_context(nc.sbuf_tensor("page_tab", [1, NB * PAGES], I32))
        rb = A.at(a_tmp, 2, 512)
        rs = A.at(a_tmp + 1024, 2, 512)
        qs = A.at(a_tmp + 2048, NB * 32, parts=D_IDX)
        wi_rows = A.at(a_tmp + 2304, 2, NEW)
        wiT = A.at(a_tmp + 2368, NEW, parts=H_IDX)
        IDX_UNITS = [(qt, h) for qt in range(1, QT) for h in range(H_IDX)]
        S_UNITS = [(kc, a) for kc in range(3) for a in range(2)]
        KC = [(0, 512), (512, 512), (1024, NEW)]

        with nc.Block() as block:
            @block.sync
            def _(sp):
                sp.dma_start(page_tab[:], ins["page_table"]).then_inc(s_pt, 16)
                load_tiles(sp, T_KI + RING, T_Q)
                sp.wait_ge(s_ev2, 1)
                write(sp, outs["ki"], kiT[0:D_IDX, :])
                load_tiles(sp, T_Q, T_Z + RING)
                sp.wait_ge(s_ev2, 8)
                write(sp, outs["k"], kT)
                sp.wait_ge(s_ev2, 11)
                write(sp, outs["v"][:, 0:4, :], v_tok[:, 0:4, :])
                write(sp, outs["v"][0:NEW, 4, :], v_tok[0:NEW, 4, :])

            @block.gpsimd
            def _(pool):
                pool.wait_ge(s_pt, 16)
                with pool.Fori(0, NB) as b:
                    of_seq = [pool.value_load(page_tab[0:1, bass.ds(b * PAGES + j, 1)], min_val=0,
                                            max_val=POOL - 1) for j in range(PAGES)]
                    for j in range(PAGES):
                        pool.dma_start(
                            kidx[:, bass.ds(b, 1), j * PAGE:(j + 1) * PAGE].rearrange("p a n -> p (a n)"),
                            ins["pages_i"][bass.ds(of_seq[j], 1)].rearrange("a p n -> (a p) n"),
                        ).then_inc(s_kidx, 16)

            @block.tensor
            def _(pe):
                unit = [0]

                def free_pair():
                    if unit[0] >= 2:
                        pe.wait_ge(s_ev2, unit[0] - 1)
                    unit[0] += 1
                    return pair[(unit[0] - 1) % 2], 2 * ((unit[0] - 1) % 2)

                def tile(n):
                    tile_ready(pe, n)
                    out, _ = free_pair()
                    project(pe, n, out, hT).then_inc(w_used, 1)

                tile(T_KI)
                for i in range(4):
                    tile(T_QI + i)
                tile_ready(pe, T_SMALL)
                _, bank = free_pair()
                for i in range(5):
                    m = P if i < 4 else NEW
                    for c in range(DC):
                        pe.matmul(psum[0:m, bank, 24 * i:24 * i + 24], lhsT=hT[:, c, P * i:P * i + m],
                                  rhs=w_of(T_SMALL, c, 0, 24), start=(c == 0), stop=(c == DC - 1))
                for c in range(DC):
                    mm = pe.matmul(psum[0:H_IDX, bank + 1, 0:NEW], lhsT=w_of(T_SMALL, c, 16, 24),
                                   rhs=hT[:, c, SEQ:NT], start=(c == 0), stop=(c == DC - 1))
                mm.then_inc(w_used, 1)
                tile(T_K)
                tile(T_K + 1)
                tile_ready(pe, T_V)
                tile_ready(pe, T_V + 1)
                for u in range(3):
                    _, bank = free_pair()
                    for i in range(2 * u, min(2 * u + 2, 5)):
                        m = P if i < 4 else NEW
                        for kv in range(KV):
                            for c in range(DC):
                                mm = pe.matmul(psum[0:m, bank + i % 2, kv * P:kv * P + P],
                                               lhsT=hT[:, c, P * i:P * i + m], rhs=w_of(T_V + kv, c),
                                               start=(c == 0), stop=(c == DC - 1))
                    if u < 2:
                        mm.then_inc(s_pl, 1)
                mm.then_inc(w_used, 2)
                pe.wait_ge(s_ev2, 7)
                pe.matmul(psum[:, 7, 0:NEW], lhsT=const("head_rows", H_IDX), rhs=wiT, start=True,
                          stop=True).then_inc(s_wisel, 1)

                def index_unit(k):
                    qt, h = IDX_UNITS[k]
                    lo, w = 64 * (h % 2), (qt + 1) * P
                    if k >= 4:
                        pe.wait_ge(s_relu, k - 3)
                    if k == 3:
                        pe.wait_ge(s_wi, 1)
                    pe.matmul(psum[:, 4 + k % 4, 0:w], lhsT=qiT[lo:lo + 64, h // 2, qt * P:qt * P + P],
                              rhs=kiT[lo:lo + 64, 0:w], start=True, stop=True).then_inc(s_pl, 1)

                for j in range(8):
                    tile(T_Q + j)
                    for k in range(3 * j, 3 * j + 3):
                        index_unit(k)

                def new_logits(s):
                    kc, a = S_UNITS[s]
                    at, w = KC[kc]
                    if s >= 2:
                        pe.wait_ge(s_srelu, s - 1)
                    if kc < 2:
                        for b4 in range(4):
                            b = 4 * a + b4
                            mm = pe.matmul(psum[32 * b4:32 * b4 + 32, 4 + s % 2, 0:w],
                                           lhsT=qs[:, 32 * b:32 * b + 32], rhs=kidx[:, b, at:at + w],
                                           start=True, stop=True)
                    else:
                        mm = pe.matmul(psum[:, 4 + s % 2, 0:w], lhsT=qs[:, P * a:P * a + P],
                                       rhs=kiT[0:D_IDX, SEQ:NT], start=True, stop=True)
                    mm.then_inc(s_sl, 1)

                def new_score(s):
                    kc, a = S_UNITS[s]
                    w = KC[kc][1]
                    pe.wait_ge(s_srelu, s + 1)
                    if s == 4:
                        pe.wait_ge(s_scopy, 1)
                    mm = pe.matmul(psum[0:NEW, 6 + kc % 2, 0:w], lhsT=wi_rows[:, a, :], rhs=rs[:, s % 2, 0:w],
                                   start=(a == 0), stop=(a == 1))
                    mm.then_inc(s_sscore, 1)

                pe.wait_ge(s_kidx, 16 * NB * PAGES)
                pe.wait_ge(s_qs, 2)
                pe.wait_ge(s_relu, len(IDX_UNITS))
                for s in range(6):
                    new_logits(s)
                    if s:
                        new_score(s - 1)
                new_score(5)

            @block.scalar
            def _(act):
                def out(src, dst):
                    return act.activation(dst, src, ACT.Copy)

                def tile(n, u, dst):
                    act.wait_ge(w_used, n + 1)
                    out(pair[u % 2], halves(dst)).then_inc(s_ev2, 1)

                tile(T_KI, 0, kiT)
                for i in range(4):
                    tile(T_QI + i, 1 + i, qiT[:, i, :])
                act.wait_ge(w_used, T_SMALL + 1)
                out(psum[:, 2, 0:96].rearrange("p (a b) -> p a b", b=24), small[:, 0:4, :])
                out(psum[0:NEW, 2, 96:120], small[0:NEW, 4, :])
                out(psum[0:H_IDX, 3, 0:NEW], wiT).then_inc(s_ev2, 1)
                tile(T_K, 6, kT[:, 0, :])
                tile(T_K + 1, 7, kT[:, 1, :])
                for u in range(3):
                    b = 2 * ((8 + u) % 2)
                    if u < 2:
                        act.wait_ge(s_pl, u + 1)
                        out(psum[:, b:b + 2, 0:256], v_tok[:, 2 * u:2 * u + 2, :]).then_inc(s_ev2, 1)
                    else:
                        act.wait_ge(w_used, T_V + 2)
                        out(psum[0:NEW, b, 0:256], v_tok[0:NEW, 4, :]).then_inc(s_ev2, 1)
                for j in range(8):
                    tile(T_Q + j, 11 + j, qT[:, j, :])
                    for k in range(3 * j, 3 * j + 3):
                        qt, h = IDX_UNITS[k]
                        w = (qt + 1) * P
                        act.wait_ge(s_pl, 2 + k + 1)
                        if k >= 2:
                            act.wait_ge(s_acc, 1 + k - 1)
                        act.activation(rb[:, k % 2, 0:w], psum[:, 4 + k % 4, 0:w], ACT.Relu,
                                       scale=relu_scale).then_inc(s_relu, 1)
                for s, (kc, a) in enumerate(S_UNITS):
                    w = KC[kc][1]
                    act.wait_ge(s_sl, s + 1)
                    if s >= 2:
                        act.wait_ge(s_sscore, s - 1)
                    act.activation(rs[:, s % 2, 0:w], psum[:, 4 + s % 2, 0:w], ACT.Relu,
                                   scale=relu_scale).then_inc(s_srelu, 1)

            @block.vector
            def _(dve):
                link = Link(dve, v_link2)
                dve.sem_inc(s_acc, 1)
                dve.wait_ge(s_ev2, 5)
                to = qs.rearrange("p (b j o t) -> p b j o t", j=4, o=2, t=NS)
                for odd in range(2):
                    src = qiT[64 * odd:64 * odd + 64, :, SEQ:NT].rearrange("p j (b t) -> p b j t", t=NS)
                    for b in range(NB):
                        last = dve.tensor_copy(to[:, b, :, odd, :], src[:, b])
                    last.then_inc(s_qs, 1)
                dve.wait_ge(s_wisel, 1)
                for a in range(2):
                    last = dve.tensor_tensor(
                        wi_rows[:, a, :], const("row_token").rearrange("p (a n) -> p a n", a=2)[:, a, :],
                        psum[:, 7, 0:NEW], ALU.mult)
                last.then_inc(s_wi, 1)
                for k, (qt, h) in enumerate(IDX_UNITS):
                    w = (qt + 1) * P
                    dve.wait_ge(s_relu, k + 1)
                    wcol = small[:, qt, 16 + h:17 + h]
                    if h == 0:
                        ins_ = dve.tensor_scalar(score_p[qt], rb[:, k % 2, 0:w], wcol, None, ALU.mult)
                    else:
                        ins_ = dve.scalar_tensor_tensor(score_p[qt], rb[:, k % 2, 0:w], wcol, score_p[qt],
                                                        ALU.mult, ALU.add)
                    ins_.then_inc(s_acc, 1)
                    dve.wait_ge(s_acc, 1 + k + 1)
                    if h == H_IDX - 1:
                        dg = score_p[qt][:, qt * P:(qt + 1) * P]
                        link(dve.tensor_tensor(dg, dg, const("future"), ALU.add))
                for kc in range(3):
                    at, w = KC[kc]
                    dve.wait_ge(s_sscore, 2 * kc + 2)
                    src = psum[0:NEW, 6 + kc % 2, 0:w]
                    if kc < 2:
                        dve.tensor_copy(score_s[:, at:at + w], src).then_inc(s_scopy, 1)
                    else:
                        dve.tensor_tensor(score_s[:, at:at + w], src, const("new_keys", NEW),
                                          ALU.add).then_inc(s_scopy, 1)

        s_ev3, s_fill, s_conv, s_silu, s_state, s_cg, s_cgst, s_scd, s_top, s_raw = (sem(n) for n in (
            "tile_out3", "conv_fill", "conv_ready", "silu_done", "conv_state_saved", "cg_ready", "sc_state_saved",
            "sc_done", "top_step", "raw_read"))
        v_link3, p_link3 = sem("dve_link3"), sem("pool_link3")
        yc = A.at(a_x, 8, NT)
        tsc = A.at(a_tmp, 2, 3, NT)
        cg = A.at(a_tmp + 3264, 2, W_SC)
        u_sc = A.at(a_tmp + 3264 + 2 * W_SC, W_SC - 2)
        a_ca = a_tmp + 3264 + 3 * W_SC
        cacc = A.at(a_ca, 2, W_XB - 3)
        conv_state = A.at(a_ca + 2 * (W_XB - 3), XBC, 27)
        sc_state = A.at(a_ca + 2 * (W_XB - 3) + XBC * 27, 8, 18)
        LX = W_XB - 3
        LS = W_SC - 2

        def seq_new(row, start, seg, lo, hi):
            return row[:, start:start + NB * seg].rearrange("p (b s) -> p b s", s=seg)[:, :, lo:hi]

        with nc.Block() as block:
            @block.sync
            def _(sp):
                load_tiles(sp, T_Z + RING, T_ADA2 + RING)
                sp.wait_ge(s_state, XBC)
                write(sp, outs["conv"], conv_state)
                sp.wait_ge(s_cgst, 8)
                write(sp, outs["sc_conv"], sc_state)

            @block.gpsimd
            def _(pool):
                for m in range(XBC):
                    pool.memset(xb[:, m, 0:3], 0.0)
                    last = pool.tensor_copy(
                        seq_new(xb[:, m, :], SEG_P, SEG_S, 0, 3),
                        param("conv_prev").rearrange("p (m b k) -> p m b k", b=NB, k=3)[:, m])
                last.then_inc(s_fill, 1)
                for i in range(2):
                    last = pool.memset(cg[:, i, 0:2], 0.0)
                last.then_inc(s_fill, 1)
                for m in range(XBC):
                    pool.wait_ge(s_ev3, 8 + m + 1)
                    pool.tensor_copy(conv_state[:, m, 0:3], xb[:, m, SEQ:SEQ + 3])
                    pool.tensor_copy(conv_state[:, m, 3:27].rearrange("p (b k) -> p b k", k=3),
                                     seq_new(xb[:, m, :], SEG_P, SEG_S, 4, 7)).then_inc(s_state, 1)

            @block.tensor
            def _(pe):
                for u in range(48):
                    tile_ready(pe, T_Z + u)
                    if u >= 4:
                        pe.wait_ge(s_ev3, u - 3)
                    project(pe, T_Z + u, pair[u % 4], hT).then_inc(w_used, 1)

            @block.scalar
            def _(act):
                for u in range(8):
                    act.wait_ge(w_used, T_Z + u + 1)
                    act.activation(halves(zT[:, u, :]), pair[u % 4], ACT.Copy).then_inc(s_ev3, 1)
                rest = SEQ - HALF
                for u in range(8, 24):
                    m, src = u - 8, pair[u % 4]
                    act.wait_ge(w_used, T_Z + u + 1)
                    act.activation(xb[:, m, 3:3 + HALF], src[:, 0, :], ACT.Copy)
                    act.activation(xb[:, m, 3 + HALF:3 + SEQ], src[:, 1, 0:rest], ACT.Copy)
                    act.activation(seq_new(xb[:, m, :], SEG_P, SEG_S, 3, 7),
                                   src[:, 1, rest:HALF].rearrange("p (b t) -> p b t", t=NS),
                                   ACT.Copy).then_inc(s_ev3, 1)
                for m in range(8):
                    for i in range(3):
                        u = 24 + 3 * m + i
                        act.wait_ge(w_used, T_Z + u + 1)
                        if m >= 2:
                            act.wait_ge(s_scd, m - 1)
                        act.activation(halves(tsc[:, m % 2, i, :]), pair[u % 4], ACT.Copy).then_inc(s_ev3, 1)
                    for j in (2 * m, 2 * m + 1):
                        act.wait_ge(s_conv, j + 1)
                        act.wait_ge(s_state, j + 1)
                        act.activation(xb[:, j, 0:LX], cacc[:, j % 2, :], ACT.Silu).then_inc(s_silu, 1)

            @block.vector
            def _(dve):
                link = Link(dve, v_link3)
                rows = [(score_p[1], TOPK_P), (score_p[2], TOPK_P), (score_p[3], TOPK_P), (score_s, TOPK_S)]
                steps = 0
                for r in range(TOPK_S // 8):
                    live = [(i, s) for i, (s, k) in enumerate(rows) if r < k // 8]
                    for i, s in live:
                        dve.max(best8[0:s.shape[0], i, :], s).then_inc(s_top, 1)
                    for n, (i, s) in enumerate(live):
                        dve.wait_ge(s_top, steps + n + 1)
                        dve.match_replace(s, best8[0:s.shape[0], i, :], s, CHOSEN).then_inc(s_top, 1)
                    steps += 2 * len(live)
                    dve.wait_ge(s_top, steps)
                for s, _ in rows:
                    link(dve.tensor_scalar(s, s, CHOSEN * 0.7, NEG_ADD, ALU.is_gt, ALU.mult))

                def conv(m):
                    if m == 0:
                        dve.wait_ge(s_fill, 2)
                    dve.wait_ge(s_ev3, 8 + m + 1)
                    if m >= 2:
                        dve.wait_ge(s_silu, m - 1)
                    w = param("conv_w").rearrange("p (m k) -> p m k", k=K_SSD)[:, m, :]
                    acc = cacc[:, m % 2, :]
                    link(dve.tensor_scalar(acc, xb[:, m, 0:LX], w[:, 0:1], param("conv_b")[:, m:m + 1],
                                           ALU.mult, ALU.add))
                    for k in range(1, K_SSD):
                        last = dve.scalar_tensor_tensor(acc, xb[:, m, k:k + LX], w[:, k:k + 1], acc,
                                                        ALU.mult, ALU.add)
                        if k < K_SSD - 1:
                            link(last)
                    last.then_inc(s_conv, 1)

                def short(m):
                    row = cg[:, m % 2, :]
                    c_, h_, b_ = (tsc[:, m % 2, i, :] for i in range(3))
                    by_seq = lambda a: a[:, SEQ:NT].rearrange("p (b t) -> p b t", t=NS)
                    dve.wait_ge(s_ev3, 24 + 3 * m + 3)
                    dve.tensor_tensor(row[:, 2:2 + SEQ], c_[:, 0:SEQ], h_[:, 0:SEQ], ALU.mult)
                    dve.tensor_copy(seq_new(row, SSEG_P, SSEG_S, 0, 2),
                                    param("sc_prev").rearrange("p (m b k) -> p m b k", b=NB, k=2)[:, m])
                    link(dve.tensor_tensor(seq_new(row, SSEG_P, SSEG_S, 2, 6), by_seq(c_), by_seq(h_),
                                           ALU.mult))
                    dve.tensor_copy(sc_state[:, m, 0:2], row[:, SEQ:SEQ + 2])
                    dve.tensor_copy(sc_state[:, m, 2:18].rearrange("p (b k) -> p b k", k=2),
                                    seq_new(row, SSEG_P, SSEG_S, 4, 6)).then_inc(s_cgst, 1)
                    w = param("sc_w").rearrange("p (m k) -> p m k", k=K_SC)[:, m, :]
                    link(dve.tensor_scalar(u_sc, row[:, 0:LS], w[:, 0:1], None, ALU.mult))
                    for k in range(1, K_SC):
                        link(dve.scalar_tensor_tensor(u_sc, row[:, k:k + LS], w[:, k:k + 1], u_sc,
                                                      ALU.mult, ALU.add))
                    dve.tensor_tensor(yc[:, m, 0:SEQ], u_sc[:, 0:SEQ], b_[:, 0:SEQ], ALU.mult)
                    u_new = u_sc[:, SSEG_P:SSEG_P + (NB - 1) * SSEG_S + NS]
                    for b in range(NB):
                        at = SSEG_P + b * SSEG_S
                        last = dve.tensor_tensor(yc[:, m, SEQ + b * NS:SEQ + b * NS + NS],
                                                 u_sc[:, at:at + NS],
                                                 b_[:, SEQ + b * NS:SEQ + b * NS + NS], ALU.mult)
                    link(last)
                    dve.sem_inc(s_scd, 1)

                for m in range(8):
                    conv(2 * m)
                    conv(2 * m + 1)
                    short(m)

        s_rel, s_relout, s_reld, s_near, s_qk, s_lg, s_max, s_exp, s_prob, s_pt4, s_ptout, s_pv, s_o = (
            sem(n) for n in ("rel_in_psum", "rel_in_sbuf", "rel_in_dram", "near_loaded", "qk_ready", "logits_read",
                             "max_ready", "exp_ready", "probs_ready", "probs_turned", "turned_out", "pv_ready",
                             "att_out"))
        v_link4 = sem("dve_link4")
        near = A.at(a_tmp, H_ATT, 2 * P)
        sp4 = A.at(a_tmp + 2048, 3, 512)
        pt4 = A.at(a_tmp + 2048 + 1536, 2, 512)
        a_st = a_tmp + 2048 + 1536 + 1024
        nmax, esum = A.at(a_st, 32), A.at(a_st + 32, 32)
        rel_sb = A.at(a_st + 64, REL, parts=H_ATT)
        A_UNITS = [(qt, h) for qt in range(QT) for h in range(H_ATT)]
        NU = len(A_UNITS)

        with nc.Block() as block:
            @block.sync
            def _(sp):
                sp.wait_ge(s_relout, 1)
                sp.dma_start(rel_dram[:, :, 0:REL], rel_sb.unsqueeze(1).to_broadcast([H_ATT, P, REL])).then_inc(
                    s_reld, 16)
                sp.wait_ge(s_reld, 16)
                sp.dma_start(near, slid(0, P, 0, 2 * P).rearrange("h q k -> q h k")).then_inc(s_near, 16)
                load_tiles(sp, T_ADA2 + RING, T_MERGE + RING)

            @block.tensor
            def _(pe):
                pe.matmul(psum[0:H_ATT, 7, 0:REL], lhsT=param("rel_bias", 32), rhs=const("rel_cols", 32),
                          start=True, stop=True).then_inc(s_rel, 1)

                def qk(k):
                    qt, h = A_UNITS[k]
                    if k >= 2:
                        pe.wait_ge(s_lg, k - 1)
                    pe.matmul(psum[:, k % 2, 0:(qt + 1) * P], lhsT=qT[:, h, qt * P:qt * P + P],
                              rhs=kT[:, h // GRP, 0:(qt + 1) * P], start=True, stop=True).then_inc(s_qk, 1)

                def turn(k):
                    qt, h = A_UNITS[k]
                    pe.wait_ge(s_prob, k + 1)
                    if k >= 2:
                        pe.wait_ge(s_ptout, k - 1)
                    for j in range(qt + 1):
                        mm = pe.transpose(psum[:, 2 + k % 2, j * P:j * P + P], sp4[:, k % 3, j * P:j * P + P],
                                          const("ident"))
                    mm.then_inc(s_pt4, 1)

                def pv(k):
                    qt, h = A_UNITS[k]
                    kv = h // GRP
                    pe.wait_ge(s_ptout, k + 1)
                    if k >= 2:
                        pe.wait_ge(s_o, k - 1)
                    for j in range(qt + 1):
                        mm = pe.matmul(psum[:, 4 + k % 2, 0:P], lhsT=v_tok[:, j, kv * DH:kv * DH + DH],
                                       rhs=pt4[:, k % 2, j * P:j * P + P], start=(j == 0), stop=(j == qt))
                    mm.then_inc(s_pv, 1)

                def modulation(k):
                    tile_ready(pe, T_ADA2 + k)
                    for c in range(DC):
                        mm = pe.matmul(psum[:, 6, k * NSEQ:(k + 1) * NSEQ], lhsT=w_of(T_ADA2 + k, c),
                                       rhs=c_silu[:, c, :], start=(c == 0), stop=(c == DC - 1))
                    mm.then_inc(w_used, 1)

                for k in range(NU + 2):
                    if k < NU:
                        qk(k)
                        modulation(k)
                    if 1 <= k <= NU:
                        turn(k - 1)
                    if k >= 2:
                        pv(k - 2)

            @block.scalar
            def _(act):
                act.wait_ge(s_rel, 1)
                act.activation(rel_sb, psum[0:H_ATT, 7, 0:REL], ACT.Copy).then_inc(s_relout, 1)
                for k in range(NU + 2):
                    if k < NU:
                        w = (A_UNITS[k][0] + 1) * P
                        act.wait_ge(s_max, k + 1)
                        act.activation(sp4[:, k % 3, 0:w], sp4[:, k % 3, 0:w], ACT.Exp, bias=nmax[:, k:k + 1],
                                       accum_out=esum[:, k:k + 1]).then_inc(s_exp, 1)
                    if 1 <= k <= NU:
                        w = (A_UNITS[k - 1][0] + 1) * P
                        act.wait_ge(s_pt4, k)
                        if k >= 3:
                            act.wait_ge(s_pv, k - 2)
                        act.activation(pt4[:, (k - 1) % 2, 0:w], psum[:, 2 + (k - 1) % 2, 0:w],
                                       ACT.Copy).then_inc(s_ptout, 1)
                    if k >= 2:
                        qt, h = A_UNITS[k - 2]
                        act.wait_ge(s_pv, k - 1)
                        act.activation(qT[:, h, qt * P:qt * P + P], psum[:, 4 + k % 2, 0:P],
                                       ACT.Copy).then_inc(s_o, 1)

            @block.vector
            def _(dve):
                link = Link(dve, v_link4)
                dve.wait_ge(s_near, 16)
                for k in range(NU + 1):
                    if k < NU:
                        qt, h = A_UNITS[k]
                        w = (qt + 1) * P
                        s = sp4[:, k % 3, 0:w]
                        mask = score_p[qt] if qt else const("future_add")
                        dve.wait_ge(s_qk, k + 1)
                        if k >= 3:
                            dve.wait_ge(s_pt4, k - 2)
                        dve.scalar_tensor_tensor(s, psum[:, k % 2, 0:w], DH ** -0.5, mask, ALU.mult,
                                                 ALU.add).then_inc(s_lg, 1)
                        dve.wait_ge(s_lg, k + 1)
                        last, nb = (s[:, w - 256:w], near[:, h, :]) if qt else (s, near[:, h, P:2 * P])
                        link(dve.tensor_tensor(last, last, nb, ALU.add))
                        dve.tensor_reduce(nmax[:, k:k + 1], s, AX, ALU.max, negate=True).then_inc(s_max, 1)
                    if k >= 1:
                        w = (A_UNITS[k - 1][0] + 1) * P
                        s = sp4[:, (k - 1) % 3, 0:w]
                        dve.wait_ge(s_exp, k)
                        link(dve.reciprocal(esum[:, k - 1:k], esum[:, k - 1:k]))
                        dve.tensor_scalar(s, s, esum[:, k - 1:k], None, ALU.mult).then_inc(s_prob, 1)
                dve.wait_ge(w_used, T_MERGE)
                link(dve.tensor_tensor(
                    mods[:, T_KI:48, :], psum[:, 6, 0:32 * NSEQ].rearrange("p (m n) -> p m n", n=NSEQ),
                    param("ada_b")[:, T_KI:48].unsqueeze(2).to_broadcast([P, 32, NSEQ]), ALU.add))
                gain_of(dve, link, 1, "norm2")

        s_kv, s_kvused, s_qz, s_slog, s_sl5, s_smax, s_sexp, s_sprob, s_st, s_stout, s_spv, s_so, s_qz0, s_nearl = (
            sem(n) for n in ("pages_loaded", "pages_used", "q_spread", "slogits_ready", "slogits_read", "smax_ready",
                             "sexp_ready", "sprobs_ready", "sprobs_turned", "sturned_out", "spv_ready", "satt_out",
                             "q_zeroed", "snear_loaded"))
        s_kvs = [sem(f"pages_loaded{i}") for i in range(2)]
        v_link5 = sem("dve_link5")
        pages = A.at(a_tmp, 2, PAGES * 256)
        ss5 = A.at(a_tmp + 4096, KEYS)
        pts = A.at(a_tmp + 4096 + KEYS, PAGES, P)
        ptn = A.at(a_tmp + 4096 + KEYS + 1024, P, parts=NEW)
        snear = A.at(a_tmp + 4096 + KEYS + 1152, P + NS)
        st5 = A.at(a_tmp + 4096 + KEYS + 1152 + P + NS, 4)
        qz = A.at(a_sc, NB, KV, 32)

        def pages_in(eng, k):
            for u in range(0, 16, 4):
                src = ins["pages_k" if u % 8 < 4 else "pages_v"]
                with eng.Fori(0, 2) as q:
                    first = (q * 2 + (4 * (u // 8) + k)) * PAGES
                    of_seq = [eng.value_load(page_tab[0:1, bass.ds(first + j, 1)], min_val=0, max_val=POOL - 1)
                              for j in range(PAGES)]
                    eng.wait_ge(s_kvused, q * 2 + (u + k + 1))
                    for j in range(PAGES):
                        eng.dma_start(pages[:, k, j * 256:j * 256 + 256],
                                      src[bass.ds(of_seq[j], 1)].rearrange("a p n -> (a p) n")).then_inc(s_kvs[k], 16)

        with nc.Block() as block:
            @block.sync
            def _(sp):
                for g in range(4):
                    sp.dma_start(snear[32 * g:32 * g + 32, :], slid(0, NS, 0, P + NS)).then_inc(s_nearl, 16)
                pages_in(sp, 0)

            @block.gpsimd
            def _(pool):
                pool.memset(qz, 0.0).then_inc(s_qz0, 1)
                pages_in(pool, 1)

            @block.tensor
            def _(pe):
                pe.sem_inc(s_kvused, 2)
                pe.wait_ge(s_qz, NB)
                for a in range(2):
                    if a:
                        pe.wait_ge(s_sl5, 1)
                    for kc in range(3):
                        at, w = KC[kc]
                        pe.matmul(psum[:, kc, 0:w],
                                  lhsT=const("token_row", NEW).rearrange("p (a n) -> p a n", a=2)[:, a, :],
                                  rhs=score_s[:, at:at + w], start=True, stop=False)
                    for b4 in range(4):
                        u, b = 8 * a + b4, 4 * a + b4
                        pe.wait_ge(s_kvs[u % 2], 16 * PAGES * (u // 2 + 1))
                        page = pages[:, u % 2, :].rearrange("p (j v n) -> p j v n", v=KV, n=PAGE)
                        for kc in range(3):
                            w = KC[kc][1]
                            for kv in range(KV):
                                rhs = page[:, 4 * kc:4 * kc + 4, kv, :] if kc < 2 else kT[:, kv, SEQ:NT]
                                out = psum[32 * b4:32 * b4 + 32, kc, 0:w]
                                if kc < 2:
                                    out = out.rearrange("p (j n) -> p j n", n=PAGE)
                                mm = pe.matmul(out, lhsT=qz[:, b, kv, :], rhs=rhs, start=False, stop=(kv == 1))
                        mm.then_inc(s_kvused, 1)
                    pe.wait_ge(s_sprob, a + 1)
                    for j in range(PAGES):
                        pe.transpose(psum[:, 3 + j // 4, (j % 4) * P:(j % 4) * P + P],
                                     ss5[:, j * P:j * P + P], const("ident"))
                    pe.transpose(psum[0:NEW, 5, 0:P], ss5[:, PAST:KEYS], const("ident")).then_inc(s_st, 1)
                    pe.wait_ge(s_stout, a + 1)
                    if a:
                        pe.wait_ge(s_so, 1)
                    for b4 in range(4):
                        u = 8 * a + 4 + b4
                        pe.wait_ge(s_kvs[u % 2], 16 * PAGES * (u // 2 + 1))
                        for kv in range(KV):
                            col = 32 * b4 + 16 * kv
                            out = psum[:, 6, col:col + 16]
                            for j in range(PAGES):
                                at = j * 256 + kv * DH
                                pe.matmul(out, lhsT=pages[:, u % 2, at:at + DH], rhs=pts[:, j, col:col + 16],
                                          start=(j == 0), stop=False)
                            mm = pe.matmul(out, lhsT=v_tok[0:NEW, 4, kv * DH:kv * DH + DH],
                                           rhs=ptn[:, col:col + 16], start=False, stop=True)
                        mm.then_inc(s_kvused, 1)

            @block.scalar
            def _(act):
                act.wait_ge(s_qz0, 1)
                for b in range(NB):
                    for kv in range(KV):
                        last = act.activation(
                            qz[:, b, kv, 16 * kv:16 * kv + 16].rearrange("p (g t) -> p g t", t=NS),
                            qT[:, GRP * kv:GRP * kv + GRP, SEQ + NS * b:SEQ + NS * b + NS], ACT.Copy,
                            scale=DH ** -0.5)
                    last.then_inc(s_qz, 1)
                for a in range(2):
                    act.wait_ge(s_smax, a + 1)
                    act.activation(ss5, ss5, ACT.Exp, bias=st5[:, 2 * a:2 * a + 1],
                                   accum_out=st5[:, 2 * a + 1:2 * a + 2]).then_inc(s_sexp, 1)
                    act.wait_ge(s_st, a + 1)
                    act.activation(pts[:, 0:4, :], psum[:, 3, :].rearrange("p (j n) -> p j n", n=P), ACT.Copy)
                    act.activation(pts[:, 4:8, :], psum[:, 4, :].rearrange("p (j n) -> p j n", n=P), ACT.Copy)
                    act.activation(ptn, psum[0:NEW, 5, 0:P], ACT.Copy).then_inc(s_stout, 1)
                    act.wait_ge(s_kvused, 2 + 8 * a + 8)
                    for b4 in range(4):
                        at = SEQ + NS * (4 * a + b4)
                        last = act.activation(
                            qT[:, :, at:at + NS],
                            psum[:, 6, 32 * b4:32 * b4 + 32].rearrange("p (h t) -> p h t", t=NS), ACT.Copy)
                    last.then_inc(s_so, 1)

            @block.vector
            def _(dve):
                link = Link(dve, v_link5)
                dve.wait_ge(s_nearl, 16 * 4)
                for a in range(2):
                    dve.wait_ge(s_kvused, 2 + 8 * a + 4)
                    if a:
                        dve.wait_ge(s_st, a)
                    flat = psum[:, 0:3, :].rearrange("p a b -> p (a b)")
                    far = PAST - P
                    dve.tensor_copy(ss5[:, 0:far], flat[:, 0:far])
                    dve.tensor_tensor(ss5[:, far:PAST], flat[:, far:PAST], snear[:, 0:P], ALU.add)
                    link(dve.tensor_tensor(
                        ss5[:, PAST:KEYS].rearrange("p (b t) -> p b t", t=NS),
                        flat[:, PAST:KEYS].rearrange("p (b t) -> p b t", t=NS),
                        snear[:, P:P + NS].unsqueeze(1).to_broadcast([P, NB, NS]), ALU.add))
                    dve.sem_inc(s_sl5, 1)
                    dve.tensor_reduce(st5[:, 2 * a:2 * a + 1], ss5, AX, ALU.max, negate=True).then_inc(s_smax, 1)
                    dve.wait_ge(s_sexp, a + 1)
                    link(dve.reciprocal(st5[:, 2 * a + 1:2 * a + 2], st5[:, 2 * a + 1:2 * a + 2]))
                    dve.tensor_scalar(ss5, ss5, st5[:, 2 * a + 1:2 * a + 2], None, ALU.mult).then_inc(s_sprob, 1)

        retire([*w_full, w_used, s_out])

        s_st6, s_v6, s_e6, s_dt, s_small6, s_csout, s_t6, s_xdt, s_btok, s_csb, s_pre, s_e, s_mid, s_ys, s_post = (
            sem(n) for n in ("states_loaded", "softplus_in", "softplus_parts", "dt_ready", "cumsum_in_psum",
                             "cumsum_ready", "chunk_turned", "xdt_ready", "btok_ready", "decays_in_psum",
                             "decay_args", "decays_ready", "mix_ready", "y_in_psum", "y_out"))
        v_link6, a_link6 = sem("dve_link6"), sem("act_link6")
        states = A.at(a_sc, NB, D)
        a_s6 = a_q + 8 * NT
        stT = A.at(a_s6, D)
        xdt = A.at(a_s6 + 1024, D)
        xdtd = A.at(a_s6 + 2048, D)
        btok = A.at(a_s6 + 3072, 512)
        ebuf = A.at(a_s6 + 3584, 2, 512)
        a_s6b = a_sc + NB * D
        chb = A.at(a_s6b, 512)
        cbm = A.at(a_s6b + 512, P)
        cbm2 = A.at(a_s6b + 640, P)
        ecl = A.at(a_s6b + 768, 2, HPG)
        dt5 = A.at(a_s6b + 776, 5, H_SSD)
        adt = A.at(a_s6b + 856, 5, H_SSD)
        cs5 = A.at(a_s6b + 936, 5, H_SSD)
        dte = A.at(a_s6b + 1016, 5, H_SSD)
        a_neg = A.at(a_s6b + 1096, H_SSD)
        sp_e = A.at(a_s6b + 1112, 5, H_SSD)
        C_UNITS = [(i, g) for i in range(QT) for g in range(G_SSD)]
        NCU = len(C_UNITS)

        with nc.Block() as block:
            @block.sync
            def _(sp):
                sp.dma_start(states, ins["state"].rearrange("n (b d) -> n b d", b=NB)).then_inc(s_st6, 16)
                sp.wait_ge(s_post, NCU)
                write(sp, outs["ssm_p"], stT)
                sp.wait_ge(s_out, outs_written[0])

            @block.scalar
            def _(act):
                act.wait_ge(s_v6, 1)
                act.activation(sp_e, sp_e, ACT.Exp).then_inc(a_link6, 1)
                act.activation(a_neg, param("a_log"), ACT.Exp)
                act.wait_ge(a_link6, 1)
                act.activation(sp_e, sp_e, ACT.Ln, bias=1.0).then_inc(s_e6, 1)
                act.wait_ge(s_small6, 1)
                for lo, m, k in ((0, P, 4), (4, NEW, 1)):
                    for to, at, func in ((cs5, 0, ACT.Copy), (dte, 80, ACT.Exp)):
                        at += lo * H_SSD
                        last = act.activation(
                            to[0:m, lo:lo + k, :],
                            psum[0:m, 3, at:at + k * H_SSD].rearrange("p (a b) -> p a b", b=H_SSD), func)
                last.then_inc(s_csout, 1)
                for k, (i, g) in enumerate(C_UNITS):
                    if g == 0:
                        act.wait_ge(s_t6, i + 1)
                        if i:
                            act.wait_ge(s_ys, k)
                        act.activation(btok, psum[:, 2, :], ACT.Copy).then_inc(s_btok, 1)
                    act.wait_ge(s_csb, k + 1)
                    if k >= 1:
                        act.wait_ge(s_ys, k)
                        act.wait_ge(s_post, k)
                    act.wait_ge(s_pre, k + 1)
                    act.activation(chb, psum[:, 4 + k % 2, :], ACT.Exp)
                    act.activation(ebuf[:, k % 2, :], ebuf[:, k % 2, :], ACT.Exp).then_inc(s_e, 1)

            @block.tensor
            def _(pe):
                pe.wait_ge(s_dt, 1)
                for i in range(5):
                    m = P if i < 4 else NEW
                    for k, (whole, new) in enumerate((("upto", "upto_new"), ("after", "after_new"))):
                        lhsT = const(whole) if i < 4 else const(new, NEW)
                        at = 80 * k + H_SSD * i
                        mm = pe.matmul(psum[0:m, 3, at:at + H_SSD], lhsT=lhsT, rhs=adt[0:m, i, :],
                                       start=True, stop=True)
                mm.then_inc(s_small6, 1)

                def turn(i):
                    if i:
                        pe.wait_ge(s_xdt, i)
                        pe.wait_ge(s_btok, i)
                    for m in range(12):
                        mm = pe.transpose(psum[:, m // 4, (m % 4) * P:(m % 4) * P + P],
                                          xb[:, m, i * P:i * P + P], const("ident"))
                    mm.then_inc(s_t6, 1)

                def decays(k):
                    i, g = C_UNITS[k]
                    if k >= 2:
                        pe.wait_ge(s_e, k - 1)
                    if k >= 1:
                        pe.wait_ge(s_pre, k)
                    if k == 0:
                        pe.wait_ge(s_csout, 1)
                    pe.matmul(psum[:, 3, 0:P], lhsT=xb[:, 8 + g, i * P:i * P + P],
                              rhs=xb[:, 12 + g, i * P:i * P + P], start=True, stop=True)
                    for j in range(HPG):
                        h = HPG * g + j
                        mm = pe.matmul(psum[:, 4 + k % 2, j * P:j * P + P],
                                       lhsT=adt[:, i, h:h + 1].to_broadcast([P, P]), rhs=const("upto"),
                                       start=True, stop=True)
                    mm.then_inc(s_csb, 1)

                def ys(k):
                    i, g = C_UNITS[k]
                    pe.wait_ge(s_mid, k + 1)
                    pe.wait_ge(s_btok, i + 1)
                    if k >= 1:
                        pe.wait_ge(s_post, k)
                    for j in range(HPG):
                        h = HPG * g + j
                        lo = 64 * (h % 2)
                        out = psum[lo:lo + 64, 6, (j // 2) * P:(j // 2) * P + P]
                        pe.matmul(out, lhsT=xdt[:, h * 64:h * 64 + 64], rhs=ebuf[:, k % 2, j * P:j * P + P],
                                  start=True, stop=(i == 0))
                        if i:
                            pe.matmul(out, lhsT=stT[:, h * 64:h * 64 + 64], rhs=chb[:, j * P:j * P + P],
                                      start=False, stop=True)
                    pe.matmul(psum[:, 7, 0:256], lhsT=btok[:, g * P:g * P + P],
                              rhs=xdtd[:, g * 256:g * 256 + 256], start=True, stop=True).then_inc(s_ys, 1)

                for k in range(NCU + 1):
                    if k < NCU and C_UNITS[k][1] == 0:
                        turn(C_UNITS[k][0])
                    if k < NCU:
                        decays(k)
                    if k >= 1:
                        ys(k - 1)

            @block.vector
            def _(dve):
                link = Link(dve, v_link6)
                link(dve.tensor_tensor(dt5, small[:, :, 0:H_SSD],
                                       param("dt_bias").unsqueeze(1).to_broadcast([P, 5, H_SSD]), ALU.add))
                link(dve.scalar_tensor_tensor(sp_e, dt5, -1.0, dt5, ALU.mult, ALU.min))
                dve.sem_inc(s_v6, 1)
                link(dve.tensor_scalar(dt5, dt5, 0.0, None, ALU.max))
                dve.wait_ge(s_e6, 1)
                link(dve.tensor_tensor(dt5, dt5, sp_e, ALU.add))
                dve.scalar_tensor_tensor(adt, dt5, -1.0, a_neg.unsqueeze(1).to_broadcast([P, 5, H_SSD]),
                                         ALU.mult, ALU.mult).then_inc(s_dt, 1)
                dve.wait_ge(s_csout, 1)

                def heads(ap):
                    return ap.rearrange("p (h n) -> p h n", n=P_SSD)

                def pre(k):
                    i, g = C_UNITS[k]
                    if g == 0:
                        dve.wait_ge(s_t6, i + 1)
                        if i:
                            dve.wait_ge(s_ys, k)
                        link(dve.tensor_tensor(
                            heads(xdt), psum[:, 0:2, :].rearrange("p a (h n) -> p (a h) n", n=P_SSD),
                            dt5[:, i, :].unsqueeze(2).to_broadcast([P, H_SSD, P_SSD]), ALU.mult))
                        dve.tensor_tensor(heads(xdtd), heads(xdt),
                                          dte[:, i, :].unsqueeze(2).to_broadcast([P, H_SSD, P_SSD]),
                                          ALU.mult).then_inc(s_xdt, 1)
                    dve.wait_ge(s_csb, k + 1)
                    e = ebuf[:, k % 2, :].rearrange("p (j n) -> p j n", n=P)
                    if k >= 2:
                        dve.wait_ge(s_ys, k - 1)
                    link(dve.tensor_tensor(
                        e, psum[:, 4 + k % 2, :].rearrange("p (j n) -> p j n", n=P),
                        cs5[:, i, HPG * g:HPG * g + HPG].unsqueeze(2).to_broadcast([P, HPG, P]),
                        ALU.subtract))
                    dve.tensor_tensor((cbm, cbm2)[k % 2], psum[:, 3, 0:P], const("upto"), ALU.mult)
                    dve.tensor_scalar(e, e, 0.0, None, ALU.min).then_inc(s_pre, 1)

                def mid(k):
                    i, g = C_UNITS[k]
                    dve.wait_ge(s_e, k + 1)
                    e = ebuf[:, k % 2, :].rearrange("p (j n) -> p j n", n=P)
                    ch = chb.rearrange("p (j n) -> p j n", n=P)
                    link(dve.tensor_copy(ecl[:, k % 2, :], ch[:, :, P - 1]))
                    dve.tensor_tensor(ch, ch, xb[:, 12 + g, i * P:i * P + P].unsqueeze(1).to_broadcast(
                        [P, HPG, P]), ALU.mult)
                    dve.tensor_tensor(e, e, (cbm, cbm2)[k % 2].unsqueeze(1).to_broadcast([P, HPG, P]),
                                      ALU.mult).then_inc(s_mid, 1)

                def post(k):
                    i, g = C_UNITS[k]
                    dve.wait_ge(s_ys, k + 1)
                    for j in range(2):
                        m = 2 * g + j
                        x_ = xb[:, m, i * P:i * P + P]
                        dve.scalar_tensor_tensor(x_, x_, param("d_skip")[:, m:m + 1],
                                                 psum[:, 6, j * P:j * P + P], ALU.mult, ALU.add)
                    st = stT[:, g * 256:g * 256 + 256]
                    if i:
                        link(dve.tensor_tensor(heads(st), heads(st), ecl[:, k % 2, :].unsqueeze(2).to_broadcast(
                            [P, HPG, P_SSD]), ALU.mult))
                        dve.tensor_tensor(st, st, psum[:, 7, 0:256], ALU.add).then_inc(s_post, 1)
                    else:
                        dve.tensor_copy(st, psum[:, 7, 0:256]).then_inc(s_post, 1)

                for k in range(NCU + 1):
                    if k < NCU:
                        pre(k)
                    if k >= 1:
                        post(k - 1)
                    if k < NCU:
                        mid(k)

        s_xn, s_t7, s_csb7, s_xd7, s_b7, s_e7, s_g7, s_y7, s_bm, s_su, s_sud, s_sou, s_c7 = (sem(n) for n in (
            "new_compact", "new_turned", "new_decays_psum", "new_xdt", "new_btok", "new_decays", "new_mix",
            "new_y_psum", "bmask_ready", "state_add_psum", "state_ready", "bmask_used", "new_args"))
        v_link7, a_link7, p_link7 = sem("dve_link7"), sem("act_link7"), sem("pool_link7")
        xn = A.at(a_s6, XBC, NEW)
        xdt7 = A.at(a_s6 + 512, D, parts=NEW)
        xdtd7 = A.at(a_s6 + 1536, D, parts=NEW)
        bt7 = A.at(a_s6 + 2560, 512, parts=NEW)
        bm7 = A.at(a_s6 + 3072, NB * P, parts=NEW)
        bm7b = A.at(a_xb + 8 * W_XB, 3, NB * P, parts=NEW)
        e7 = A.at(a_s6 + 4096, H_SSD * NEW, parts=NEW)
        ecp = A.at(a_s6 + 4608, 8, NEW)
        yn = A.at(a_xb + 8 * W_XB + 3072, 8, NEW)
        ytmp = A.at(a_xb + 8 * W_XB + 3072 + 256, 8, NEW)
        dec7 = A.at(a_xb + 8 * W_XB + 3072 + 512, H_SSD, NB)
        cb7 = A.at(a_xb + 8 * W_XB + 3072 + 640, G_SSD, NEW, parts=NEW)

        with nc.Block() as block:
            @block.gpsimd
            def _(pool):
                for m in range(XBC):
                    last = pool.tensor_copy(xn[:, m, :].rearrange("p (b t) -> p b t", t=NS),
                                            seq_new(xb[:, m, :], SEG_P, SEG_S, 0, NS))
                last.then_inc(s_xn, 1)
                pool.wait_ge(s_b7, 1)
                for g in range(G_SSD):
                    to = (bm7 if g == 0 else bm7b[:, g - 1, :]).rearrange("p (b n) -> p b n", n=P)
                    pool.tensor_tensor(to, bt7[:, g * P:g * P + P].unsqueeze(1).to_broadcast([NEW, NB, P]),
                                       const("in_seq", NEW).unsqueeze(2).to_broadcast([NEW, NB, P]),
                                       ALU.mult).then_inc(s_bm, 1)

            @block.tensor
            def _(pe):
                pe.wait_ge(s_xn, 1)
                for m in range(12):
                    mm = pe.transpose(psum[0:NEW, m // 4, (m % 4) * P:(m % 4) * P + P], xn[:, m, :],
                                      const("ident"))
                mm.then_inc(s_t7, 1)
                for g in range(G_SSD):
                    pe.matmul(psum[0:NEW, 3, g * NEW:g * NEW + NEW], lhsT=xn[:, 8 + g, :], rhs=xn[:, 12 + g, :],
                              start=True, stop=True)
                for h in range(H_SSD):
                    mm = pe.matmul(psum[:, 4, h * NEW:h * NEW + NEW],
                                   lhsT=adt[0:NEW, 4, h:h + 1].to_broadcast([NEW, P]),
                                   rhs=const("upto_new", NEW), start=True, stop=True)
                mm.then_inc(s_csb7, 1)
                pe.wait_ge(s_st6, 16)
                for b in range(NB):
                    for m in range(8):
                        mm = pe.matmul(psum[:, 5, m * NEW + b * NS:m * NEW + b * NS + NS],
                                       lhsT=states[:, b, m * P:m * P + P],
                                       rhs=xn[:, 12 + m // 2, b * NS:b * NS + NS], start=True, stop=True)
                pe.wait_ge(s_g7, 1)
                for h in range(H_SSD):
                    lo = 64 * (h % 2)
                    mm = pe.matmul(psum[lo:lo + 64, 6, (h // 2) * NEW:(h // 2) * NEW + NEW],
                                   lhsT=xdt7[:, h * 64:h * 64 + 64], rhs=e7[:, h * NEW:h * NEW + NEW],
                                   start=True, stop=True)
                mm.then_inc(s_y7, 1)
                pe.wait_ge(s_bm, G_SSD)
                for b in range(NB):
                    if b == 0:
                        pe.wait_ge(s_b7, 1)
                        pe.wait_ge(s_c7, 1)
                    if b >= 2:
                        pe.wait_ge(s_sud, b - 1)
                    for g in range(G_SSD):
                        bm = bm7 if g == 0 else bm7b[:, g - 1, :]
                        mm = pe.matmul(psum[:, 2 * (b % 2) + g // 2, (g % 2) * 256:(g % 2) * 256 + 256],
                                       lhsT=bm[:, b * P:b * P + P], rhs=xdtd7[:, g * 256:g * 256 + 256],
                                       start=True, stop=True)
                    mm.then_inc(s_su, 1)

            @block.scalar
            def _(act):
                act.wait_ge(s_t7, 1)
                act.activation(bt7, psum[0:NEW, 2, :], ACT.Copy).then_inc(s_b7, 1)
                act.wait_ge(s_c7, 1)
                csb = psum[:, 4, :].rearrange("p (m o n) -> p m o n", o=2, n=NEW)
                for o in range(2):
                    act.activation(ecp[64 * o:64 * o + 64], csb[64 * o:64 * o + 64, :, o, :], ACT.Exp)
                act.activation(dec7, psum[:, 4, :].rearrange("p (h b t) -> p h b t", b=NB, t=NS)[:, :, :, NS - 1],
                               ACT.Exp)
                act.activation(e7, e7, ACT.Exp).then_inc(s_e7, 1)

            @block.vector
            def _(dve):
                link = Link(dve, v_link7)
                heads = lambda ap: ap.rearrange("p (h n) -> p h n", n=P_SSD)
                dve.wait_ge(s_t7, 1)
                bc = lambda a: a[0:NEW, 4, :].unsqueeze(2).to_broadcast([NEW, H_SSD, P_SSD])
                link(dve.tensor_tensor(heads(xdt7), psum[0:NEW, 0:2, :].rearrange(
                    "p a (h n) -> p (a h) n", n=P_SSD), bc(dt5), ALU.mult))
                link(dve.tensor_tensor(heads(xdtd7), heads(xdt7), bc(dte), ALU.mult))
                dve.wait_ge(s_csb7, 1)
                e3 = e7.rearrange("p (h n) -> p h n", n=NEW)
                link(dve.tensor_tensor(e3, psum[0:NEW, 4, :].rearrange("p (h n) -> p h n", n=NEW),
                                       cs5[0:NEW, 4, :].unsqueeze(2).to_broadcast([NEW, H_SSD, NEW]),
                                       ALU.subtract))
                dve.tensor_tensor(cb7, psum[0:NEW, 3, 0:G_SSD * NEW].rearrange("p (g n) -> p g n", n=NEW),
                                  const("upto_new", NEW).unsqueeze(1).to_broadcast([NEW, G_SSD, NEW]), ALU.mult)
                dve.tensor_scalar(e7, e7, 0.0, None, ALU.min).then_inc(s_c7, 1)
                dve.wait_ge(s_e7, 1)
                for g in range(G_SSD):
                    at = g * HPG * NEW
                    e_g = e7[:, at:at + HPG * NEW].rearrange("p (j n) -> p j n", n=NEW)
                    last = dve.tensor_tensor(e_g, e_g, cb7[:, g, :].unsqueeze(1).to_broadcast(
                        [NEW, HPG, NEW]), ALU.mult)
                last.then_inc(s_g7, 1)
                dve.wait_ge(s_y7, 1)
                p7 = lambda bank: psum[:, bank, 0:8 * NEW].rearrange("p (m n) -> p m n", n=NEW)
                link(dve.tensor_tensor(ytmp, p7(5), ecp, ALU.mult))
                link(dve.tensor_tensor(ytmp, ytmp, p7(6), ALU.add))
                link(dve.tensor_tensor(yn, xn[:, 0:8, :], param("d_skip").unsqueeze(2).to_broadcast(
                    [P, 8, NEW]), ALU.mult))
                link(dve.tensor_tensor(yn, yn, ytmp, ALU.add))
                for b in range(NB):
                    st = states[:, b, :].rearrange("p (h n) -> p h n", n=P_SSD)
                    link(dve.tensor_tensor(st, st, dec7[:, :, b].unsqueeze(2).to_broadcast(
                        [P, H_SSD, P_SSD]), ALU.mult))
                    dve.wait_ge(s_su, b + 1)
                    bank = 2 * (b % 2)
                    dve.tensor_tensor(states[:, b, :], states[:, b, :],
                                      psum[:, bank:bank + 2, :].rearrange("p a n -> p (a n)"),
                                      ALU.add).then_inc(s_sud, 1)

            @block.sync
            def _(sp):
                for b in range(NB):
                    sp.wait_ge(s_sud, b + 1)
                    write(sp, outs["ssm_s"][:, b * D:(b + 1) * D], states[:, b, :])
                sp.wait_ge(s_out, outs_written[0])

        s_sz, s_gy, s_sq8, s_sqfree, s_ss8, s_std8, s_ya = (sem(n) for n in (
            "silu_z", "gated_y", "gated_squares", "squares_used", "group_sums", "group_std", "ya_ready"))
        v_link8 = sem("dve_link8")
        sq8 = A.at(a_s6, 2, NT)
        rs8 = A.at(a_s6 + 2 * NT, 2, NT)

        with nc.Block() as block:
            @block.scalar
            def _(act):
                for m in range(8):
                    act.activation(zT[:, m, :], zT[:, m, :], ACT.Silu).then_inc(s_sz, 1)
                for m in range(8):
                    act.wait_ge(s_gy, m + 1)
                    if m >= 2:
                        act.wait_ge(s_sqfree, m - 1)
                    act.activation(sq8[:, m % 2, :], zT[:, m, :], ACT.Square).then_inc(s_sq8, 1)
                for g in range(G_SSD):
                    act.wait_ge(s_ss8, g + 1)
                    if g >= 2:
                        act.wait_ge(s_ya, 2 * g - 2)
                    act.activation(halves(rs8[:, g % 2, :]), pair[g], ACT.Sqrt, bias=eps_col[:, 0:1],
                                   scale=1.0 / 256).then_inc(s_std8, 1)

            @block.tensor
            def _(pe):
                for m in range(8):
                    pe.wait_ge(s_sq8, m + 1)
                    for h in range(2):
                        mm = pe.matmul(pair[m // 2][:, h, :], lhsT=const("ones"),
                                       rhs=sq8[:, m % 2, h * HALF:(h + 1) * HALF],
                                       start=(m % 2 == 0), stop=(m % 2 == 1))
                    mm.then_inc(s_sqfree, 1)
                    if m % 2:
                        pe.wait_ge(s_sqfree, m + 1)
                        pe.sem_inc(s_ss8, 1)

            @block.vector
            def _(dve):
                link = Link(dve, v_link8)
                for m in range(8):
                    dve.wait_ge(s_sz, m + 1)
                    dve.tensor_tensor(zT[:, m, 0:SEQ], zT[:, m, 0:SEQ], xb[:, m, 0:SEQ], ALU.mult)
                    link(dve.tensor_tensor(zT[:, m, SEQ:NT], zT[:, m, SEQ:NT], yn[:, m, :], ALU.mult))
                    dve.sem_inc(s_gy, 1)
                for g in range(G_SSD):
                    r = rs8[:, g % 2, :]
                    dve.wait_ge(s_std8, g + 1)
                    link(dve.reciprocal(r, r))
                    for m in (2 * g, 2 * g + 1):
                        dve.scalar_tensor_tensor(zT[:, m, :], zT[:, m, :], param("ssm_norm")[:, m:m + 1], r,
                                                 ALU.mult, ALU.mult).then_inc(s_ya, 1)

        s_sig, s_pd, s_mg = sem("gate_ready"), sem("branch_added"), sem("merged_ready")
        v_link9 = sem("dve_link9")
        merged = A.at(a_xb, DC, NT)
        sg9 = A.at(a_tmp, 2, NT)
        tm9 = A.at(a_tmp + 2 * NT, NT)
        branch_of = [zT, A.at(a_q, 8, NT), yc]

        with nc.Block() as block:
            @block.sync
            def _(sp):
                load_tiles(sp, T_MERGE + RING, T_END)

            @block.tensor
            def _(pe):
                for u in range(48):
                    tile_ready(pe, T_MERGE + u)
                    e = u // 2
                    if e >= 2:
                        pe.wait_ge(s_sig if u % 2 else s_pd, e - 1)
                    act_of = hT if u % 2 else branch_of[e % 3]
                    project(pe, T_MERGE + u, pair[u % 4], act_of).then_inc(w_used, 1)

            @block.scalar
            def _(act):
                for e in range(24):
                    act.wait_ge(w_used, T_MERGE + 2 * e + 2)
                    if e >= 2:
                        act.wait_ge(s_pd, e - 1)
                    act.activation(halves(sg9[:, e % 2, :]), pair[(2 * e + 1) % 4],
                                   ACT.Sigmoid).then_inc(s_sig, 1)

            @block.vector
            def _(dve):
                for e in range(24):
                    m, i = e // 3, e % 3
                    dve.wait_ge(s_sig, e + 1)
                    to = tm9 if i else merged[:, m, :]
                    if e:
                        dve.wait_ge(s_mg, e)
                    dve.tensor_tensor(halves(to), halves(sg9[:, e % 2, :]), pair[(2 * e) % 4],
                                      ALU.mult).then_inc(s_pd, 1)
                    dve.wait_ge(s_pd, e + 1)
                    if i:
                        dve.tensor_tensor(merged[:, m, :], merged[:, m, :], tm9, ALU.add).then_inc(s_mg, 1)
                    else:
                        dve.sem_inc(s_mg, 1)

        s_x10, s_res = sem("x_again"), sem("residual_done")
        v_link10 = sem("dve_link10")

        def by_seq(a):
            return a.rearrange("p (b t) -> p b t", t=NS)

        def per_seq(cols):
            return cols[:, 1:NSEQ].unsqueeze(2).to_broadcast([P, NB, NS])

        with nc.Block() as block:
            @block.sync
            def _(sp):
                sp.dma_start(xT, ins["x"]).then_inc(s_x10, 16)

            @block.tensor
            def _(pe):
                for u in range(8):
                    tile_ready(pe, T_O + u)
                    if u >= 4:
                        pe.wait_ge(s_res, u - 3)
                    project(pe, T_O + u, pair[u % 4], merged).then_inc(w_used, 1)

            @block.vector
            def _(dve):
                link = Link(dve, v_link10)
                tmp = A.at(a_tmp, NEW)
                dve.wait_ge(s_x10, 16)
                rest = SEQ - HALF
                for m in range(8):
                    ps, gate = pair[m % 4], mods[:, 16 + m, :]
                    dve.wait_ge(w_used, T_O + m + 1)
                    for dst, src in ((xT[:, m, 0:HALF], ps[:, 0, :]), (xT[:, m, HALF:SEQ], ps[:, 1, 0:rest])):
                        dve.scalar_tensor_tensor(dst, src, gate[:, 0:1], dst, ALU.mult, ALU.add)
                    link(dve.tensor_tensor(by_seq(tmp), by_seq(ps[:, 1, rest:HALF]), per_seq(gate), ALU.mult))
                    new = xT[:, m, SEQ:NT]
                    link(dve.tensor_tensor(new, new, tmp, ALU.add))
                    dve.sem_inc(s_res, 1)

        s_sq11, s_ss11, s_std11, s_n11, s_hp11, s_hs11, s_rt, s_rl, s_ge, s_gi, s_pe2, s_pe2o = (sem(n) for n in (
            "squares2", "square_sums2", "std2", "normed2", "h2_prompt", "h2_sample", "router_logits",
            "router_logits_out", "group_exp", "group_args", "expert_exp", "expert_args"))
        s_row_ps, s_row_sb, s_rank, s_slot, s_tabinit, s_tabw, s_h2w, s_tabsrc, s_pad = (sem(n) for n in (
            "rows_in_psum", "rows_in_sbuf", "ranks_in_psum", "slots_ready", "table_cleared", "table_written",
            "h2_written", "table_source", "router_padded"))
        v_link11 = sem("dve_link11")
        s_h2w = (s_h2w, sem("h2_written1"))
        sq11 = A.at(a_z, DC, NT)
        rstd11 = A.at(a_tmp, NT)
        a_r = a_tmp + NT
        NR = 5
        lg = A.at(a_r, NR, 36)
        gpad = A.at(a_r + 180, NR, 8)
        g8, e8 = A.at(a_r + 220, NR, 8), A.at(a_r + 260, NR, 8)
        gi8, ei8 = A.at(a_r + 300, NR, 8), A.at(a_r + 340, NR, 8)
        gif, eif = A.at(a_r + 380, NR, 1), A.at(a_r + 385, NR, 2)
        goh = A.at(a_r + 395, NR, NG)
        gexp = A.at(a_r + 415, NR, NG)
        gsum = A.at(a_r + 435, NR)
        masked = A.at(a_r + 440, NR, NG, EPG)
        fine = A.at(a_r + 600, NR, EPG)
        oh = [A.at(a_r + 640 + 40 * k, NR, EPG) for k in range(2)]
        full = [A.at(a_r + 720 + 160 * k, NR, NE) for k in range(2)]
        both = A.at(a_r + 1040, NR, NE)
        slotm = A.at(a_r + 1200, NR, NE)
        tmp32 = A.at(a_r + 1360, NR, NE)
        slotf = A.at(a_r + 1520, 2, NR)
        p2 = A.at(a_r + 1530, NR)
        cnt = A.at(a_r + 1535, NE)
        mx = A.at(a_r + 1567, 8)
        wcol = A.at(a_param + PARAM_AT["conv_prev"][0], 2, NR)
        a_keep = a_param + PARAM_AT["conv_prev"][0] + 16
        slot_i = A.at(a_keep, 2, NR).bitcast(I32)
        value_i = A.at(a_keep + 10, 2, NR).bitcast(I32)
        rounds_i = A.at(a_keep + 20, 1).bitcast(I32)
        none_i = A.at(a_keep + 21, NR * NE).bitcast(I32)
        rows11 = A.at(a_xb, 2, D)
        CAP = P
        NO_ROW = 4 * NT
        table = nc.dram_tensor("slot_table", [NR * CAP * NE, 1], I32).ap()
        h2_rows = nc.dram_tensor("h2_rows", [NT, D], F32).ap()
        y_rows = nc.dram_tensor("y_rows", [2 * NT, D], F32).ap()

        with nc.Block() as block:
            @block.scalar
            def _(act):
                for c in range(DC):
                    act.activation(sq11[:, c, :], xT[:, c, :], ACT.Square).then_inc(s_sq11, 1)
                act.wait_ge(s_ss11, 1)
                act.activation(halves(rstd11), pair[0], ACT.Sqrt, bias=eps_col[:, 0:1],
                               scale=1.0 / D).then_inc(s_std11, 1)
                for c in range(DC):
                    act.wait_ge(s_n11, c + 1)
                    act.activation(hT[:, c, 0:SEQ], sq11[:, c, 0:SEQ], ACT.Identity,
                                   bias=mods[:, 24 + c, 0:1], scale=gain[:, 1, c, 0:1]).then_inc(s_hp11, 1)
                act.wait_ge(s_gi, 1)
                act.activation(gexp, gexp, ACT.Exp).then_inc(s_ge, 1)
                act.wait_ge(s_pe2o, 1)
                act.activation(p2, p2, ACT.Exp).then_inc(s_pe2, 1)
                for i in range(NR):
                    m = P if i < 4 else NEW
                    act.wait_ge(s_row_ps, i + 1)
                    if i >= 2:
                        act.wait_ge(s_h2w[i % 2], 16 * (i // 2))
                    b = 2 + 2 * (i % 2)
                    act.activation(rows11[0:m, i % 2, :].rearrange("p (a n) -> p a n", n=512),
                                   psum[0:m, b:b + 2, :], ACT.Copy).then_inc(s_row_sb, 1)

            @block.tensor
            def _(pe):
                for c in range(DC):
                    pe.wait_ge(s_sq11, c + 1)
                    for h in range(2):
                        mm = pe.matmul(pair[0][:, h, :], lhsT=const("ones"),
                                       rhs=sq11[:, c, h * HALF:(h + 1) * HALF],
                                       start=(c == 0), stop=(c == DC - 1))
                mm.then_inc(s_ss11, 1)
                pe.wait_ge(s_hp11, DC)
                pe.wait_ge(s_hs11, DC)
                router = param("router").rearrange("p (c n) -> p c n", n=36)
                for i in range(NR):
                    m = P if i < 4 else NEW
                    for c in range(DC):
                        mm = pe.matmul(psum[0:m, 6, i * 36:i * 36 + 36], lhsT=hT[:, c, i * P:i * P + m],
                                       rhs=router[:, c, :], start=(c == 0), stop=(c == DC - 1))
                mm.then_inc(s_rt, 1)
                for i in range(NR):
                    m = P if i < 4 else NEW
                    if i >= 2:
                        pe.wait_ge(s_row_sb, i - 1)
                    for c in range(DC):
                        mm = pe.transpose(psum[0:m, 2 + 2 * (i % 2) + c // 4, (c % 4) * P:(c % 4) * P + P],
                                          hT[:, c, i * P:i * P + m], const("ident"))
                    mm.then_inc(s_row_ps, 1)
                pe.wait_ge(s_rl, 2)
                for i in range(NR):
                    m = P if i < 4 else NEW
                    for j in range(i):
                        pe.matmul(psum[0:m, 7, i * NE:i * NE + NE], lhsT=const("ones")[:, 0:m],
                                  rhs=both[:, j, :], start=(j == 0), stop=False)
                    pe.matmul(psum[0:m, 7, i * NE:i * NE + NE], lhsT=const("upto")[0:m, 0:m],
                              rhs=both[0:m, i, :], start=(i == 0), stop=True)
                for j in range(NR):
                    m = P if j < 4 else NEW
                    mm = pe.matmul(psum[:, 7, NR * NE:(NR + 1) * NE], lhsT=const("ones")[0:m, :],
                                   rhs=both[0:m, j, :], start=(j == 0), stop=(j == NR - 1))
                mm.then_inc(s_rank, 1)

            @block.vector
            def _(dve):
                link = Link(dve, v_link11)
                dve.memset(none_i, NO_ROW).then_inc(s_tabinit, 1)
                dve.memset(lg[:, 4, :], 0.0)
                dve.memset(slotm[:, 4, :], 0.0)
                link(dve.memset(gpad, -3e38))
                dve.wait_ge(s_std11, 1)
                link(dve.reciprocal(rstd11, rstd11))
                for c in range(DC):
                    dve.tensor_tensor(sq11[:, c, :], xT[:, c, :], rstd11, ALU.mult).then_inc(s_n11, 1)
                dve.wait_ge(s_n11, DC)
                for c in range(DC):
                    new = by_seq(sq11[:, c, SEQ:NT])
                    link(dve.tensor_tensor(new, new, per_seq(gain[:, 1, c, :]), ALU.mult))
                    dve.tensor_tensor(by_seq(hT[:, c, SEQ:NT]), new, per_seq(mods[:, 24 + c, :]),
                                      ALU.add).then_inc(s_hs11, 1)
                dve.wait_ge(s_rt, 1)
                dve.tensor_copy(lg[:, 0:4, :], psum[:, 6, 0:144].rearrange("p (a b) -> p a b", b=36))
                link(dve.tensor_copy(lg[0:NEW, 4, :], psum[0:NEW, 6, 144:180]))
                link(dve.tensor_copy(gpad[:, :, 0:NG], lg[:, :, 0:NG]))

                def top_of(vals, best, idx):
                    for i in range(NR):
                        last = dve.max(best[:, i, :], vals[:, i, :])
                    link(last)
                    for i in range(NR):
                        last = dve.max_index(idx[:, i, :].bitcast(U32), best[:, i, :], vals[:, i, :])
                    link(last)

                bc = lambda a, *s: a.to_broadcast([P, *s])
                iota = const("iota8")
                top_of(gpad, g8, gi8)
                link(dve.tensor_copy(gif, gi8[:, :, 0:1].bitcast(U32)))
                dve.tensor_tensor(goh, bc(iota[:, 0:NG].unsqueeze(1), NR, NG), bc(gif, NR, NG), ALU.is_equal)
                link(dve.tensor_tensor(gexp, lg[:, :, 0:NG], bc(g8[:, :, 0:1], NR, NG), ALU.subtract))
                dve.sem_inc(s_gi, 1)
                link(dve.tensor_tensor(masked, lg[:, :, NG:NG + NE].rearrange("p i (g e) -> p i g e", e=EPG),
                                       bc(goh.unsqueeze(3), NR, NG, EPG), ALU.mult))
                link(dve.tensor_reduce(fine, masked.rearrange("p i g e -> p i e g"), AX, ALU.add))
                top_of(fine, e8, ei8)
                link(dve.tensor_copy(eif, ei8[:, :, 0:2].bitcast(U32)))
                for k in range(2):
                    link(dve.tensor_tensor(oh[k], bc(iota.unsqueeze(1), NR, EPG),
                                           bc(eif[:, :, k:k + 1], NR, EPG), ALU.is_equal))
                    for g in range(NG):
                        last = dve.tensor_tensor(full[k][:, :, g * EPG:g * EPG + EPG], oh[k],
                                                 bc(goh[:, :, g:g + 1], NR, EPG), ALU.mult)
                    link(last)
                link(dve.tensor_tensor(both, full[0], full[1], ALU.add))
                dve.sem_inc(s_rl, 2)
                link(dve.tensor_tensor(p2, e8[:, :, 1], e8[:, :, 0], ALU.subtract))
                dve.sem_inc(s_pe2o, 1)
                dve.wait_ge(s_ge, 1)
                link(dve.tensor_reduce(gsum, gexp, AX, ALU.add))
                dve.wait_ge(s_pe2, 1)
                link(dve.scalar_tensor_tensor(mx[:, 0:NR], p2, 1.0, gsum, ALU.add, ALU.mult))
                link(dve.reciprocal(wcol[:, 0, :], mx[:, 0:NR]))
                link(dve.tensor_tensor(wcol[:, 1, :], wcol[:, 0, :], p2, ALU.mult))
                dve.wait_ge(s_rank, 1)
                dve.tensor_scalar(slotm[:, 0:4, :], psum[:, 7, 0:4 * NE].rearrange("p (a b) -> p a b", b=NE),
                                  -1.0, float(NE), ALU.add, ALU.mult)
                dve.tensor_scalar(slotm[0:NEW, 4, :], psum[0:NEW, 7, 4 * NE:5 * NE], -1.0, float(NE),
                                  ALU.add, ALU.mult)
                link(dve.tensor_reduce(mx[:, 0:1], psum[:, 7, NR * NE:(NR + 1) * NE], AX, ALU.max))
                link(dve.tensor_tensor(slotm, slotm, bc(const("iota32").unsqueeze(1), NR, NE), ALU.add))
                for k in range(2):
                    link(dve.tensor_tensor(tmp32, slotm, full[k], ALU.mult))
                    link(dve.tensor_reduce(slotf[:, k, :], tmp32, AX, ALU.add))
                dve.tensor_copy(slot_i, slotf)
                link(dve.tensor_scalar(mx[:, 1:2], mx[:, 0:1], float(CAP), 1.0, ALU.is_gt, ALU.add))
                for j in range(2, NR):
                    link(dve.scalar_tensor_tensor(mx[:, j:j + 1], mx[:, 0:1], float(CAP * j),
                                                  mx[:, j - 1:j], ALU.is_gt, ALU.add))
                link(dve.tensor_copy(rounds_i, mx[:, NR - 1:NR]))
                link(dve.tensor_copy(value_i, const("row_values").rearrange("p (a b) -> p a b", b=NR)))
                dve.sem_inc(s_slot, 1)

            @block.sync
            def _(sp):
                for i in range(NR):
                    m = P if i < 4 else NEW
                    sp.wait_ge(s_row_sb, i + 1)
                    sp.dma_start(h2_rows[i * P:i * P + m, :], rows11[0:m, i % 2, :]).then_inc(s_h2w[i % 2], 16)
                sp.wait_ge(s_h2w[0], 16 * 3)
                sp.wait_ge(s_h2w[1], 16 * 2)

            @block.gpsimd
            def _(pool):
                pool.wait_ge(s_tabinit, 1)
                pool.dma_start(table.rearrange("(p n) o -> p (n o)", p=P), none_i).then_inc(s_tabw, 16)
                pool.wait_ge(s_slot, 1)
                pool.wait_ge(s_tabw, 16)
                for k in range(2):
                    for i in range(NR):
                        m = P if i < 4 else NEW
                        pool.indirect_dma_start(
                            out=table, out_offset=bass.IndirectOffsetOnAxis(slot_i[0:m, k, i:i + 1], 0),
                            in_=value_i[0:m, k, i:i + 1], in_offset=None).then_inc(s_tabw, 16)
                pool.wait_ge(s_tabw, 16 * (1 + 2 * NR))

        s_tab, s_idx, s_gath, s_scat, s_rows, s_wgu, s_wdn, s_xps, s_xsb, s_gu, s_act, s_silu12, s_aps, s_asb = (
            sem(n) for n in ("table_loaded", "gather_index", "rows_gathered", "rows_scattered", "rows_cleared",
                             "wgu_loaded", "wdown_loaded", "x_turned", "x_out", "gate_up", "act_ready",
                             "silu_ready", "act_turned", "act_out"))
        s_dn, s_yo, s_gath1, s_scat1, s_wgu1, s_wdn1, s_round, s_passed = (sem(n) for n in (
            "down_ready", "y_staged", "rows_gathered1", "rows_scattered1", "wgu_loaded1", "wdown_loaded1",
            "round_done", "dma_may_start"))
        v_link12 = sem("dve_link12")
        gath, scat, wgu_full, wdn_full = (s_gath, s_gath1), (s_scat, s_scat1), (s_wgu, s_wgu1), (s_wdn, s_wdn1)
        a_e = a_q
        w_gu = A.at(a_e, 2, 2 * DC * FF)
        w_dn = A.at(a_e + 8192, 2, 2 * D)
        xg = A.at(a_e + 12288, 2, D)
        xgT = A.at(a_e + 14336, 2, DC * P)
        actb = A.at(a_e + 16384, 2, FF)
        actT = A.at(a_e + 16896, 2, 2 * P)
        yst = A.at(a_e + 17408, 2, D)
        sil = A.at(a_e + 19456, 2, FF)
        tab_i = A.at(a_e + 19968, NE).bitcast(I32)
        gat_i = A.at(a_e + 20000, NE).bitcast(I32)

        with nc.Block() as block:
            def rounds(eng):
                return eng.value_load(rounds_i[0:1, 0:1], min_val=1, max_val=NR)

            @block.sync
            def _(sp):
                def gate_up_in(r, e2, k):
                    sp.wait_ge(s_gu, r * NE + e2 * 2 + (k + 1))
                    sp.dma_start(w_gu[:, k, :], ins["w_gu"][bass.ds(e2 * 2 + k, 1)].rearrange(
                        "a p n -> (a p) n")).then_inc(wgu_full[k], 16)

                def down_in(r, e2, k):
                    sp.wait_ge(s_dn, r * NE + e2 * 2 + (k + 1))
                    sp.dma_start(w_dn[:, k, :], ins["w_down"][bass.ds(e2 * 2 + k, 1)].rearrange(
                        "a p n -> (a p) n")).then_inc(wdn_full[k], 16)

                with sp.Fori(0, rounds(sp)) as r:
                    sp.wait_ge(s_round, r + 1)
                    sp.dma_start(tab_i, table[bass.ds(r * (CAP * NE), CAP * NE), :].rearrange(
                        "(p n) o -> p (n o)", p=P)).then_inc(s_tab, 16)
                    gate_up_in(r, 0, 0)
                    gate_up_in(r, 0, 1)
                    with sp.Fori(1, NE // 2) as e2:
                        down_in(r, e2 - 1, 0)
                        gate_up_in(r, e2, 0)
                        down_in(r, e2 - 1, 1)
                        gate_up_in(r, e2, 1)
                    down_in(r, NE // 2 - 1, 0)
                    down_in(r, NE // 2 - 1, 1)

            @block.gpsimd
            def _(pool):
                pool.memset(xg, 0.0).then_inc(s_rows, 1)
                pool.sem_inc(s_xps, 2)
                pool.sem_inc(s_round, 1)
                last_token, last_row = pool.to_reg(NT - 1), pool.to_reg(2 * NT - 1)
                with pool.Fori(0, rounds(pool)) as r:
                    pool.wait_ge(s_idx, r + 1)
                    pool.wait_ge(s_rows, 1)
                    for e in range(NE + 3):
                        k = e % 2
                        if e < NE:
                            pool.wait_ge(s_xps, r * NE + (e + 1))
                            pool.sem_inc(s_passed, 1)
                            pool.indirect_dma_start(
                                out=xg[:, k, :], out_offset=None, in_=h2_rows,
                                in_offset=bass.IndirectOffsetOnAxis(gat_i[:, e:e + 1], 0),
                                bounds_check=last_token, oob_is_err=False).then_inc(gath[k], 16)
                        if e >= 3:
                            k = (e - 3) % 2
                            pool.wait_ge(s_yo, r * NE + (e - 1))
                            pool.sem_inc(s_passed, 1)
                            pool.indirect_dma_start(
                                out=y_rows, out_offset=bass.IndirectOffsetOnAxis(tab_i[:, e - 3:e - 2], 0),
                                in_=yst[:, k, :], in_offset=None,
                                bounds_check=last_row, oob_is_err=False).then_inc(scat[k], 16)
                    pool.wait_ge(scat[0], r * (8 * NE) + 8 * NE)
                    pool.wait_ge(scat[1], r * (8 * NE) + 8 * NE)
                    pool.sem_inc(s_round, 1)

            @block.tensor
            def _(pe):
                def at(r, e2, k):
                    return r * NE + e2 * 2 + k, r * (8 * NE) + e2 * 16 + 16

                def turn_x(r, e2, k):
                    n, half = at(r, e2, k)
                    pe.wait_ge(gath[k], half)
                    pe.wait_ge(s_xsb, n + 1)
                    for c in range(DC):
                        mm = pe.transpose(psum[:, c // 4, (c % 4) * P:(c % 4) * P + P],
                                          xg[:, k, c * P:c * P + P], const("ident"))
                    mm.then_inc(s_xps, 1)

                def gate_up(r, e2, k):
                    n, half = at(r, e2, k)
                    pe.wait_ge(s_xsb, n + 2)
                    pe.wait_ge(wgu_full[k], half)
                    pe.wait_ge(s_act, n + 1)
                    wv = w_gu[:, k, :].rearrange("p (o c f) -> p c o f", o=2, c=DC)
                    for c in range(DC):
                        mm = pe.matmul(psum[:, 2 + k, :].rearrange("p (o f) -> p o f", o=2),
                                       lhsT=xgT[:, k, c * P:c * P + P], rhs=wv[:, c],
                                       start=(c == 0), stop=(c == DC - 1))
                    mm.then_inc(s_gu, 1)

                def turn_act(r, e2, k):
                    n, _ = at(r, e2, k)
                    pe.wait_ge(s_act, n + 3)
                    for f in range(2):
                        mm = pe.transpose(psum[:, 6, f * P:f * P + P], actb[:, k, f * P:f * P + P],
                                          const("ident"))
                    mm.then_inc(s_aps, 1)

                def down(r, e2, k):
                    n, half = at(r, e2, k)
                    pe.wait_ge(s_asb, n + 1)
                    pe.wait_ge(wdn_full[k], half)
                    pe.wait_ge(s_yo, n + 1)
                    for h in range(2):
                        for f in range(2):
                            mm = pe.matmul(psum[:, 4 + h, :], lhsT=actT[:, k, f * P:f * P + P],
                                           rhs=w_dn[:, k, f * D + h * 512:f * D + h * 512 + 512],
                                           start=(f == 0), stop=(f == 1))
                    mm.then_inc(s_dn, 1)

                def two_experts(r, e2, first=False, last=False):
                    gate_up(r, e2, 0)
                    turn_x(r, e2, 1)
                    if not first:
                        down(r, e2 - 1, 1)
                    turn_act(r, e2, 0)
                    gate_up(r, e2, 1)
                    if not last:
                        turn_x(r, e2 + 1, 0)
                    down(r, e2, 0)
                    turn_act(r, e2, 1)

                pe.sem_inc(s_gu, 2)
                pe.sem_inc(s_dn, 2)
                with pe.Fori(0, rounds(pe)) as r:
                    turn_x(r, 0, 0)
                    two_experts(r, 0, first=True)
                    with pe.Fori(1, NE // 2 - 1) as e2:
                        two_experts(r, e2)
                    two_experts(r, NE // 2 - 1, last=True)
                    down(r, NE // 2 - 1, 1)

            @block.scalar
            def _(act):
                def x_out(r, e2, k):
                    act.wait_ge(s_xps, r * NE + e2 * 2 + k + 3)
                    act.activation(xgT[:, k, :].rearrange("p (a n) -> p a n", n=512), psum[:, 0:2, :],
                                   ACT.Copy).then_inc(s_xsb, 1)

                def two_experts(r, e2, last=False):
                    for k in range(2):
                        n = r * NE + e2 * 2 + k
                        act.wait_ge(s_gu, n + 3)
                        act.activation(sil[:, k, :], psum[:, 2 + k, 0:FF], ACT.Silu).then_inc(s_silu12, 1)
                        if k == 0:
                            x_out(r, e2, 1)
                        elif not last:
                            x_out(r, e2 + 1, 0)
                        act.wait_ge(s_aps, n + 1)
                        act.activation(actT[:, k, :], psum[:, 6, 0:2 * P], ACT.Copy).then_inc(s_asb, 1)

                act.sem_inc(s_xsb, 1)
                with act.Fori(0, rounds(act)) as r:
                    x_out(r, 0, 0)
                    with act.Fori(0, NE // 2 - 1) as e2:
                        two_experts(r, e2)
                    two_experts(r, NE // 2 - 1, last=True)

            @block.vector
            def _(dve):
                def mix(r, e2, k):
                    n = r * NE + e2 * 2 + k
                    dve.wait_ge(s_silu12, n + 1)
                    dve.tensor_tensor(actb[:, k, :], sil[:, k, :], psum[:, 2 + k, FF:2 * FF],
                                      ALU.mult).then_inc(s_act, 1)

                def y_out(r, e2, k, first=False):
                    dve.wait_ge(s_dn, r * NE + e2 * 2 + k + 3)
                    if not first:
                        dve.wait_ge(scat[k], r * (8 * NE) + e2 * 16)
                    dve.tensor_copy(yst[:, k, :].rearrange("p (a n) -> p a n", n=512),
                                    psum[:, 4:6, :]).then_inc(s_yo, 1)

                dve.sem_inc(s_act, 2)
                dve.sem_inc(s_yo, 1)
                with dve.Fori(0, rounds(dve)) as r:
                    dve.wait_ge(s_tab, r * 16 + 16)
                    dve.tensor_scalar(gat_i, tab_i, 1, None, ALU.logical_shift_right).then_inc(s_idx, 1)
                    mix(r, 0, 0)
                    mix(r, 0, 1)
                    y_out(r, 0, 0, first=True)
                    mix(r, 1, 0)
                    y_out(r, 0, 1, first=True)
                    mix(r, 1, 1)
                    y_out(r, 1, 0)
                    with dve.Fori(2, NE // 2) as e2:
                        mix(r, e2, 0)
                        y_out(r, e2 - 1, 1)
                        mix(r, e2, 1)
                        y_out(r, e2, 0)
                    y_out(r, NE // 2 - 1, 1)

        s_yr, s_yc, s_yt, s_yres, s_sq13, s_ss13, s_std13, s_y13 = (sem(n) for n in (
            "y_rows_loaded", "y_rows_added", "y_rows_turned", "y_residual", "squares3", "square_sums3", "std3",
            "y_ready"))
        v_link13 = sem("dve_link13")
        yr = A.at(a_q, NR, 2 * D)
        sq13 = A.at(a_q + NR * 2 * D, DC, NT)
        rstd13 = A.at(a_q + NR * 2 * D + DC * NT, NT)
        tmp13 = A.at(a_q + NR * 2 * D + DC * NT + NT, NEW)

        with nc.Block() as block:
            @block.sync
            def _(sp):
                for i in range(NR):
                    m = P if i < 4 else NEW
                    sp.dma_start(yr[0:m, i, :], y_rows[2 * i * P:2 * i * P + 2 * m, :].rearrange(
                        "(p w) n -> p (w n)", w=2)).then_inc(s_yr, 16)
                for c in range(DC):
                    sp.wait_ge(s_y13, c + 1)
                    write(sp, outs["y"][:, c, :], sq13[:, c, :])
                sp.wait_ge(s_out, outs_written[0])

            @block.tensor
            def _(pe):
                for i in range(NR):
                    m = P if i < 4 else NEW
                    pe.wait_ge(s_yc, i + 1)
                    if i >= 2:
                        pe.wait_ge(s_yres, i - 1)
                    for c in range(DC):
                        mm = pe.transpose(psum[:, 2 * (i % 2) + c // 4, (c % 4) * P:(c % 4) * P + m],
                                          yr[0:m, i, c * P:c * P + P], const("ident", m)[:, 0:m])
                    mm.then_inc(s_yt, 1)
                for c in range(DC):
                    pe.wait_ge(s_sq13, c + 1)
                    for h in range(2):
                        mm = pe.matmul(pair[2][:, h, :], lhsT=const("ones"),
                                       rhs=sq13[:, c, h * HALF:(h + 1) * HALF],
                                       start=(c == 0), stop=(c == DC - 1))
                mm.then_inc(s_ss13, 1)

            @block.scalar
            def _(act):
                act.wait_ge(s_yres, NR)
                for c in range(DC):
                    act.activation(sq13[:, c, :], xT[:, c, :], ACT.Square).then_inc(s_sq13, 1)
                act.wait_ge(s_ss13, 1)
                act.activation(halves(rstd13), pair[2], ACT.Sqrt, bias=eps_col[:, 0:1],
                               scale=1.0 / D).then_inc(s_std13, 1)

            @block.vector
            def _(dve):
                link = Link(dve, v_link13)
                for i in range(NR):
                    m = P if i < 4 else NEW
                    dve.wait_ge(s_yr, 16 * NR)
                    a, b = yr[0:m, i, 0:D], yr[0:m, i, D:2 * D]
                    link(dve.tensor_scalar(a, a, wcol[0:m, 0, i:i + 1], None, ALU.mult))
                    dve.scalar_tensor_tensor(a, b, wcol[0:m, 1, i:i + 1], a, ALU.mult,
                                             ALU.add).then_inc(s_yc, 1)
                for i in range(NR):
                    dve.wait_ge(s_yt, i + 1)
                    for c in range(DC):
                        ps = psum[:, 2 * (i % 2) + c // 4, (c % 4) * P:(c % 4) * P + (P if i < 4 else NEW)]
                        if i < 4:
                            dst = xT[:, c, i * P:i * P + P]
                            last = dve.scalar_tensor_tensor(dst, ps, mods[:, 40 + c, 0:1], dst, ALU.mult, ALU.add)
                        else:
                            link(dve.tensor_tensor(by_seq(tmp13), by_seq(ps), per_seq(mods[:, 40 + c, :]),
                                                   ALU.mult))
                            last = dve.tensor_tensor(xT[:, c, SEQ:NT], xT[:, c, SEQ:NT], tmp13, ALU.add)
                            link(last)
                    if i < 4:
                        last.then_inc(s_yres, 1)
                    else:
                        dve.sem_inc(s_yres, 1)
                dve.wait_ge(s_std13, 1)
                link(dve.reciprocal(rstd13, rstd13))
                for c in range(DC):
                    dve.scalar_tensor_tensor(sq13[:, c, :], xT[:, c, :], param("final")[:, c:c + 1], rstd13,
                                             ALU.mult, ALU.mult).then_inc(s_y13, 1)



def inputs_of(x_prompt, x_sample, c_prompt, c_sample, cache_k, cache_v, cache_kidx, state_ssm, state_ssm_conv,
              state_sc_conv, page_table, ada_w, ada_b, norm1_w, norm2_w, w_in, ssm_conv_w, ssm_conv_b,
              ssm_dt_bias, ssm_a_log, ssm_d, ssm_norm_w, sc_conv_w, rel_bias, w_out_ssm, w_out_att, w_out_sc,
              w_o, router_group_w, router_expert_w, exp_w_gate, exp_w_up, exp_w_down, final_norm_w):
    f = lambda a: np.asarray(a)

    def cols(v):
        v = f(v)
        return v.reshape(-1, P).T

    def tiles(w):
        w = f(w)
        return w.reshape(DC, P, -1, P).transpose(2, 1, 0, 3).reshape(-1, P, DC * P)

    wi = f(w_in)[0]

    def cut(at, n):
        return tiles(wi[:, at:at + n])

    ki = wi[:, O_KI:O_KI + D_IDX]
    narrow = np.concatenate([wi[:, O_DT:O_DT + H_SSD], wi[:, O_WI:O_WI + H_IDX],
                             np.zeros((D, P - 24), wi.dtype)], 1)
    c_, h_, b_ = cut(O_GC, D), cut(O_HV, D), cut(O_GB, D)
    gates = [cut(O_GATE + i * D, D) for i in range(3)]
    projections = [tiles(f(w)[0]) for w in (w_out_ssm, w_out_att, w_out_sc)]
    ada = tiles(f(ada_w)[0])
    stream = [ada[:T_KI], tiles(np.concatenate([ki, ki], 1)), cut(O_QI, 512), tiles(narrow),
              cut(O_K, 256), cut(O_V, 256), cut(O_Q, D), cut(O_Z, D), cut(O_XBC, 2048),
              np.stack([c_, h_, b_], 1).reshape(24, P, D), ada[T_KI:],
              np.stack([projections[0], gates[0], projections[1], gates[1], projections[2], gates[2]],
                       1).reshape(48, P, D),
              tiles(f(w_o)[0])]
    weights = np.concatenate(stream, 0)
    assert weights.shape[0] == T_END

    def feat(a):
        return f(a).reshape(-1, DC, P).transpose(2, 1, 0)

    x = np.concatenate([f(x_prompt).reshape(SEQ, D), f(x_sample).reshape(NEW, D)], 0)
    c = np.concatenate([f(c_prompt), f(c_sample)], 0)
    router = np.concatenate([f(router_group_w)[0], f(router_expert_w)[0]], 1)
    rel = np.zeros((P, H_ATT), np.float32)
    rel[:32] = f(rel_bias)
    part = {
        "ada_b": cols(f(ada_b)[0]), "norm1": cols(f(norm1_w)[0]), "norm2": cols(f(norm2_w)[0]),
        "final": cols(final_norm_w),
        "conv_w": f(ssm_conv_w)[0].reshape(K_SSD, XBC, P).transpose(2, 1, 0).reshape(P, -1),
        "conv_b": cols(f(ssm_conv_b)[0]),
        "sc_w": f(sc_conv_w)[0].reshape(K_SC, 8, P).transpose(2, 1, 0).reshape(P, -1),
        "dt_bias": np.broadcast_to(f(ssm_dt_bias), (P, H_SSD)), "a_log": np.broadcast_to(f(ssm_a_log), (P, H_SSD)),
        "d_skip": cols(np.repeat(f(ssm_d)[0], P_SSD)), "ssm_norm": cols(f(ssm_norm_w)[0]), "rel_bias": rel,
        "c": feat(c).reshape(P, -1), "router": router.reshape(DC, P, 36).transpose(1, 0, 2).reshape(P, -1),
        "conv_prev": f(state_ssm_conv)[0].reshape(NB, 3, XBC, P).transpose(3, 2, 0, 1).reshape(P, -1),
        "sc_prev": f(state_sc_conv)[0].reshape(NB, 2, 8, P).transpose(3, 2, 0, 1).reshape(P, -1),
    }
    params = np.concatenate([part[n] for n in PARAM_AT], 1)
    assert params.shape == (P, PARAM_W)
    ck, cv, ci = f(cache_k)[0], f(cache_v)[0], f(cache_kidx)[0]
    pages_k = ck.transpose(0, 3, 2, 1).reshape(POOL, P, KV * PAGE)
    pages_v = cv.reshape(POOL, PAGE, KV * DH)
    pages_i = ci.transpose(0, 2, 1)
    state = f(state_ssm)[0].transpose(3, 0, 1, 2).reshape(N_SSD, NB * D)
    w_gu = np.stack([f(exp_w_gate)[0], f(exp_w_up)[0]], 1)
    w_gu = w_gu.reshape(NE, 2, DC, P, FF).transpose(0, 3, 1, 2, 4).reshape(NE, P, 2 * DC * FF)
    w_down = f(exp_w_down)[0].reshape(NE, 2, P, D).transpose(0, 2, 1, 3).reshape(NE, P, 2 * D)
    arrays = {"weights": weights, "params": params, "consts": np.concatenate(list(shape_constants().values()), 1),
              "x": feat(x), "pages_k": pages_k, "pages_v": pages_v, "pages_i": pages_i, "state": state,
              "page_table": f(page_table).reshape(1, -1), "w_gu": w_gu, "w_down": w_down}
    return {k: np.ascontiguousarray(v) for k, v in arrays.items()}


OUTS = {"y": (P, DC, NT), "k": (P, 2, NT), "v": (P, 5, 256), "ki": (D_IDX, NT), "ssm_p": (N_SSD, D),
        "conv": (P, XBC, 27), "sc_conv": (P, 8, 18), "ssm_s": (N_SSD, NB * D)}


def launch(nc, arrays):
    ins = {k: nc.dram_tensor(f"in_{k}", a.shape, mybir.dt.from_np(a.dtype), kind="ExternalInput").ap()
           for k, a in arrays.items()}
    outs = {k: nc.dram_tensor(f"out_{k}", s, F32, kind="ExternalOutput").ap() for k, s in OUTS.items()}
    build(nc, ins, outs)


def kernel(**inputs):
    import concourse.bacc as _bacc
    from concourse.bass_utils import run_bass_kernel_spmd as _run

    arrays = inputs_of(**inputs)
    nc = _bacc.Bacc("TRN2", target_bir_lowering=False, num_devices=1)
    launch(nc, arrays)
    r = _run(nc, [{f"in_{k}": a for k, a in arrays.items()}], core_ids=[0]).results[0]
    o = {k: r[f"out_{k}"] for k in OUTS}
    y = o["y"].transpose(2, 1, 0).reshape(NT, D)
    k = o["k"].transpose(2, 1, 0)
    ki = o["ki"].T
    v = o["v"].transpose(1, 0, 2).reshape(5 * P, KV, DH)
    ssm_p = o["ssm_p"].reshape(N_SSD, H_SSD, P_SSD).transpose(1, 2, 0)
    ssm_s = o["ssm_s"].reshape(N_SSD, NB, H_SSD, P_SSD).transpose(1, 2, 3, 0)
    conv = o["conv"].transpose(2, 1, 0).reshape(27, XBC * P)
    sc = o["sc_conv"].transpose(2, 1, 0).reshape(18, D)
    c = np.ascontiguousarray
    return (c(y[:SEQ].reshape(1, SEQ, D)), c(y[SEQ:].reshape(NB, NS, D)),
            c(k[:SEQ].reshape(1, 1, SEQ, KV, DH)), c(v[:SEQ].reshape(1, 1, SEQ, KV, DH)),
            c(ki[:SEQ].reshape(1, 1, SEQ, D_IDX)), c(ssm_p[None, None]), c(conv[:3][None, None]),
            c(sc[:2][None, None]), c(k[SEQ:].reshape(1, NB, NS, KV, DH)),
            c(v[SEQ:SEQ + NEW].reshape(1, NB, NS, KV, DH)), c(ki[SEQ:].reshape(1, NB, NS, D_IDX)),
            c(ssm_s[None]), c(conv[3:].reshape(1, NB, 3, XBC * P)), c(sc[2:].reshape(1, NB, 2, D)))
```

```python
from contextlib import ExitStack

import numpy as np

import concourse.bass as bass
from concourse import mybir

F32 = mybir.dt.float32
I32 = mybir.dt.int32
U32 = mybir.dt.uint32
ACT = mybir.ActivationFunctionType
ALU = mybir.AluOpType
AX = mybir.AxisListType.X

P = 128
D = 1024
DC = D // P
SEQ = 512
QT = SEQ // P
NB, NS = 8, 4
NEW = NB * NS
NT = SEQ + NEW
HALF = NT // 2
NSEQ = 1 + NB
PAGE = 128
PAGES = 8
PAST = PAGE * PAGES
POOL = 80
KEYS = PAST + NEW
H_ATT, DH, KV = 8, 128, 2
GRP = H_ATT // KV
H_IDX, D_IDX = 8, 64
TOPK_P, TOPK_S = min(256, SEQ // 4), min(256, (PAST + NS) // 4)
H_SSD, P_SSD, N_SSD, G_SSD = 16, 64, 128, 4
HPG = H_SSD // G_SSD
XBC = 16
K_SSD, K_SC = 4, 3
SEG_P, SEG_S = K_SSD - 1 + SEQ, K_SSD - 1 + NS
W_XB = SEG_P + NB * SEG_S
SSEG_P, SSEG_S = K_SC - 1 + SEQ, K_SC - 1 + NS
W_SC = SSEG_P + NB * SSEG_S
NE, FF = 32, 256
NG, EPG = 4, 8
EPS = 1e-6
NEG_ADD = -1e30
NOT_KEY = -1e38
CHOSEN = -3e38
REL = 384
REL_TOP = 255
RING = 8

T_ADA = 0
T_KI = 16
T_QI = T_KI + 1
T_SMALL = T_QI + 4
T_K = T_SMALL + 1
T_V = T_K + 2
T_Q = T_V + 2
T_Z = T_Q + 8
T_XBC = T_Z + 8
T_SC = T_XBC + 16
T_ADA2 = T_SC + 24
T_SHORT = T_ADA2 + 32
T_MERGE = T_SHORT + 16
T_O = T_MERGE + 32
T_END = T_O + 8

O_Z, O_XBC, O_DT, O_Q, O_K, O_V, O_QI, O_KI, O_WI, O_GB, O_GC, O_HV, O_GATE = (
    0, 1024, 3072, 3088, 4112, 4368, 4624, 5136, 5200, 5208, 6232, 7256, 8280)


def t5_bucket_of(dist):
    n = np.maximum(dist, 0)
    large = 16 + np.floor(np.log(np.maximum(n, 1) / 16.0) / np.log(8.0) * 16 + 1e-9).astype(np.int64)
    return np.where(n < 16, n, np.minimum(large, 31))


def shape_constants():
    i = np.arange(P)
    row_b, row_h, row_t = i // 32, (i // 4) % 8, i % 4
    new_b, new_t = np.arange(NEW) // NS, np.arange(NEW) % NS
    same = new_b[:, None] == new_b[None, :]
    parts = {}

    def put(name, a):
        full = np.zeros((P,) + a.shape[1:], np.float32)
        full[:a.shape[0]] = a
        parts[name] = full.reshape(P, -1)

    put("ident", np.eye(P))
    put("ones", np.ones((P, P)))
    put("upto", (i[:, None] <= i[None, :]))
    put("after", (i[:, None] > i[None, :]))
    put("future", np.where(i[None, :] > i[:, None], NOT_KEY, 0.0))
    put("future_add", np.where(i[None, :] > i[:, None], NEG_ADD, 0.0))
    put("upto_new", same & (new_t[:, None] <= new_t[None, :]))
    put("after_new", same & (new_t[:, None] > new_t[None, :]))
    put("new_keys", np.where(same & (new_t[None, :] <= new_t[:, None]), 0.0, NOT_KEY))
    put("head_rows", (np.arange(8)[:, None] == row_h[None, :]))
    sel = np.stack([((row_b[:, None] + 4 * a) == new_b[None, :]) & (row_t[:, None] == new_t[None, :])
                    for a in range(2)], 1)
    put("row_token", sel.reshape(P, -1))
    put("token_row", np.transpose(sel, (2, 1, 0)).reshape(NEW, -1))
    put("in_seq", (new_b[:, None] == np.arange(NB)[None, :]))
    dist = REL_TOP - np.arange(REL)
    onehot = (t5_bucket_of(dist)[None, :] == np.arange(32)[:, None]).astype(np.float32)
    onehot[31] -= 1.0
    put("rel_cols", onehot)
    put("iota8", np.broadcast_to(np.arange(8), (P, 8)))
    put("iota32", np.broadcast_to(np.arange(NE), (P, NE)))
    token = np.arange(5)[None, None, :] * P + i[:, None, None]
    put("row_values", 2 * token + np.arange(2)[None, :, None])
    return parts


CONST_AT = {}
_at = 0
for _name, _a in shape_constants().items():
    CONST_AT[_name] = (_at, _a.shape[1])
    _at += _a.shape[1]
CONST_W = _at

PARAM_AT = {}
_at = 0
for _name, _w in (("ada_b", 48), ("norm1", 8), ("norm2", 8), ("final", 8), ("conv_w", XBC * K_SSD),
                  ("conv_b", XBC), ("sc_w", 8 * K_SC), ("dt_bias", H_SSD), ("a_log", H_SSD), ("d_skip", 8),
                  ("ssm_norm", 8), ("rel_bias", H_ATT), ("c", DC * NSEQ), ("router", DC * 36),
                  ("conv_prev", XBC * NB * (K_SSD - 1)), ("sc_prev", 8 * NB * (K_SC - 1))):
    PARAM_AT[_name] = (_at, _w)
    _at += _w
PARAM_W = _at


class Link:

    def __init__(self, eng, sem):
        self.eng, self.sem, self.n = eng, sem, 0

    def __call__(self, ins):
        ins.then_inc(self.sem, 1)
        self.n += 1
        self.eng.wait_ge(self.sem, self.n)


class Arena:

    def __init__(self, tensor, size):
        self.t, self.size = tensor, size

    def at(self, start, *dims, parts=P, base=0):
        n = int(np.prod(dims))
        assert start + n <= self.size, (start, dims, self.size)
        v = self.t[base:base + parts, start:start + n]
        if len(dims) == 2:
            v = v.rearrange("p (a b) -> p a b", b=dims[1])
        if len(dims) == 3:
            v = v.rearrange("p (a b c) -> p a b c", b=dims[1], c=dims[2])
        return v


def build(nc, ins, outs):
    ctx = ExitStack()
    with ctx:
        in_use = []

        def sem(name):
            in_use.append(nc.alloc_semaphore(name=name))
            return in_use[-1]

        def retire(keep):
            nc.clear_and_free_semaphores([s for s in in_use if s not in keep])
            in_use[:] = list(keep)
            nc.all_engine_barrier()

        size = 53120
        A = Arena(ctx.enter_context(nc.sbuf_tensor("arena", [P, size], F32)), size)
        top = [0]

        def take(n):
            top[0] += n
            return top[0] - n

        a_const, a_param = take(CONST_W), take(PARAM_W)

        def const(name, parts=P):
            at, w = CONST_AT[name]
            return A.at(a_const + at, w, parts=parts)

        def param(name, parts=P):
            at, w = PARAM_AT[name]
            return A.at(a_param + at, w, parts=parts)

        mods = A.at(take(48 * NSEQ), 48, NSEQ)
        gain = A.at(take(2 * DC * NSEQ), 2, DC, NSEQ)
        c_silu = A.at(take(DC * NSEQ), DC, NSEQ)
        eps_col = A.at(take(2), 2)
        small = A.at(take(5 * 24), 5, 24)
        a_ring = take(RING * 1024)
        ring = A.at(a_ring, RING, DC * P)
        a_h = take(DC * NT)
        hT = A.at(a_h, DC, NT)
        a_x = take(DC * NT)
        xT = A.at(a_x, DC, NT)
        a_q = take(15 * NT)
        qT, kT, qiT, kiT = (A.at(a_q, 8, NT), A.at(a_q + 8 * NT, 2, NT), A.at(a_q + 10 * NT, 4, NT),
                            A.at(a_q + 14 * NT, NT))
        v_tok = A.at(take(5 * 256), 5, 256)
        a_z = take(8 * NT)
        zT = A.at(a_z, 8, NT)
        a_xb = take(XBC * W_XB)
        xb = A.at(a_xb, XBC, W_XB)
        kidx = A.at(a_xb, NB, PAST, parts=D_IDX)
        a_sc = take(256 + 384 + 512)
        score_at = [None, (a_sc, 256), (a_sc + 256, 384), (a_sc + 640, 512)]
        score_p = [None] + [A.at(*score_at[i]) for i in (1, 2, 3)]
        a_ss = take(KEYS)
        score_s = A.at(a_ss, KEYS, parts=NEW)
        best8 = A.at(take(32), 4, 8)
        a_tmp = top[0]
        assert size - a_tmp > 7300, (size - a_tmp)

        psum = ctx.enter_context(nc.psum_tensor("psum", [P, 8, 512], F32))
        pair = [psum[:, 2 * i:2 * i + 2, 0:HALF] for i in range(4)]

        def halves(ap):
            return ap.rearrange("p (h n) -> p h n", h=2)

        rel_dram = nc.dram_tensor("rel_dram", [H_ATT, P, REL + 1], F32).ap()

        short_dram = nc.dram_tensor("short_dram", [8, P, NT], F32).ap()

        def slid(q0, nq, k0, nk, h0=0, nh=H_ATT):
            return bass.AP(tensor=rel_dram.tensor, offset=rel_dram.offset + h0 * P * (REL + 1) + q0 * REL + P - 1 + k0,
                           ap=[[P * (REL + 1), nh], [REL, nq], [1, nk]])

        w_full = [sem(f"w_full{i}") for i in range(RING)]
        w_used = sem("w_used")


        def load_tile(sp, n):
            if n >= RING:
                sp.wait_ge(w_used, n - RING + 1)
            sp.dma_start(ring[:, n % RING, :], ins["weights"][n]).then_inc(w_full[n % RING], 16)

        def load_tiles(sp, a, b):
            b = min(b, T_END)
            while a < b and (a % RING or b - a < RING):
                load_tile(sp, a)
                a += 1
            if a < b:
                with sp.Fori(a // RING, b // RING) as r:
                    for s in range(RING):
                        if a > 0:
                            sp.wait_ge(w_used, r * RING + (s - RING + 1))
                        sp.dma_start(ring[:, s, :], ins["weights"][bass.ds(r * RING + s, 1)].rearrange(
                            "a p n -> (a p) n")).then_inc(w_full[s], 16)
                for n in range(b // RING * RING, b):
                    load_tile(sp, n)

        def tile_ready(pe, n):
            pe.wait_ge(w_full[n % RING], 16 * (n // RING + 1))

        def w_of(n, c, a=0, b=P):
            return ring[:, n % RING, c * P + a:c * P + b]

        def gain_of(dve, link, k, name):
            link(dve.tensor_scalar(gain[:, k], mods[:, 24 * k + 8:24 * k + 16, :], 1.0, None, ALU.add))
            link(dve.tensor_tensor(gain[:, k], gain[:, k],
                                   param(name).unsqueeze(2).to_broadcast([P, DC, NSEQ]), ALU.mult))

        def project(pe, n, out, act):
            for c in range(DC):
                for h in range(2):
                    mm = pe.matmul(out[:, h, :], lhsT=w_of(n, c), rhs=act[:, c, h * HALF:(h + 1) * HALF],
                                   start=(c == 0), stop=(c == DC - 1))
            return mm

        s_in, s_x, s_csilu, s_modps, s_gain = (sem(n) for n in (
            "in_loaded", "x_loaded", "c_silu_ready", "mods_in_psum", "gain_ready"))
        s_sq, s_ss, s_std, s_xn, s_h, s_hs, v_link1 = (sem(n) for n in (
            "squares_ready", "square_sums", "std_ready", "x_normed", "h_prompt", "h_sample", "dve_link1"))
        s_par = sem("params_loaded")
        s_eps, s_mrow1 = sem("eps_ready"), sem("modulation_rows1")
        mrow1 = A.at(a_tmp, T_KI * P, parts=NSEQ)
        s_out = sem("out_written")
        outs_written = [0]

        def write(eng, dst, src):
            eng.dma_start(dst, src).then_inc(s_out, 16)
            outs_written[0] += 16

        a_sq, a_rstd = a_q, a_q + DC * NT
        sqT, rstd = A.at(a_sq, DC, NT), A.at(a_rstd, NT)

        with nc.Block() as block:
            @block.sync
            def _(sp):
                sp.dma_start(A.at(a_param, PARAM_W), ins["params"]).then_inc(s_par, 16)
                for n in range(3):
                    load_tile(sp, n)
                sp.dma_start(A.at(a_const, CONST_W), ins["consts"]).then_inc(s_in, 16)
                sp.dma_start(xT, ins["x"]).then_inc(s_x, 16)
                for n in range(3, RING):
                    load_tile(sp, n)
                load_tiles(sp, RING, T_KI + RING)

            @block.scalar
            def _(act):
                act.wait_ge(s_par, 16)
                act.activation(c_silu, param("c").rearrange("p (c n) -> p c n", n=NSEQ),
                               ACT.Silu).then_inc(s_csilu, 1)
                act.wait_ge(s_x, 16)
                for c in range(DC):
                    act.activation(sqT[:, c, :], xT[:, c, :], ACT.Square).then_inc(s_sq, 1)
                act.wait_ge(s_ss, 1)
                act.wait_ge(s_eps, 1)
                act.activation(halves(rstd), pair[0], ACT.Sqrt, bias=eps_col[:, 0:1],
                               scale=1.0 / D).then_inc(s_std, 1)
                for g in range(4):
                    act.wait_ge(w_used, 4 * g + 4)
                    act.activation(mrow1[:, g * 512:g * 512 + 512], psum[0:NSEQ, 2 + g, :],
                                   ACT.Copy).then_inc(s_mrow1, 1)
                act.wait_ge(s_gain, 1)
                for c in range(DC):
                    act.wait_ge(s_xn, c + 1)
                    act.activation(hT[:, c, 0:SEQ], sqT[:, c, 0:SEQ], ACT.Identity,
                                   bias=mods[:, c, 0:1], scale=gain[:, 0, c, 0:1]).then_inc(s_h, 1)

            @block.tensor
            def _(pe):
                pe.wait_ge(s_csilu, 1)
                for n in range(T_KI):
                    if n == 8:
                        pe.wait_ge(s_in, 16)
                        for c in range(DC):
                            pe.wait_ge(s_sq, c + 1)
                            for h in range(2):
                                mm = pe.matmul(pair[0][:, h, :], lhsT=const("ones"),
                                               rhs=sqT[:, c, h * HALF:(h + 1) * HALF],
                                               start=(c == 0), stop=(c == DC - 1))
                        mm.then_inc(s_ss, 1)
                    tile_ready(pe, n)
                    for c in range(DC):
                        mm = pe.matmul(psum[0:NSEQ, 2 + n // 4, (n % 4) * P:(n % 4) * P + P],
                                       lhsT=c_silu[:, c, :], rhs=w_of(n, c), start=(c == 0), stop=(c == DC - 1))
                    mm.then_inc(w_used, 1)
                for n in range(T_KI):
                    pe.wait_ge(s_mrow1, n // 4 + 1)
                    mm = pe.transpose(psum[:, 7, n * NSEQ:(n + 1) * NSEQ], mrow1[:, n * P:n * P + P],
                                      const("ident", NSEQ)[:, 0:NSEQ])
                mm.then_inc(s_modps, 1)

            @block.vector
            def _(dve):
                link = Link(dve, v_link1)
                dve.memset(small[:, 4, :], 0.0)
                dve.memset(eps_col, EPS).then_inc(s_eps, 1)
                dve.wait_ge(s_std, 1)
                link(dve.reciprocal(rstd, rstd))
                for c in range(DC):
                    dve.tensor_tensor(sqT[:, c, :], xT[:, c, :], rstd, ALU.mult).then_inc(s_xn, 1)
                dve.wait_ge(s_modps, 1)
                link(dve.tensor_tensor(
                    mods[:, 0:T_KI, :], psum[:, 7, 0:T_KI * NSEQ].rearrange("p (m n) -> p m n", n=NSEQ),
                    param("ada_b")[:, 0:T_KI].unsqueeze(2).to_broadcast([P, T_KI, NSEQ]), ALU.add))
                gain_of(dve, link, 0, "norm1")
                dve.sem_inc(s_gain, 1)
                dve.wait_ge(s_xn, DC)
                for c in range(DC):
                    new = sqT[:, c, SEQ:NT].rearrange("p (b t) -> p b t", t=NS)
                    link(dve.tensor_tensor(new, new, gain[:, 0, c, 1:NSEQ].unsqueeze(2).to_broadcast(
                        [P, NB, NS]), ALU.mult))
                    dve.tensor_tensor(hT[:, c, SEQ:NT].rearrange("p (b t) -> p b t", t=NS), new,
                                      mods[:, c, 1:NSEQ].unsqueeze(2).to_broadcast([P, NB, NS]),
                                      ALU.add).then_inc(s_hs, 1)

        s_pt, s_kidx, s_ev2, s_relu, s_acc, s_pl, s_qs = (sem(n) for n in (
            "page_table_loaded", "kidx_loaded", "att_tile_out", "relu_ready", "relu_used", "index_logits",
            "qs_ready"))
        s_wisel, s_wi, s_sl, s_srelu, s_sscore, s_scopy = (sem(n) for n in (
            "wi_spread", "wi_ready", "new_index_logits", "new_relu_ready", "new_score_summed", "new_score_out"))
        v_link2 = sem("dve_link2")
        relu_scale = D_IDX ** -0.5 * H_IDX ** -0.5
        page_tab = ctx.enter_context(nc.sbuf_tensor("page_tab", [1, NB * PAGES], I32))
        rb = A.at(a_tmp, 2, 512)
        rs = A.at(a_tmp + 1024, 2, 512)
        qs = A.at(a_tmp + 2048, NB * 32, parts=D_IDX)
        wi_rows = A.at(a_tmp + 2304, 2, NEW)
        wiT = A.at(a_tmp + 2368, NEW, parts=H_IDX)
        IDX_UNITS = [(qt, h) for qt in range(1, QT) for h in range(H_IDX)]
        S_UNITS = [(kc, a) for kc in range(3) for a in range(2)]
        KC = [(0, 512), (512, 512), (1024, NEW)]

        with nc.Block() as block:
            @block.sync
            def _(sp):
                sp.dma_start(page_tab[:], ins["page_table"]).then_inc(s_pt, 16)
                load_tiles(sp, T_KI + RING, T_Q)
                sp.wait_ge(s_ev2, 1)
                write(sp, outs["ki"], kiT[0:D_IDX, :])
                load_tiles(sp, T_Q, T_Z + RING)
                sp.wait_ge(s_ev2, 8)
                write(sp, outs["k"], kT)
                sp.wait_ge(s_ev2, 11)
                write(sp, outs["v"][:, 0:4, :], v_tok[:, 0:4, :])
                write(sp, outs["v"][0:NEW, 4, :], v_tok[0:NEW, 4, :])

            @block.gpsimd
            def _(pool):
                pool.wait_ge(s_pt, 16)
                with pool.Fori(0, NB) as b:
                    of_seq = [pool.value_load(page_tab[0:1, bass.ds(b * PAGES + j, 1)], min_val=0,
                                            max_val=POOL - 1) for j in range(PAGES)]
                    for j in range(PAGES):
                        pool.dma_start(
                            kidx[:, bass.ds(b, 1), j * PAGE:(j + 1) * PAGE].rearrange("p a n -> p (a n)"),
                            ins["pages_i"][bass.ds(of_seq[j], 1)].rearrange("a p n -> (a p) n"),
                        ).then_inc(s_kidx, 16)

            @block.tensor
            def _(pe):
                unit = [0]

                def free_pair():
                    if unit[0] >= 2:
                        pe.wait_ge(s_ev2, unit[0] - 1)
                    unit[0] += 1
                    return pair[(unit[0] - 1) % 2], 2 * ((unit[0] - 1) % 2)

                def tile(n):
                    tile_ready(pe, n)
                    out, _ = free_pair()
                    project(pe, n, out, hT).then_inc(w_used, 1)

                tile(T_KI)
                for i in range(4):
                    tile(T_QI + i)
                tile_ready(pe, T_SMALL)
                _, bank = free_pair()
                for i in range(5):
                    m = P if i < 4 else NEW
                    for c in range(DC):
                        pe.matmul(psum[0:m, bank, 24 * i:24 * i + 24], lhsT=hT[:, c, P * i:P * i + m],
                                  rhs=w_of(T_SMALL, c, 0, 24), start=(c == 0), stop=(c == DC - 1))
                for c in range(DC):
                    mm = pe.matmul(psum[0:H_IDX, bank + 1, 0:NEW], lhsT=w_of(T_SMALL, c, 16, 24),
                                   rhs=hT[:, c, SEQ:NT], start=(c == 0), stop=(c == DC - 1))
                mm.then_inc(w_used, 1)
                tile(T_K)
                tile(T_K + 1)
                tile_ready(pe, T_V)
                tile_ready(pe, T_V + 1)
                for u in range(3):
                    _, bank = free_pair()
                    for i in range(2 * u, min(2 * u + 2, 5)):
                        m = P if i < 4 else NEW
                        for kv in range(KV):
                            for c in range(DC):
                                mm = pe.matmul(psum[0:m, bank + i % 2, kv * P:kv * P + P],
                                               lhsT=hT[:, c, P * i:P * i + m], rhs=w_of(T_V + kv, c),
                                               start=(c == 0), stop=(c == DC - 1))
                    if u < 2:
                        mm.then_inc(s_pl, 1)
                mm.then_inc(w_used, 2)
                pe.wait_ge(s_ev2, 7)
                pe.matmul(psum[:, 7, 0:NEW], lhsT=const("head_rows", H_IDX), rhs=wiT, start=True,
                          stop=True).then_inc(s_wisel, 1)

                def index_unit(k):
                    qt, h = IDX_UNITS[k]
                    lo, w = 64 * (h % 2), (qt + 1) * P
                    if k >= 4:
                        pe.wait_ge(s_relu, k - 3)
                    if k == 3:
                        pe.wait_ge(s_wi, 1)
                    pe.matmul(psum[:, 4 + k % 4, 0:w], lhsT=qiT[lo:lo + 64, h // 2, qt * P:qt * P + P],
                              rhs=kiT[lo:lo + 64, 0:w], start=True, stop=True).then_inc(s_pl, 1)

                for j in range(8):
                    tile(T_Q + j)
                    for k in range(3 * j, 3 * j + 3):
                        index_unit(k)

                def new_logits(s):
                    kc, a = S_UNITS[s]
                    at, w = KC[kc]
                    if s >= 2:
                        pe.wait_ge(s_srelu, s - 1)
                    if kc < 2:
                        for b4 in range(4):
                            b = 4 * a + b4
                            mm = pe.matmul(psum[32 * b4:32 * b4 + 32, 4 + s % 2, 0:w],
                                           lhsT=qs[:, 32 * b:32 * b + 32], rhs=kidx[:, b, at:at + w],
                                           start=True, stop=True)
                    else:
                        mm = pe.matmul(psum[:, 4 + s % 2, 0:w], lhsT=qs[:, P * a:P * a + P],
                                       rhs=kiT[0:D_IDX, SEQ:NT], start=True, stop=True)
                    mm.then_inc(s_sl, 1)

                def new_score(s):
                    kc, a = S_UNITS[s]
                    w = KC[kc][1]
                    pe.wait_ge(s_srelu, s + 1)
                    if s == 4:
                        pe.wait_ge(s_scopy, 1)
                    mm = pe.matmul(psum[0:NEW, 6 + kc % 2, 0:w], lhsT=wi_rows[:, a, :], rhs=rs[:, s % 2, 0:w],
                                   start=(a == 0), stop=(a == 1))
                    mm.then_inc(s_sscore, 1)

                pe.wait_ge(s_kidx, 16 * NB * PAGES)
                pe.wait_ge(s_qs, 2)
                pe.wait_ge(s_relu, len(IDX_UNITS))
                for s in range(6):
                    new_logits(s)
                    if s:
                        new_score(s - 1)
                new_score(5)

            @block.scalar
            def _(act):
                def out(src, dst):
                    return act.activation(dst, src, ACT.Copy)

                def tile(n, u, dst):
                    act.wait_ge(w_used, n + 1)
                    out(pair[u % 2], halves(dst)).then_inc(s_ev2, 1)

                tile(T_KI, 0, kiT)
                for i in range(4):
                    tile(T_QI + i, 1 + i, qiT[:, i, :])
                act.wait_ge(w_used, T_SMALL + 1)
                out(psum[:, 2, 0:96].rearrange("p (a b) -> p a b", b=24), small[:, 0:4, :])
                out(psum[0:NEW, 2, 96:120], small[0:NEW, 4, :])
                out(psum[0:H_IDX, 3, 0:NEW], wiT).then_inc(s_ev2, 1)
                tile(T_K, 6, kT[:, 0, :])
                tile(T_K + 1, 7, kT[:, 1, :])
                for u in range(3):
                    b = 2 * ((8 + u) % 2)
                    if u < 2:
                        act.wait_ge(s_pl, u + 1)
                        out(psum[:, b:b + 2, 0:256], v_tok[:, 2 * u:2 * u + 2, :]).then_inc(s_ev2, 1)
                    else:
                        act.wait_ge(w_used, T_V + 2)
                        out(psum[0:NEW, b, 0:256], v_tok[0:NEW, 4, :]).then_inc(s_ev2, 1)
                for j in range(8):
                    tile(T_Q + j, 11 + j, qT[:, j, :])
                    for k in range(3 * j, 3 * j + 3):
                        qt, h = IDX_UNITS[k]
                        w = (qt + 1) * P
                        act.wait_ge(s_pl, 2 + k + 1)
                        if k >= 2:
                            act.wait_ge(s_acc, 1 + k - 1)
                        act.activation(rb[:, k % 2, 0:w], psum[:, 4 + k % 4, 0:w], ACT.Relu,
                                       scale=relu_scale).then_inc(s_relu, 1)
                for s, (kc, a) in enumerate(S_UNITS):
                    w = KC[kc][1]
                    act.wait_ge(s_sl, s + 1)
                    if s >= 2:
                        act.wait_ge(s_sscore, s - 1)
                    act.activation(rs[:, s % 2, 0:w], psum[:, 4 + s % 2, 0:w], ACT.Relu,
                                   scale=relu_scale).then_inc(s_srelu, 1)

            @block.vector
            def _(dve):
                link = Link(dve, v_link2)
                dve.sem_inc(s_acc, 1)
                dve.wait_ge(s_ev2, 5)
                to = qs.rearrange("p (b j o t) -> p b j o t", j=4, o=2, t=NS)
                for odd in range(2):
                    src = qiT[64 * odd:64 * odd + 64, :, SEQ:NT].rearrange("p j (b t) -> p b j t", t=NS)
                    for b in range(NB):
                        last = dve.tensor_copy(to[:, b, :, odd, :], src[:, b])
                    last.then_inc(s_qs, 1)
                dve.wait_ge(s_wisel, 1)
                for a in range(2):
                    last = dve.tensor_tensor(
                        wi_rows[:, a, :], const("row_token").rearrange("p (a n) -> p a n", a=2)[:, a, :],
                        psum[:, 7, 0:NEW], ALU.mult)
                last.then_inc(s_wi, 1)
                for k, (qt, h) in enumerate(IDX_UNITS):
                    w = (qt + 1) * P
                    dve.wait_ge(s_relu, k + 1)
                    wcol = small[:, qt, 16 + h:17 + h]
                    if h == 0:
                        ins_ = dve.tensor_scalar(score_p[qt], rb[:, k % 2, 0:w], wcol, None, ALU.mult)
                    else:
                        ins_ = dve.scalar_tensor_tensor(score_p[qt], rb[:, k % 2, 0:w], wcol, score_p[qt],
                                                        ALU.mult, ALU.add)
                    ins_.then_inc(s_acc, 1)
                    dve.wait_ge(s_acc, 1 + k + 1)
                    if h == H_IDX - 1:
                        dg = score_p[qt][:, qt * P:(qt + 1) * P]
                        link(dve.tensor_tensor(dg, dg, const("future"), ALU.add))
                for kc in range(3):
                    at, w = KC[kc]
                    dve.wait_ge(s_sscore, 2 * kc + 2)
                    src = psum[0:NEW, 6 + kc % 2, 0:w]
                    if kc < 2:
                        dve.tensor_copy(score_s[:, at:at + w], src).then_inc(s_scopy, 1)
                    else:
                        dve.tensor_tensor(score_s[:, at:at + w], src, const("new_keys", NEW),
                                          ALU.add).then_inc(s_scopy, 1)

        s_ev3, s_fill, s_conv, s_silu, s_state, s_cgst, s_scd, s_top = (sem(n) for n in (
            "tile_out3", "conv_fill", "conv_ready", "silu_done", "conv_state_saved", "sc_state_saved",
            "sc_done", "top_step"))
        v_link3 = sem("dve_link3")
        yc = A.at(a_x, 8, NT)
        tsc = A.at(a_tmp, 2, 3, NT)
        cg = A.at(a_tmp + 3264, 2, W_SC)
        u_sc = A.at(a_tmp + 3264 + 2 * W_SC, W_SC - 2)
        a_ca = a_tmp + 3264 + 3 * W_SC
        cacc = A.at(a_ca, 2, W_XB - 3)
        conv_state = A.at(a_ca + 2 * (W_XB - 3), XBC, 27)
        sc_state = A.at(a_ca + 2 * (W_XB - 3) + XBC * 27, 8, 18)
        LX = W_XB - 3
        LS = W_SC - 2

        def seq_new(row, start, seg, lo, hi):
            return row[:, start:start + NB * seg].rearrange("p (b s) -> p b s", s=seg)[:, :, lo:hi]

        with nc.Block() as block:
            @block.sync
            def _(sp):
                load_tiles(sp, T_Z + RING, T_ADA2 + RING)
                sp.wait_ge(s_state, XBC)
                write(sp, outs["conv"], conv_state)
                sp.wait_ge(s_cgst, 8)
                write(sp, outs["sc_conv"], sc_state)

            @block.gpsimd
            def _(pool):
                for m in range(XBC):
                    pool.memset(xb[:, m, 0:3], 0.0)
                    last = pool.tensor_copy(
                        seq_new(xb[:, m, :], SEG_P, SEG_S, 0, 3),
                        param("conv_prev").rearrange("p (m b k) -> p m b k", b=NB, k=3)[:, m])
                last.then_inc(s_fill, 1)
                for i in range(2):
                    last = pool.memset(cg[:, i, 0:2], 0.0)
                last.then_inc(s_fill, 1)
                for m in range(XBC):
                    pool.wait_ge(s_ev3, 8 + m + 1)
                    pool.tensor_copy(conv_state[:, m, 0:3], xb[:, m, SEQ:SEQ + 3])
                    pool.tensor_copy(conv_state[:, m, 3:27].rearrange("p (b k) -> p b k", k=3),
                                     seq_new(xb[:, m, :], SEG_P, SEG_S, 4, 7)).then_inc(s_state, 1)

            @block.tensor
            def _(pe):
                for u in range(48):
                    tile_ready(pe, T_Z + u)
                    if u >= 4:
                        pe.wait_ge(s_ev3, u - 3)
                    project(pe, T_Z + u, pair[u % 4], hT).then_inc(w_used, 1)

            @block.scalar
            def _(act):
                for u in range(8):
                    act.wait_ge(w_used, T_Z + u + 1)
                    act.activation(halves(zT[:, u, :]), pair[u % 4], ACT.Copy).then_inc(s_ev3, 1)
                rest = SEQ - HALF
                for u in range(8, 24):
                    m, src = u - 8, pair[u % 4]
                    act.wait_ge(w_used, T_Z + u + 1)
                    act.activation(xb[:, m, 3:3 + HALF], src[:, 0, :], ACT.Copy)
                    act.activation(xb[:, m, 3 + HALF:3 + SEQ], src[:, 1, 0:rest], ACT.Copy)
                    act.activation(seq_new(xb[:, m, :], SEG_P, SEG_S, 3, 7),
                                   src[:, 1, rest:HALF].rearrange("p (b t) -> p b t", t=NS),
                                   ACT.Copy).then_inc(s_ev3, 1)
                for m in range(8):
                    for i in range(3):
                        u = 24 + 3 * m + i
                        act.wait_ge(w_used, T_Z + u + 1)
                        if m >= 2:
                            act.wait_ge(s_scd, m - 1)
                        act.activation(halves(tsc[:, m % 2, i, :]), pair[u % 4], ACT.Copy).then_inc(s_ev3, 1)
                    for j in (2 * m, 2 * m + 1):
                        act.wait_ge(s_conv, j + 1)
                        act.wait_ge(s_state, j + 1)
                        act.activation(xb[:, j, 0:LX], cacc[:, j % 2, :], ACT.Silu).then_inc(s_silu, 1)

            @block.vector
            def _(dve):
                link = Link(dve, v_link3)
                rows = [(score_p[1], TOPK_P), (score_p[2], TOPK_P), (score_p[3], TOPK_P), (score_s, TOPK_S)]
                steps = 0
                for r in range(TOPK_S // 8):
                    live = [(i, s) for i, (s, k) in enumerate(rows) if r < k // 8]
                    for i, s in live:
                        dve.max(best8[0:s.shape[0], i, :], s).then_inc(s_top, 1)
                    for n, (i, s) in enumerate(live):
                        dve.wait_ge(s_top, steps + n + 1)
                        dve.match_replace(s, best8[0:s.shape[0], i, :], s, CHOSEN).then_inc(s_top, 1)
                    steps += 2 * len(live)
                    dve.wait_ge(s_top, steps)
                for s, _ in rows:
                    link(dve.tensor_scalar(s, s, CHOSEN * 0.7, NEG_ADD, ALU.is_gt, ALU.mult))

                def conv(m):
                    if m == 0:
                        dve.wait_ge(s_fill, 2)
                    dve.wait_ge(s_ev3, 8 + m + 1)
                    if m >= 2:
                        dve.wait_ge(s_silu, m - 1)
                    w = param("conv_w").rearrange("p (m k) -> p m k", k=K_SSD)[:, m, :]
                    acc = cacc[:, m % 2, :]
                    link(dve.tensor_scalar(acc, xb[:, m, 0:LX], w[:, 0:1], param("conv_b")[:, m:m + 1],
                                           ALU.mult, ALU.add))
                    for k in range(1, K_SSD):
                        last = dve.scalar_tensor_tensor(acc, xb[:, m, k:k + LX], w[:, k:k + 1], acc,
                                                        ALU.mult, ALU.add)
                        if k < K_SSD - 1:
                            link(last)
                    last.then_inc(s_conv, 1)

                def short(m):
                    row = cg[:, m % 2, :]
                    c_, h_, b_ = (tsc[:, m % 2, i, :] for i in range(3))
                    by_seq = lambda a: a[:, SEQ:NT].rearrange("p (b t) -> p b t", t=NS)
                    dve.wait_ge(s_ev3, 24 + 3 * m + 3)
                    dve.tensor_tensor(row[:, 2:2 + SEQ], c_[:, 0:SEQ], h_[:, 0:SEQ], ALU.mult)
                    dve.tensor_copy(seq_new(row, SSEG_P, SSEG_S, 0, 2),
                                    param("sc_prev").rearrange("p (m b k) -> p m b k", b=NB, k=2)[:, m])
                    link(dve.tensor_tensor(seq_new(row, SSEG_P, SSEG_S, 2, 6), by_seq(c_), by_seq(h_),
                                           ALU.mult))
                    dve.tensor_copy(sc_state[:, m, 0:2], row[:, SEQ:SEQ + 2])
                    dve.tensor_copy(sc_state[:, m, 2:18].rearrange("p (b k) -> p b k", k=2),
                                    seq_new(row, SSEG_P, SSEG_S, 4, 6)).then_inc(s_cgst, 1)
                    w = param("sc_w").rearrange("p (m k) -> p m k", k=K_SC)[:, m, :]
                    link(dve.tensor_scalar(u_sc, row[:, 0:LS], w[:, 0:1], None, ALU.mult))
                    for k in range(1, K_SC):
                        link(dve.scalar_tensor_tensor(u_sc, row[:, k:k + LS], w[:, k:k + 1], u_sc,
                                                      ALU.mult, ALU.add))
                    dve.tensor_tensor(yc[:, m, 0:SEQ], u_sc[:, 0:SEQ], b_[:, 0:SEQ], ALU.mult)
                    for b in range(NB):
                        at = SSEG_P + b * SSEG_S
                        last = dve.tensor_tensor(yc[:, m, SEQ + b * NS:SEQ + b * NS + NS],
                                                 u_sc[:, at:at + NS],
                                                 b_[:, SEQ + b * NS:SEQ + b * NS + NS], ALU.mult)
                    link(last)
                    dve.sem_inc(s_scd, 1)

                for m in range(8):
                    conv(2 * m)
                    conv(2 * m + 1)
                    short(m)

        (s_rel, s_relout, s_reld, s_near, s_qk, s_lg, s_max, s_exp, s_prob, s_pt4, s_ptout, s_pv,
         s_o) = (sem(n) for n in (
            "rel_in_psum", "rel_in_sbuf", "rel_in_dram", "near_loaded", "qk_ready", "logits_read", "max_ready",
            "exp_ready", "probs_ready", "probs_turned", "turned_out", "pv_ready", "att_out"))
        v_link4 = sem("dve_link4")
        near = A.at(a_tmp, H_ATT, 2 * P)
        sp4 = A.at(a_tmp + 2048, 3, 512)
        pt4 = A.at(a_tmp + 2048 + 1536, 2, 512)
        a_st = a_tmp + 2048 + 1536 + 1024
        nmax, esum = A.at(a_st, 32), A.at(a_st + 32, 32)
        rel_sb = A.at(a_st + 64, REL, parts=H_ATT)
        s_mrow, s_mturn = sem("modulation_rows"), sem("modulation_turned")
        mrow = A.at(a_st + 64 + REL, 2, 512, parts=NSEQ)
        A_UNITS = [(qt, h) for qt in range(QT) for h in range(H_ATT)]
        NU = len(A_UNITS)

        with nc.Block() as block:
            @block.sync
            def _(sp):
                sp.wait_ge(s_relout, 1)
                sp.dma_start(rel_dram[:, :, 0:REL], rel_sb.unsqueeze(1).to_broadcast([H_ATT, P, REL])).then_inc(
                    s_reld, 16)
                sp.wait_ge(s_reld, 16)
                sp.dma_start(near, slid(0, P, 0, 2 * P).rearrange("h q k -> q h k")).then_inc(s_near, 16)
                load_tiles(sp, T_ADA2 + RING, T_SHORT + RING)

            @block.tensor
            def _(pe):
                pe.matmul(psum[0:H_ATT, 7, 0:REL], lhsT=param("rel_bias", 32), rhs=const("rel_cols", 32),
                          start=True, stop=True).then_inc(s_rel, 1)

                def qk(k):
                    qt, h = A_UNITS[k]
                    if k >= 2:
                        pe.wait_ge(s_lg, k - 1)
                    pe.matmul(psum[:, k % 2, 0:(qt + 1) * P], lhsT=qT[:, h, qt * P:qt * P + P],
                              rhs=kT[:, h // GRP, 0:(qt + 1) * P], start=True, stop=True).then_inc(s_qk, 1)

                def turn(k):
                    qt, h = A_UNITS[k]
                    pe.wait_ge(s_prob, k + 1)
                    if k >= 2:
                        pe.wait_ge(s_ptout, k - 1)
                    for j in range(qt + 1):
                        mm = pe.transpose(psum[:, 2 + k % 2, j * P:j * P + P], sp4[:, k % 3, j * P:j * P + P],
                                          const("ident"))
                    mm.then_inc(s_pt4, 1)

                def pv(k):
                    qt, h = A_UNITS[k]
                    kv = h // GRP
                    pe.wait_ge(s_ptout, k + 1)
                    if k >= 2:
                        pe.wait_ge(s_o, k - 1)
                    for j in range(qt + 1):
                        mm = pe.matmul(psum[:, 4 + k % 2, 0:P], lhsT=v_tok[:, j, kv * DH:kv * DH + DH],
                                       rhs=pt4[:, k % 2, j * P:j * P + P], start=(j == 0), stop=(j == qt))
                    mm.then_inc(s_pv, 1)

                def modulation(k):
                    tile_ready(pe, T_ADA2 + k)
                    if k >= 4 and k % 4 == 0:
                        pe.wait_ge(s_mrow, k // 4)
                    for c in range(DC):
                        mm = pe.matmul(psum[0:NSEQ, 6, (k % 4) * P:(k % 4) * P + P], lhsT=c_silu[:, c, :],
                                       rhs=w_of(T_ADA2 + k, c), start=(c == 0), stop=(c == DC - 1))
                    mm.then_inc(w_used, 1)

                def modulation_turn(g):
                    pe.wait_ge(s_mrow, g + 1)
                    for q in range(4):
                        at = (4 * g + q) * NSEQ
                        mm = pe.transpose(psum[:, 7, at:at + NSEQ], mrow[:, g % 2, q * P:q * P + P],
                                          const("ident", NSEQ)[:, 0:NSEQ])
                    mm.then_inc(s_mturn, 1)

                for k in range(NU + 2):
                    if k < NU:
                        qk(k)
                        modulation(k)
                    if k % 4 == 1 and k > 4:
                        modulation_turn(k // 4 - 1)
                    if 1 <= k <= NU:
                        turn(k - 1)
                    if k >= 2:
                        pv(k - 2)

            @block.scalar
            def _(act):
                act.wait_ge(s_rel, 1)
                act.activation(rel_sb, psum[0:H_ATT, 7, 0:REL], ACT.Copy).then_inc(s_relout, 1)
                for k in range(NU + 2):
                    if k < NU:
                        w = (A_UNITS[k][0] + 1) * P
                        act.wait_ge(s_max, k + 1)
                        act.activation(sp4[:, k % 3, 0:w], sp4[:, k % 3, 0:w], ACT.Exp, bias=nmax[:, k:k + 1],
                                       accum_out=esum[:, k:k + 1]).then_inc(s_exp, 1)
                    if 1 <= k <= NU:
                        w = (A_UNITS[k - 1][0] + 1) * P
                        act.wait_ge(s_pt4, k)
                        if k >= 3:
                            act.wait_ge(s_pv, k - 2)
                        act.activation(pt4[:, (k - 1) % 2, 0:w], psum[:, 2 + (k - 1) % 2, 0:w],
                                       ACT.Copy).then_inc(s_ptout, 1)
                    if k >= 2:
                        qt, h = A_UNITS[k - 2]
                        act.wait_ge(s_pv, k - 1)
                        act.activation(qT[:, h, qt * P:qt * P + P], psum[:, 4 + k % 2, 0:P],
                                       ACT.Copy).then_inc(s_o, 1)
                    if k % 4 == 3:
                        g = k // 4
                        act.wait_ge(w_used, T_ADA2 + k + 1)
                        if g >= 2:
                            act.wait_ge(s_mturn, g - 1)
                        act.activation(mrow[:, g % 2, :], psum[0:NSEQ, 6, :], ACT.Copy).then_inc(s_mrow, 1)

            @block.vector
            def _(dve):
                link = Link(dve, v_link4)
                dve.wait_ge(s_near, 16)
                for k in range(NU + 1):
                    if k < NU:
                        qt, h = A_UNITS[k]
                        w = (qt + 1) * P
                        s = sp4[:, k % 3, 0:w]
                        mask = score_p[qt] if qt else const("future_add")
                        dve.wait_ge(s_qk, k + 1)
                        if k >= 3:
                            dve.wait_ge(s_pt4, k - 2)
                        dve.scalar_tensor_tensor(s, psum[:, k % 2, 0:w], DH ** -0.5, mask, ALU.mult,
                                                 ALU.add).then_inc(s_lg, 1)
                        dve.wait_ge(s_lg, k + 1)
                        last, nb = (s[:, w - 256:w], near[:, h, :]) if qt else (s, near[:, h, P:2 * P])
                        link(dve.tensor_tensor(last, last, nb, ALU.add))
                        dve.tensor_reduce(nmax[:, k:k + 1], s, AX, ALU.max, negate=True).then_inc(s_max, 1)
                    if k >= 1:
                        w = (A_UNITS[k - 1][0] + 1) * P
                        s = sp4[:, (k - 1) % 3, 0:w]
                        dve.wait_ge(s_exp, k)
                        link(dve.reciprocal(esum[:, k - 1:k], esum[:, k - 1:k]))
                        dve.tensor_scalar(s, s, esum[:, k - 1:k], None, ALU.mult).then_inc(s_prob, 1)
                dve.wait_ge(s_mturn, 8)
                link(dve.tensor_tensor(
                    mods[:, T_KI:48, :], psum[:, 7, 0:32 * NSEQ].rearrange("p (m n) -> p m n", n=NSEQ),
                    param("ada_b")[:, T_KI:48].unsqueeze(2).to_broadcast([P, 32, NSEQ]), ALU.add))
                gain_of(dve, link, 1, "norm2")

        s_kvused, s_qz, s_sl5, s_smax, s_sexp, s_sprob, s_st, s_stout, s_so, s_qz0, s_nearl = (sem(n) for n in (
            "pages_used", "q_spread", "slogits_read", "smax_ready", "sexp_ready", "sprobs_ready",
            "sprobs_turned", "sturned_out", "satt_out", "q_zeroed", "snear_loaded"))
        s_kvs = [sem(f"pages_loaded{i}") for i in range(2)]
        v_link5 = sem("dve_link5")
        pages = A.at(a_tmp, 2, PAGES * 256)
        ss5 = A.at(a_tmp + 4096, KEYS)
        pts = A.at(a_tmp + 4096 + KEYS, PAGES, P)
        ptn = A.at(a_tmp + 4096 + KEYS + 1024, P, parts=NEW)
        snear = A.at(a_tmp + 4096 + KEYS + 1152, P + NS)
        st5 = A.at(a_tmp + 4096 + KEYS + 1152 + P + NS, 4)
        qz = A.at(a_sc, NB, KV, 32)
        s_shps, s_shsig, s_short = sem("short_in_psum"), sem("short_gate"), sem("short_gated")
        s_shout = [sem(f"short_written{i}") for i in range(2)]
        sg5 = A.at(a_q + 10 * NT, 2, HALF)
        short5 = A.at(a_q + 11 * NT, 2, NT)

        def pages_in(eng, k):
            for u in range(0, 16, 4):
                src = ins["pages_k" if u % 8 < 4 else "pages_v"]
                with eng.Fori(0, 2) as q:
                    first = (q * 2 + (4 * (u // 8) + k)) * PAGES
                    of_seq = [eng.value_load(page_tab[0:1, bass.ds(first + j, 1)], min_val=0, max_val=POOL - 1)
                              for j in range(PAGES)]
                    eng.wait_ge(s_kvused, q * 2 + (u + k + 1))
                    for j in range(PAGES):
                        eng.dma_start(pages[:, k, j * 256:j * 256 + 256],
                                      src[bass.ds(of_seq[j], 1)].rearrange("a p n -> (a p) n")).then_inc(s_kvs[k], 16)

        with nc.Block() as block:
            @block.sync
            def _(sp):
                for g in range(4):
                    sp.dma_start(snear[32 * g:32 * g + 32, :], slid(0, NS, 0, P + NS)).then_inc(s_nearl, 16)
                pages_in(sp, 0)

            @block.gpsimd
            def _(pool):
                pool.memset(qz, 0.0).then_inc(s_qz0, 1)
                pages_in(pool, 1)

            @block.tensor
            def _(pe):
                pe.sem_inc(s_kvused, 2)
                pe.wait_ge(s_qz, NB)

                def short_half(j):
                    m, h = j // 2, j % 2
                    if j:
                        pe.wait_ge(s_short, j)
                    for k, (bank, act_of) in enumerate(((5, yc), (7, hT))):
                        n = T_SHORT + 2 * m + k
                        tile_ready(pe, n)
                        for c in range(DC):
                            mm = pe.matmul(psum[:, bank, 0:HALF], lhsT=w_of(n, c),
                                           rhs=act_of[:, c, h * HALF:(h + 1) * HALF],
                                           start=(c == 0), stop=(c == DC - 1))
                        mm.then_inc(w_used if h else s_shps, 1)

                for a in range(2):
                    if a:
                        pe.wait_ge(s_sl5, 1)
                    for kc in range(3):
                        at, w = KC[kc]
                        pe.matmul(psum[:, kc, 0:w],
                                  lhsT=const("token_row", NEW).rearrange("p (a n) -> p a n", a=2)[:, a, :],
                                  rhs=score_s[:, at:at + w], start=True, stop=False)
                    for b4 in range(4):
                        u, b = 8 * a + b4, 4 * a + b4
                        short_half(u)
                        pe.wait_ge(s_kvs[u % 2], 16 * PAGES * (u // 2 + 1))
                        page = pages[:, u % 2, :].rearrange("p (j v n) -> p j v n", v=KV, n=PAGE)
                        for kc in range(3):
                            w = KC[kc][1]
                            for kv in range(KV):
                                rhs = page[:, 4 * kc:4 * kc + 4, kv, :] if kc < 2 else kT[:, kv, SEQ:NT]
                                out = psum[32 * b4:32 * b4 + 32, kc, 0:w]
                                if kc < 2:
                                    out = out.rearrange("p (j n) -> p j n", n=PAGE)
                                mm = pe.matmul(out, lhsT=qz[:, b, kv, :], rhs=rhs, start=False, stop=(kv == 1))
                        mm.then_inc(s_kvused, 1)
                    short_half(8 * a + 4)
                    pe.wait_ge(s_sprob, a + 1)
                    if a:
                        pe.wait_ge(s_so, 1)
                    for j in range(PAGES):
                        pe.transpose(psum[:, 3 + j // 4, (j % 4) * P:(j % 4) * P + P],
                                     ss5[:, j * P:j * P + P], const("ident"))
                    pe.transpose(psum[0:NEW, 6, P:2 * P], ss5[:, PAST:KEYS], const("ident")).then_inc(s_st, 1)
                    short_half(8 * a + 5)
                    pe.wait_ge(s_stout, a + 1)
                    for b4 in range(4):
                        u = 8 * a + 4 + b4
                        if b4 in (1, 2):
                            short_half(8 * a + 5 + b4)
                        pe.wait_ge(s_kvs[u % 2], 16 * PAGES * (u // 2 + 1))
                        for kv in range(KV):
                            col = 32 * b4 + 16 * kv
                            out = psum[:, 6, col:col + 16]
                            for j in range(PAGES):
                                at = j * 256 + kv * DH
                                pe.matmul(out, lhsT=pages[:, u % 2, at:at + DH], rhs=pts[:, j, col:col + 16],
                                          start=(j == 0), stop=False)
                            mm = pe.matmul(out, lhsT=v_tok[0:NEW, 4, kv * DH:kv * DH + DH],
                                           rhs=ptn[:, col:col + 16], start=False, stop=True)
                        mm.then_inc(s_kvused, 1)

            @block.scalar
            def _(act):
                act.wait_ge(s_qz0, 1)
                for b in range(NB):
                    for kv in range(KV):
                        last = act.activation(
                            qz[:, b, kv, 16 * kv:16 * kv + 16].rearrange("p (g t) -> p g t", t=NS),
                            qT[:, GRP * kv:GRP * kv + GRP, SEQ + NS * b:SEQ + NS * b + NS], ACT.Copy,
                            scale=DH ** -0.5)
                    last.then_inc(s_qz, 1)

                def sigmoid(j):
                    m = j // 2
                    if j % 2:
                        act.wait_ge(w_used, T_SHORT + j + 1)
                    else:
                        act.wait_ge(s_shps, j + 2)
                    if j >= 2:
                        act.wait_ge(s_short, j - 1)
                    act.activation(sg5[:, j % 2, :], psum[:, 7, 0:HALF], ACT.Sigmoid).then_inc(s_shsig, 1)
                    if j % 2:
                        load_tile(act, T_SHORT + RING + j - 1)
                        load_tile(act, T_SHORT + RING + j)
                    elif j:
                        write_short(m - 1)

                def write_short(m):
                    act.wait_ge(s_short, 2 * m + 2)
                    act.dma_start(short_dram[m], short5[:, m % 2, :]).then_inc(s_shout[m % 2], 16)

                for a in range(2):
                    for j in range(8 * a, 8 * a + 4):
                        sigmoid(j)
                    act.wait_ge(s_smax, a + 1)
                    act.activation(ss5, ss5, ACT.Exp, bias=st5[:, 2 * a:2 * a + 1],
                                   accum_out=st5[:, 2 * a + 1:2 * a + 2]).then_inc(s_sexp, 1)
                    sigmoid(8 * a + 4)
                    act.wait_ge(s_st, a + 1)
                    act.activation(pts[:, 0:4, :], psum[:, 3, :].rearrange("p (j n) -> p j n", n=P), ACT.Copy)
                    act.activation(pts[:, 4:8, :], psum[:, 4, :].rearrange("p (j n) -> p j n", n=P), ACT.Copy)
                    act.activation(ptn, psum[0:NEW, 6, P:2 * P], ACT.Copy).then_inc(s_stout, 1)
                    for j in range(8 * a + 5, 8 * a + 8):
                        sigmoid(j)
                    act.wait_ge(s_kvused, 2 + 8 * a + 8)
                    for b4 in range(4):
                        at = SEQ + NS * (4 * a + b4)
                        last = act.activation(
                            qT[:, :, at:at + NS],
                            psum[:, 6, 32 * b4:32 * b4 + 32].rearrange("p (h t) -> p h t", t=NS), ACT.Copy)
                    last.then_inc(s_so, 1)
                write_short(7)
                for k in range(2):
                    act.wait_ge(s_shout[k], 16 * 4)

            @block.vector
            def _(dve):
                link = Link(dve, v_link5)
                dve.wait_ge(s_nearl, 16 * 4)

                def gated(j):
                    m, h = j // 2, j % 2
                    dve.wait_ge(s_shsig, j + 1)
                    if h == 0 and m >= 2:
                        dve.wait_ge(s_shout[m % 2], 16 * (m // 2))
                    dve.tensor_tensor(short5[:, m % 2, h * HALF:(h + 1) * HALF], sg5[:, h, :],
                                      psum[:, 5, 0:HALF], ALU.mult).then_inc(s_short, 1)

                for a in range(2):
                    for j in range(8 * a, 8 * a + 4):
                        gated(j)
                    dve.wait_ge(s_kvused, 2 + 8 * a + 4)
                    if a:
                        dve.wait_ge(s_st, a)
                    flat = psum[:, 0:3, :].rearrange("p a b -> p (a b)")
                    far = PAST - P
                    dve.tensor_copy(ss5[:, 0:far], flat[:, 0:far])
                    dve.tensor_tensor(ss5[:, far:PAST], flat[:, far:PAST], snear[:, 0:P], ALU.add)
                    link(dve.tensor_tensor(
                        ss5[:, PAST:KEYS].rearrange("p (b t) -> p b t", t=NS),
                        flat[:, PAST:KEYS].rearrange("p (b t) -> p b t", t=NS),
                        snear[:, P:P + NS].unsqueeze(1).to_broadcast([P, NB, NS]), ALU.add))
                    dve.sem_inc(s_sl5, 1)
                    dve.tensor_reduce(st5[:, 2 * a:2 * a + 1], ss5, AX, ALU.max, negate=True).then_inc(s_smax, 1)
                    dve.wait_ge(s_sexp, a + 1)
                    link(dve.reciprocal(st5[:, 2 * a + 1:2 * a + 2], st5[:, 2 * a + 1:2 * a + 2]))
                    dve.tensor_scalar(ss5, ss5, st5[:, 2 * a + 1:2 * a + 2], None, ALU.mult).then_inc(s_sprob, 1)
                    for j in range(8 * a + 4, 8 * a + 8):
                        gated(j)

        retire([*w_full, w_used, s_out])

        (s_st6, s_v6, s_e6, s_dt, s_small6, s_csout, s_t6, s_xdt, s_btok, s_csb, s_pre, s_e, s_mid, s_ys,
         s_post) = (sem(n) for n in (
            "states_loaded", "softplus_in", "softplus_parts", "dt_ready", "cumsum_in_psum", "cumsum_ready",
            "chunk_turned", "xdt_ready", "btok_ready", "decays_in_psum", "decay_args", "decays_ready",
            "mix_ready", "y_in_psum", "y_out"))
        v_link6, a_link6 = sem("dve_link6"), sem("act_link6")
        s_t6b, s_early, s_earlyout = sem("b_turned"), sem("early_in_psum"), sem("early_out")
        EARLY = 4
        early = A.at(a_x, 2 * EARLY, NT)
        states = A.at(a_sc, NB, D)
        a_s6 = a_q + 8 * NT
        stT = A.at(a_s6, D)
        xdt = A.at(a_s6 + 1024, D)
        xdtd = A.at(a_s6 + 2048, D)
        btok = A.at(a_s6 + 3072, 512)
        ebuf = A.at(a_s6 + 3584, 2, 512)
        a_s6b = a_sc + NB * D
        chb = A.at(a_s6b, 512)
        cbm = A.at(a_s6b + 512, P)
        cbm2 = A.at(a_s6b + 640, P)
        ecl = A.at(a_s6b + 768, 2, HPG)
        dt5 = A.at(a_s6b + 776, 5, H_SSD)
        adt = A.at(a_s6b + 856, 5, H_SSD)
        cs5 = A.at(a_s6b + 936, 5, H_SSD)
        dte = A.at(a_s6b + 1016, 5, H_SSD)
        a_neg = A.at(a_s6b + 1096, H_SSD)
        sp_e = A.at(a_s6b + 1112, 5, H_SSD)
        C_UNITS = [(i, g) for i in range(QT) for g in range(G_SSD)]
        NCU = len(C_UNITS)

        with nc.Block() as block:
            @block.sync
            def _(sp):
                sp.dma_start(states, ins["state"].rearrange("n (b d) -> n b d", b=NB)).then_inc(s_st6, 16)
                load_tiles(sp, T_MERGE + RING, T_MERGE + 2 * RING)
                sp.wait_ge(s_post, NCU)
                write(sp, outs["ssm_p"], stT)
                sp.wait_ge(s_out, outs_written[0])

            @block.scalar
            def _(act):
                act.wait_ge(s_v6, 1)
                act.activation(sp_e, sp_e, ACT.Exp).then_inc(a_link6, 1)
                act.activation(a_neg, param("a_log"), ACT.Exp)
                act.wait_ge(a_link6, 1)
                act.activation(sp_e, sp_e, ACT.Ln, bias=1.0).then_inc(s_e6, 1)
                act.wait_ge(s_small6, 1)
                for lo, m, k in ((0, P, 4), (4, NEW, 1)):
                    for to, at, func in ((cs5, 0, ACT.Copy), (dte, 80, ACT.Exp)):
                        at += lo * H_SSD
                        last = act.activation(
                            to[0:m, lo:lo + k, :],
                            psum[0:m, 3, at:at + k * H_SSD].rearrange("p (a b) -> p a b", b=H_SSD), func)
                last.then_inc(s_csout, 1)
                for k, (i, g) in enumerate(C_UNITS):
                    if g == 0:
                        act.wait_ge(s_t6b, i + 1)
                        if i:
                            act.wait_ge(s_ys, k)
                        act.activation(btok, psum[:, 0, :], ACT.Copy).then_inc(s_btok, 1)
                    act.wait_ge(s_csb, k + 1)
                    if k >= 1:
                        act.wait_ge(s_ys, k)
                        act.wait_ge(s_post, k)
                    act.wait_ge(s_pre, k + 1)
                    act.activation(chb, psum[:, 4 + k % 2, :], ACT.Exp)
                    act.activation(ebuf[:, k % 2, :], ebuf[:, k % 2, :], ACT.Exp).then_inc(s_e, 1)
                    act.wait_ge(s_early, k + 1)
                    act.activation(early[:, k // 2, (k % 2) * HALF:(k % 2 + 1) * HALF],
                                   psum[:, (2, 7)[k % 2], 0:HALF], ACT.Copy).then_inc(s_earlyout, 1)

            @block.tensor
            def _(pe):
                pe.wait_ge(s_dt, 1)
                for i in range(5):
                    m = P if i < 4 else NEW
                    for k, (whole, new) in enumerate((("upto", "upto_new"), ("after", "after_new"))):
                        lhsT = const(whole) if i < 4 else const(new, NEW)
                        at = 80 * k + H_SSD * i
                        mm = pe.matmul(psum[0:m, 3, at:at + H_SSD], lhsT=lhsT, rhs=adt[0:m, i, :],
                                       start=True, stop=True)
                mm.then_inc(s_small6, 1)

                def turn(i):
                    if i:
                        pe.wait_ge(s_xdt, i)
                        pe.wait_ge(s_btok, i)
                    for m in range(8):
                        mm = pe.transpose(psum[:, m // 4, (m % 4) * P:(m % 4) * P + P],
                                          xb[:, m, i * P:i * P + P], const("ident"))
                    mm.then_inc(s_t6, 1)

                def turn_b(i):
                    pe.wait_ge(s_xdt, i + 1)
                    for m in range(4):
                        mm = pe.transpose(psum[:, 0, m * P:m * P + P], xb[:, 8 + m, i * P:i * P + P],
                                          const("ident"))
                    mm.then_inc(s_t6b, 1)

                def early_half(k):
                    n, act_of = T_MERGE + k // 2, (A.at(a_q, 8, NT), hT)[k // 2 % 2]
                    tile_ready(pe, n)
                    if k >= 2:
                        pe.wait_ge(s_earlyout, k - 1)
                    for c in range(DC):
                        mm = pe.matmul(psum[:, (2, 7)[k % 2], 0:HALF], lhsT=w_of(n, c),
                                       rhs=act_of[:, c, (k % 2) * HALF:(k % 2 + 1) * HALF],
                                       start=(c == 0), stop=(c == DC - 1))
                    mm.then_inc(s_early, 1)
                    if k % 2:
                        pe.wait_ge(s_early, k + 1)
                        pe.sem_inc(w_used, 1)

                def decays(k):
                    i, g = C_UNITS[k]
                    if k >= 2:
                        pe.wait_ge(s_e, k - 1)
                    if k >= 1:
                        pe.wait_ge(s_pre, k)
                    if k == 0:
                        pe.wait_ge(s_csout, 1)
                    pe.matmul(psum[:, 3, 0:P], lhsT=xb[:, 8 + g, i * P:i * P + P],
                              rhs=xb[:, 12 + g, i * P:i * P + P], start=True, stop=True)
                    for j in range(HPG):
                        h = HPG * g + j
                        mm = pe.matmul(psum[:, 4 + k % 2, j * P:j * P + P],
                                       lhsT=adt[:, i, h:h + 1].to_broadcast([P, P]), rhs=const("upto"),
                                       start=True, stop=True)
                    mm.then_inc(s_csb, 1)

                def ys(k):
                    i, g = C_UNITS[k]
                    pe.wait_ge(s_mid, k + 1)
                    pe.wait_ge(s_btok, i + 1)
                    if k >= 1:
                        pe.wait_ge(s_post, k)
                    for j in range(HPG):
                        h = HPG * g + j
                        lo = 64 * (h % 2)
                        out = psum[lo:lo + 64, 6, (j // 2) * P:(j // 2) * P + P]
                        pe.matmul(out, lhsT=xdt[:, h * 64:h * 64 + 64], rhs=ebuf[:, k % 2, j * P:j * P + P],
                                  start=True, stop=(i == 0))
                        if i:
                            pe.matmul(out, lhsT=stT[:, h * 64:h * 64 + 64], rhs=chb[:, j * P:j * P + P],
                                      start=False, stop=True)
                    pe.matmul(psum[:, 6, 256:512], lhsT=btok[:, g * P:g * P + P],
                              rhs=xdtd[:, g * 256:g * 256 + 256], start=True, stop=True).then_inc(s_ys, 1)

                for k in range(NCU + 1):
                    if k < NCU and C_UNITS[k][1] == 0:
                        turn(C_UNITS[k][0])
                    if k < NCU:
                        decays(k)
                        early_half(k)
                    if k >= 1:
                        ys(k - 1)
                    if k < NCU and C_UNITS[k][1] == 0:
                        turn_b(C_UNITS[k][0])

            @block.vector
            def _(dve):
                link = Link(dve, v_link6)
                link(dve.tensor_tensor(dt5, small[:, :, 0:H_SSD],
                                       param("dt_bias").unsqueeze(1).to_broadcast([P, 5, H_SSD]), ALU.add))
                link(dve.scalar_tensor_tensor(sp_e, dt5, -1.0, dt5, ALU.mult, ALU.min))
                dve.sem_inc(s_v6, 1)
                link(dve.tensor_scalar(dt5, dt5, 0.0, None, ALU.max))
                dve.wait_ge(s_e6, 1)
                link(dve.tensor_tensor(dt5, dt5, sp_e, ALU.add))
                dve.scalar_tensor_tensor(adt, dt5, -1.0, a_neg.unsqueeze(1).to_broadcast([P, 5, H_SSD]),
                                         ALU.mult, ALU.mult).then_inc(s_dt, 1)
                dve.wait_ge(s_csout, 1)

                def heads(ap):
                    return ap.rearrange("p (h n) -> p h n", n=P_SSD)

                def pre(k):
                    i, g = C_UNITS[k]
                    if g == 0:
                        dve.wait_ge(s_t6, i + 1)
                        if i:
                            dve.wait_ge(s_ys, k)
                        link(dve.tensor_tensor(
                            heads(xdt), psum[:, 0:2, :].rearrange("p a (h n) -> p (a h) n", n=P_SSD),
                            dt5[:, i, :].unsqueeze(2).to_broadcast([P, H_SSD, P_SSD]), ALU.mult))
                        dve.tensor_tensor(heads(xdtd), heads(xdt),
                                          dte[:, i, :].unsqueeze(2).to_broadcast([P, H_SSD, P_SSD]),
                                          ALU.mult).then_inc(s_xdt, 1)
                    dve.wait_ge(s_csb, k + 1)
                    e = ebuf[:, k % 2, :].rearrange("p (j n) -> p j n", n=P)
                    if k >= 2:
                        dve.wait_ge(s_ys, k - 1)
                    link(dve.tensor_tensor(
                        e, psum[:, 4 + k % 2, :].rearrange("p (j n) -> p j n", n=P),
                        cs5[:, i, HPG * g:HPG * g + HPG].unsqueeze(2).to_broadcast([P, HPG, P]),
                        ALU.subtract))
                    dve.tensor_tensor((cbm, cbm2)[k % 2], psum[:, 3, 0:P], const("upto"), ALU.mult)
                    dve.tensor_scalar(e, e, 0.0, None, ALU.min).then_inc(s_pre, 1)

                def mid(k):
                    i, g = C_UNITS[k]
                    dve.wait_ge(s_e, k + 1)
                    e = ebuf[:, k % 2, :].rearrange("p (j n) -> p j n", n=P)
                    ch = chb.rearrange("p (j n) -> p j n", n=P)
                    link(dve.tensor_copy(ecl[:, k % 2, :], ch[:, :, P - 1]))
                    dve.tensor_tensor(ch, ch, xb[:, 12 + g, i * P:i * P + P].unsqueeze(1).to_broadcast(
                        [P, HPG, P]), ALU.mult)
                    dve.tensor_tensor(e, e, (cbm, cbm2)[k % 2].unsqueeze(1).to_broadcast([P, HPG, P]),
                                      ALU.mult).then_inc(s_mid, 1)

                def post(k):
                    i, g = C_UNITS[k]
                    dve.wait_ge(s_ys, k + 1)
                    for j in range(2):
                        m = 2 * g + j
                        x_ = xb[:, m, i * P:i * P + P]
                        dve.scalar_tensor_tensor(x_, x_, param("d_skip")[:, m:m + 1],
                                                 psum[:, 6, j * P:j * P + P], ALU.mult, ALU.add)
                    st = stT[:, g * 256:g * 256 + 256]
                    if i:
                        link(dve.tensor_tensor(heads(st), heads(st), ecl[:, k % 2, :].unsqueeze(2).to_broadcast(
                            [P, HPG, P_SSD]), ALU.mult))
                        dve.tensor_tensor(st, st, psum[:, 6, 256:512], ALU.add).then_inc(s_post, 1)
                    else:
                        dve.tensor_copy(st, psum[:, 6, 256:512]).then_inc(s_post, 1)

                for k in range(NCU + 1):
                    if k < NCU:
                        pre(k)
                    if k >= 1:
                        post(k - 1)
                    if k < NCU:
                        mid(k)

        s_xn, s_t7, s_csb7, s_b7, s_e7, s_g7, s_y7, s_bm, s_su, s_sud, s_c7 = (sem(n) for n in (
            "new_compact", "new_turned", "new_decays_psum", "new_btok", "new_decays", "new_mix", "new_y_psum",
            "bmask_ready", "state_add_psum", "state_ready", "new_args"))
        v_link7 = sem("dve_link7")
        xn = A.at(a_s6, XBC, NEW)
        xdt7 = A.at(a_s6 + 512, D, parts=NEW)
        xdtd7 = A.at(a_s6 + 1536, D, parts=NEW)
        bt7 = A.at(a_s6 + 2560, 512, parts=NEW)
        bm7 = A.at(a_s6 + 3072, NB * P, parts=NEW)
        bm7b = A.at(a_xb + 8 * W_XB, 3, NB * P, parts=NEW)
        e7 = A.at(a_s6 + 4096, H_SSD * NEW, parts=NEW)
        ecp = A.at(a_s6 + 4608, 8, NEW)
        yn = A.at(a_xb + 8 * W_XB + 3072, 8, NEW)
        ytmp = A.at(a_xb + 8 * W_XB + 3072 + 256, 8, NEW)
        dec7 = A.at(a_xb + 8 * W_XB + 3072 + 512, H_SSD, NB)
        cb7 = A.at(a_xb + 8 * W_XB + 3072 + 640, G_SSD, NEW, parts=NEW)

        with nc.Block() as block:
            @block.gpsimd
            def _(pool):
                for m in range(XBC):
                    last = pool.tensor_copy(xn[:, m, :].rearrange("p (b t) -> p b t", t=NS),
                                            seq_new(xb[:, m, :], SEG_P, SEG_S, 0, NS))
                last.then_inc(s_xn, 1)
                pool.wait_ge(s_b7, 1)
                for g in range(G_SSD):
                    to = (bm7 if g == 0 else bm7b[:, g - 1, :]).rearrange("p (b n) -> p b n", n=P)
                    pool.tensor_tensor(to, bt7[:, g * P:g * P + P].unsqueeze(1).to_broadcast([NEW, NB, P]),
                                       const("in_seq", NEW).unsqueeze(2).to_broadcast([NEW, NB, P]),
                                       ALU.mult).then_inc(s_bm, 1)

            @block.tensor
            def _(pe):
                pe.wait_ge(s_xn, 1)
                for m in range(12):
                    mm = pe.transpose(psum[0:NEW, m // 4, (m % 4) * P:(m % 4) * P + P], xn[:, m, :],
                                      const("ident"))
                mm.then_inc(s_t7, 1)
                for g in range(G_SSD):
                    pe.matmul(psum[0:NEW, 3, g * NEW:g * NEW + NEW], lhsT=xn[:, 8 + g, :], rhs=xn[:, 12 + g, :],
                              start=True, stop=True)
                for h in range(H_SSD):
                    mm = pe.matmul(psum[:, 4, h * NEW:h * NEW + NEW],
                                   lhsT=adt[0:NEW, 4, h:h + 1].to_broadcast([NEW, P]),
                                   rhs=const("upto_new", NEW), start=True, stop=True)
                mm.then_inc(s_csb7, 1)
                pe.wait_ge(s_st6, 16)
                for b in range(NB):
                    for m in range(8):
                        mm = pe.matmul(psum[:, 5, m * NEW + b * NS:m * NEW + b * NS + NS],
                                       lhsT=states[:, b, m * P:m * P + P],
                                       rhs=xn[:, 12 + m // 2, b * NS:b * NS + NS], start=True, stop=True)
                pe.wait_ge(s_g7, 1)
                for h in range(H_SSD):
                    lo = 64 * (h % 2)
                    mm = pe.matmul(psum[lo:lo + 64, 6, (h // 2) * NEW:(h // 2) * NEW + NEW],
                                   lhsT=xdt7[:, h * 64:h * 64 + 64], rhs=e7[:, h * NEW:h * NEW + NEW],
                                   start=True, stop=True)
                mm.then_inc(s_y7, 1)
                pe.wait_ge(s_bm, G_SSD)
                for b in range(NB):
                    if b == 0:
                        pe.wait_ge(s_b7, 1)
                        pe.wait_ge(s_c7, 1)
                    if b >= 2:
                        pe.wait_ge(s_sud, b - 1)
                    for g in range(G_SSD):
                        bm = bm7 if g == 0 else bm7b[:, g - 1, :]
                        mm = pe.matmul(psum[:, 2 * (b % 2) + g // 2, (g % 2) * 256:(g % 2) * 256 + 256],
                                       lhsT=bm[:, b * P:b * P + P], rhs=xdtd7[:, g * 256:g * 256 + 256],
                                       start=True, stop=True)
                    mm.then_inc(s_su, 1)

            @block.scalar
            def _(act):
                act.wait_ge(s_t7, 1)
                act.activation(bt7, psum[0:NEW, 2, :], ACT.Copy).then_inc(s_b7, 1)
                act.wait_ge(s_c7, 1)
                csb = psum[:, 4, :].rearrange("p (m o n) -> p m o n", o=2, n=NEW)
                for o in range(2):
                    act.activation(ecp[64 * o:64 * o + 64], csb[64 * o:64 * o + 64, :, o, :], ACT.Exp)
                act.activation(dec7, psum[:, 4, :].rearrange("p (h b t) -> p h b t", b=NB, t=NS)[:, :, :, NS - 1],
                               ACT.Exp)
                act.activation(e7, e7, ACT.Exp).then_inc(s_e7, 1)

            @block.vector
            def _(dve):
                link = Link(dve, v_link7)
                heads = lambda ap: ap.rearrange("p (h n) -> p h n", n=P_SSD)
                dve.wait_ge(s_t7, 1)
                bc = lambda a: a[0:NEW, 4, :].unsqueeze(2).to_broadcast([NEW, H_SSD, P_SSD])
                link(dve.tensor_tensor(heads(xdt7), psum[0:NEW, 0:2, :].rearrange(
                    "p a (h n) -> p (a h) n", n=P_SSD), bc(dt5), ALU.mult))
                link(dve.tensor_tensor(heads(xdtd7), heads(xdt7), bc(dte), ALU.mult))
                dve.wait_ge(s_csb7, 1)
                e3 = e7.rearrange("p (h n) -> p h n", n=NEW)
                link(dve.tensor_tensor(e3, psum[0:NEW, 4, :].rearrange("p (h n) -> p h n", n=NEW),
                                       cs5[0:NEW, 4, :].unsqueeze(2).to_broadcast([NEW, H_SSD, NEW]),
                                       ALU.subtract))
                dve.tensor_tensor(cb7, psum[0:NEW, 3, 0:G_SSD * NEW].rearrange("p (g n) -> p g n", n=NEW),
                                  const("upto_new", NEW).unsqueeze(1).to_broadcast([NEW, G_SSD, NEW]), ALU.mult)
                dve.tensor_scalar(e7, e7, 0.0, None, ALU.min).then_inc(s_c7, 1)
                dve.wait_ge(s_e7, 1)
                for g in range(G_SSD):
                    at = g * HPG * NEW
                    e_g = e7[:, at:at + HPG * NEW].rearrange("p (j n) -> p j n", n=NEW)
                    last = dve.tensor_tensor(e_g, e_g, cb7[:, g, :].unsqueeze(1).to_broadcast(
                        [NEW, HPG, NEW]), ALU.mult)
                last.then_inc(s_g7, 1)
                dve.wait_ge(s_y7, 1)
                p7 = lambda bank: psum[:, bank, 0:8 * NEW].rearrange("p (m n) -> p m n", n=NEW)
                link(dve.tensor_tensor(ytmp, p7(5), ecp, ALU.mult))
                link(dve.tensor_tensor(ytmp, ytmp, p7(6), ALU.add))
                link(dve.tensor_tensor(yn, xn[:, 0:8, :], param("d_skip").unsqueeze(2).to_broadcast(
                    [P, 8, NEW]), ALU.mult))
                link(dve.tensor_tensor(yn, yn, ytmp, ALU.add))
                for b in range(NB):
                    st = states[:, b, :].rearrange("p (h n) -> p h n", n=P_SSD)
                    link(dve.tensor_tensor(st, st, dec7[:, :, b].unsqueeze(2).to_broadcast(
                        [P, H_SSD, P_SSD]), ALU.mult))
                    dve.wait_ge(s_su, b + 1)
                    bank = 2 * (b % 2)
                    dve.tensor_tensor(states[:, b, :], states[:, b, :],
                                      psum[:, bank:bank + 2, :].rearrange("p a n -> p (a n)"),
                                      ALU.add).then_inc(s_sud, 1)

            @block.sync
            def _(sp):
                for b in range(NB):
                    sp.wait_ge(s_sud, b + 1)
                    write(sp, outs["ssm_s"][:, b * D:(b + 1) * D], states[:, b, :])
                sp.wait_ge(s_out, outs_written[0])

        s_sz, s_gy, s_sq8, s_ss8, s_std8, s_ya = (sem(n) for n in (
            "silu_z", "gated_y", "gated_squares", "group_sums", "group_std", "ya_ready"))
        s_sig, s_pd, s_mg, s_shin = (sem(n) for n in (
            "gate_ready", "branch_gated", "merged_ready", "short_loaded"))
        v_link8 = sem("dve_link8")
        merged = A.at(a_xb, DC, NT)
        rs8 = A.at(a_s6, 2, NT)
        sg8 = A.at(a_tmp, 2, NT)
        tm8 = A.at(a_tmp + 2 * NT, NT)
        sq8 = A.at(a_tmp + 3 * NT, 8, NT)
        LATE = 8 - EARLY
        N_UNITS = LATE + 8
        s_eg, s_ep = sem("early_gate"), sem("early_product")

        def pairs_of(e):
            k = 0 if e < 3 else 2 * (e % 2)
            return pair[k], pair[k + 1]

        with nc.Block() as block:
            @block.sync
            def _(sp):
                sp.wait_ge(s_gy, 8)
                sp.dma_start(merged, short_dram.rearrange("m p n -> p m n")).then_inc(s_shin, 16)
                load_tiles(sp, T_MERGE + 2 * RING, T_END)

            @block.scalar
            def _(act):
                def sigmoid(e):
                    act.wait_ge(w_used, T_MERGE + 2 * (EARLY + e) + 2)
                    if e >= 2:
                        act.wait_ge(s_pd, e - 1)
                    act.activation(halves(sg8[:, e % 2, :]), pairs_of(e)[1], ACT.Sigmoid).then_inc(s_sig, 1)

                for m in range(8):
                    act.activation(zT[:, m, :], zT[:, m, :], ACT.Silu).then_inc(s_sz, 1)
                for m in range(8):
                    act.wait_ge(s_gy, m + 1)
                    act.activation(sq8[:, m, :], zT[:, m, :], ACT.Square).then_inc(s_sq8, 1)
                for m in range(EARLY):
                    act.activation(early[:, 2 * m + 1, :], early[:, 2 * m + 1, :], ACT.Sigmoid).then_inc(s_eg, 1)
                for e in range(2):
                    sigmoid(e)
                    for g in (2 * e, 2 * e + 1):
                        act.wait_ge(s_ss8, g + 1)
                        if g >= 2:
                            act.wait_ge(s_ya, 2 * g - 2)
                        act.activation(halves(rs8[:, g % 2, :]), pair[2 + g % 2], ACT.Sqrt,
                                       bias=eps_col[:, 0:1], scale=1.0 / 256).then_inc(s_std8, 1)
                for e in range(2, N_UNITS):
                    sigmoid(e)

            @block.tensor
            def _(pe):
                for e in range(N_UNITS):
                    u = T_MERGE + 2 * (EARLY + e)
                    if e == 3:
                        pe.wait_ge(s_std8, G_SSD)
                    if e == LATE:
                        pe.wait_ge(s_ya, 8)
                    before = e if e < 3 else e - 1
                    for k, (out, act_of) in enumerate(zip(pairs_of(e), (A.at(a_q, 8, NT) if e < LATE else zT, hT))):
                        tile_ready(pe, u + k)
                        if e:
                            pe.wait_ge(s_sig if k else s_pd, before)
                        project(pe, u + k, out, act_of).then_inc(w_used, 1)
                    if e < 2:
                        for g in (2 * e, 2 * e + 1):
                            if g >= 2:
                                pe.wait_ge(s_std8, g - 1)
                            for m in (2 * g, 2 * g + 1):
                                pe.wait_ge(s_sq8, m + 1)
                                for h in range(2):
                                    mm = pe.matmul(pair[2 + g % 2][:, h, :], lhsT=const("ones"),
                                                   rhs=sq8[:, m, h * HALF:(h + 1) * HALF],
                                                   start=(m % 2 == 0), stop=(m % 2 == 1))
                            mm.then_inc(s_ss8, 1)

            @block.vector
            def _(dve):
                link = Link(dve, v_link8)
                for m in range(8):
                    dve.wait_ge(s_sz, m + 1)
                    dve.tensor_tensor(zT[:, m, 0:SEQ], zT[:, m, 0:SEQ], xb[:, m, 0:SEQ], ALU.mult)
                    link(dve.tensor_tensor(zT[:, m, SEQ:NT], zT[:, m, SEQ:NT], yn[:, m, :], ALU.mult))
                    dve.sem_inc(s_gy, 1)
                dve.wait_ge(s_shin, 16)
                for m in range(EARLY):
                    dve.wait_ge(s_eg, m + 1)
                    dve.tensor_tensor(early[:, 2 * m, :], early[:, 2 * m, :], early[:, 2 * m + 1, :],
                                      ALU.mult).then_inc(s_ep, 1)
                for m in range(EARLY):
                    dve.wait_ge(s_ep, m + 1)
                    last = dve.tensor_tensor(merged[:, m, :], merged[:, m, :], early[:, 2 * m, :], ALU.add)
                link(last)
                for e in range(N_UNITS):
                    dve.wait_ge(s_sig, e + 1)
                    if e:
                        dve.wait_ge(s_mg, e)
                    dve.tensor_tensor(halves(tm8), halves(sg8[:, e % 2, :]), pairs_of(e)[0],
                                      ALU.mult).then_inc(s_pd, 1)
                    dve.wait_ge(s_pd, e + 1)
                    m = (EARLY + e) % 8
                    dve.tensor_tensor(merged[:, m, :], merged[:, m, :], tm8, ALU.add).then_inc(s_mg, 1)
                    if e < 2:
                        for g in (2 * e, 2 * e + 1):
                            rs = rs8[:, g % 2, :]
                            dve.wait_ge(s_std8, g + 1)
                            link(dve.reciprocal(rs, rs))
                            for m in (2 * g, 2 * g + 1):
                                dve.scalar_tensor_tensor(zT[:, m, :], zT[:, m, :],
                                                         param("ssm_norm")[:, m:m + 1], rs,
                                                         ALU.mult, ALU.mult).then_inc(s_ya, 1)

        s_x10, s_res = sem("x_again"), sem("residual_done")
        v_link10 = sem("dve_link10")

        def by_seq(a):
            return a.rearrange("p (b t) -> p b t", t=NS)

        def per_seq(cols):
            return cols[:, 1:NSEQ].unsqueeze(2).to_broadcast([P, NB, NS])

        (s_tab, s_idx, s_gath, s_scat, s_rows, s_wgu, s_wdn, s_xps, s_xsb, s_gu, s_act, s_silu12, s_aps,
         s_asb) = (sem(n) for n in (
            "table_loaded", "gather_index", "rows_gathered", "rows_scattered", "rows_cleared", "wgu_loaded",
            "wdown_loaded", "x_turned", "x_out", "gate_up", "act_ready", "silu_ready", "act_turned", "act_out"))
        s_dn, s_yo, s_gath1, s_scat1, s_wgu1, s_wdn1, s_passed = (sem(n) for n in (
            "down_ready", "y_staged", "rows_gathered1", "rows_scattered1", "wgu_loaded1", "wdown_loaded1",
            "dma_may_start"))
        gath, scat, wgu_full, wdn_full = (s_gath, s_gath1), (s_scat, s_scat1), (s_wgu, s_wgu1), (s_wdn, s_wdn1)
        a_e = a_q
        w_gu = A.at(a_e, 2, 2 * DC * FF)
        w_dn = A.at(a_e + 8192, 2, 2 * D)
        xg = A.at(a_e + 12288, 2, D)
        xgT = A.at(a_e + 14336, 2, DC * P)
        actb = A.at(a_e + 16384, 2, FF)
        actT = A.at(a_e + 16896, 2, 2 * P)
        yst = A.at(a_e + 17408, 2, D)
        sil = A.at(a_e + 19456, 2, FF)
        tab_i = A.at(a_e + 19968, NE).bitcast(I32)
        gat_i = A.at(a_e + 20000, NE).bitcast(I32)
        (s_sq11, s_ss11, s_std11, s_n11, s_hp11, s_hs11, s_rt, s_rl, s_ge, s_gi, s_pe2,
         s_pe2o) = (sem(n) for n in (
            "squares2", "square_sums2", "std2", "normed2", "h2_prompt", "h2_sample", "router_logits",
            "router_logits_out", "group_exp", "group_args", "expert_exp", "expert_args"))
        s_row_ps, s_row_sb, s_rank, s_slot, s_tabinit, s_tabw, s_h2w = (sem(n) for n in (
            "rows_in_psum", "rows_in_sbuf", "ranks_in_psum", "slots_ready", "table_cleared", "table_written",
            "h2_written"))
        v_link11 = sem("dve_link11")
        s_h2w = (s_h2w, sem("h2_written1"))
        sq11 = A.at(a_z, DC, NT)
        rstd11 = A.at(a_tmp, NT)
        a_r = a_tmp + NT
        NR = 5
        lg = A.at(a_r, NR, 36)
        gpad = A.at(a_r + 180, NR, 8)
        g8, e8 = A.at(a_r + 220, NR, 8), A.at(a_r + 260, NR, 8)
        gi8, ei8 = A.at(a_r + 300, NR, 8), A.at(a_r + 340, NR, 8)
        gif, eif = A.at(a_r + 380, NR, 1), A.at(a_r + 385, NR, 2)
        goh = A.at(a_r + 395, NR, NG)
        gexp = A.at(a_r + 415, NR, NG)
        gsum = A.at(a_r + 435, NR)
        masked = A.at(a_r + 440, NR, NG, EPG)
        fine = A.at(a_r + 600, NR, EPG)
        oh = [A.at(a_r + 640 + 40 * k, NR, EPG) for k in range(2)]
        full = [A.at(a_r + 720 + 160 * k, NR, NE) for k in range(2)]
        both = A.at(a_r + 1040, NR, NE)
        slotm = A.at(a_r + 1200, NR, NE)
        tmp32 = A.at(a_r + 1360, NR, NE)
        slotf = A.at(a_r + 1520, 2, NR)
        p2 = A.at(a_r + 1530, NR)
        mx = A.at(a_r + 1567, 8)
        wcol = A.at(a_param + PARAM_AT["conv_prev"][0], 2, NR)
        a_keep = a_param + PARAM_AT["conv_prev"][0] + 16
        slot_i = A.at(a_keep, 2, NR).bitcast(I32)
        value_i = A.at(a_keep + 10, 2, NR).bitcast(I32)
        rounds_i = A.at(a_keep + 20, 1).bitcast(I32)
        none_i = A.at(a_keep + 21, NR * NE).bitcast(I32)
        rows11 = A.at(a_xb + DC * NT, 2, D)
        CAP = P
        NO_ROW = 4 * NT
        table = nc.dram_tensor("slot_table", [NR * CAP * NE, 1], I32).ap()
        h2_rows = nc.dram_tensor("h2_rows", [NT, D], F32).ap()
        y_rows = nc.dram_tensor("y_rows", [2 * NT, D], F32).ap()

        with nc.Block() as block:
            @block.sync
            def _(sp):
                sp.dma_start(xT, ins["x"]).then_inc(s_x10, 16)

            @block.tensor
            def _(pe):
                for u in range(8):
                    tile_ready(pe, T_O + u)
                    if u >= 4:
                        pe.wait_ge(s_res, u - 3)
                    project(pe, T_O + u, pair[u % 4], merged).then_inc(w_used, 1)

            @block.vector
            def _(dve):
                link = Link(dve, v_link10)
                tmp = A.at(a_tmp, NEW)
                dve.wait_ge(s_x10, 16)
                rest = SEQ - HALF
                for m in range(8):
                    ps, gate = pair[m % 4], mods[:, 16 + m, :]
                    dve.wait_ge(w_used, T_O + m + 1)
                    for dst, src in ((xT[:, m, 0:HALF], ps[:, 0, :]), (xT[:, m, HALF:SEQ], ps[:, 1, 0:rest])):
                        dve.scalar_tensor_tensor(dst, src, gate[:, 0:1], dst, ALU.mult, ALU.add)
                    link(dve.tensor_tensor(by_seq(tmp), by_seq(ps[:, 1, rest:HALF]), per_seq(gate), ALU.mult))
                    new = xT[:, m, SEQ:NT]
                    link(dve.tensor_tensor(new, new, tmp, ALU.add))
                    dve.sem_inc(s_res, 1)

            @block.scalar
            def _(act):
                for c in range(DC):
                    act.wait_ge(s_res, c + 1)
                    act.activation(sq11[:, c, :], xT[:, c, :], ACT.Square).then_inc(s_sq11, 1)
                act.wait_ge(s_ss11, 1)
                act.activation(halves(rstd11), pair[0], ACT.Sqrt, bias=eps_col[:, 0:1],
                               scale=1.0 / D).then_inc(s_std11, 1)
                for c in range(DC):
                    act.wait_ge(s_n11, c + 1)
                    act.activation(hT[:, c, 0:SEQ], sq11[:, c, 0:SEQ], ACT.Identity,
                                   bias=mods[:, 24 + c, 0:1], scale=gain[:, 1, c, 0:1]).then_inc(s_hp11, 1)

                def rows_out(i):
                    m = P if i < 4 else NEW
                    act.wait_ge(s_row_ps, i + 1)
                    if i >= 2:
                        act.wait_ge(s_h2w[i % 2], 16 * (i // 2))
                    b = 2 + 2 * (i % 2)
                    act.activation(rows11[0:m, i % 2, :].rearrange("p (a n) -> p a n", n=512),
                                   psum[0:m, b:b + 2, :], ACT.Copy).then_inc(s_row_sb, 1)

                for i in range(2):
                    rows_out(i)
                act.wait_ge(s_gi, 1)
                act.activation(gexp, gexp, ACT.Exp).then_inc(s_ge, 1)
                act.wait_ge(s_pe2o, 1)
                act.activation(p2, p2, ACT.Exp).then_inc(s_pe2, 1)
                for i in range(2, NR):
                    rows_out(i)

            @block.tensor
            def _(pe):
                pe.sem_inc(s_gu, 2)
                pe.sem_inc(s_dn, 2)
                for c in range(DC):
                    if c == 0:
                        pe.wait_ge(s_res, 5)
                    pe.wait_ge(s_sq11, c + 1)
                    for h in range(2):
                        mm = pe.matmul(pair[0][:, h, :], lhsT=const("ones"),
                                       rhs=sq11[:, c, h * HALF:(h + 1) * HALF],
                                       start=(c == 0), stop=(c == DC - 1))
                mm.then_inc(s_ss11, 1)
                pe.wait_ge(s_hp11, DC)
                pe.wait_ge(s_hs11, DC)
                router = param("router").rearrange("p (c n) -> p c n", n=36)
                for i in range(NR):
                    m = P if i < 4 else NEW
                    for c in range(DC):
                        mm = pe.matmul(psum[0:m, 6, i * 36:i * 36 + 36], lhsT=hT[:, c, i * P:i * P + m],
                                       rhs=router[:, c, :], start=(c == 0), stop=(c == DC - 1))
                mm.then_inc(s_rt, 1)

                def turn_rows(i):
                    m = P if i < 4 else NEW
                    if i >= 2:
                        pe.wait_ge(s_row_sb, i - 1)
                    for c in range(DC):
                        mm = pe.transpose(psum[0:m, 2 + 2 * (i % 2) + c // 4, (c % 4) * P:(c % 4) * P + P],
                                          hT[:, c, i * P:i * P + m], const("ident"))
                    mm.then_inc(s_row_ps, 1)

                for i in range(2):
                    turn_rows(i)
                pe.wait_ge(s_rl, 2)
                for i in range(NR):
                    m = P if i < 4 else NEW
                    for j in range(i):
                        pe.matmul(psum[0:m, 7, i * NE:i * NE + NE], lhsT=const("ones")[:, 0:m],
                                  rhs=both[:, j, :], start=(j == 0), stop=False)
                    pe.matmul(psum[0:m, 7, i * NE:i * NE + NE], lhsT=const("upto")[0:m, 0:m],
                              rhs=both[0:m, i, :], start=(i == 0), stop=True)
                for j in range(NR):
                    m = P if j < 4 else NEW
                    mm = pe.matmul(psum[:, 7, NR * NE:(NR + 1) * NE], lhsT=const("ones")[0:m, :],
                                   rhs=both[0:m, j, :], start=(j == 0), stop=(j == NR - 1))
                mm.then_inc(s_rank, 1)
                for i in range(2, NR):
                    turn_rows(i)

            @block.vector
            def _(dve):
                link = Link(dve, v_link11)
                dve.memset(none_i, NO_ROW).then_inc(s_tabinit, 1)
                dve.memset(lg[:, 4, :], 0.0)
                dve.memset(slotm[:, 4, :], 0.0)
                link(dve.memset(gpad, -3e38))
                dve.wait_ge(s_std11, 1)
                link(dve.reciprocal(rstd11, rstd11))
                for c in range(DC):
                    dve.tensor_tensor(sq11[:, c, :], xT[:, c, :], rstd11, ALU.mult).then_inc(s_n11, 1)
                dve.wait_ge(s_n11, DC)
                for c in range(DC):
                    new = by_seq(sq11[:, c, SEQ:NT])
                    link(dve.tensor_tensor(new, new, per_seq(gain[:, 1, c, :]), ALU.mult))
                    dve.tensor_tensor(by_seq(hT[:, c, SEQ:NT]), new, per_seq(mods[:, 24 + c, :]),
                                      ALU.add).then_inc(s_hs11, 1)
                dve.wait_ge(s_rt, 1)
                dve.tensor_copy(lg[:, 0:4, :], psum[:, 6, 0:144].rearrange("p (a b) -> p a b", b=36))
                link(dve.tensor_copy(lg[0:NEW, 4, :], psum[0:NEW, 6, 144:180]))
                link(dve.tensor_copy(gpad[:, :, 0:NG], lg[:, :, 0:NG]))

                def top_of(vals, best, idx):
                    for i in range(NR):
                        last = dve.max(best[:, i, :], vals[:, i, :])
                    link(last)
                    for i in range(NR):
                        last = dve.max_index(idx[:, i, :].bitcast(U32), best[:, i, :], vals[:, i, :])
                    link(last)

                bc = lambda a, *s: a.to_broadcast([P, *s])
                iota = const("iota8")
                top_of(gpad, g8, gi8)
                link(dve.tensor_copy(gif, gi8[:, :, 0:1].bitcast(U32)))
                dve.tensor_tensor(goh, bc(iota[:, 0:NG].unsqueeze(1), NR, NG), bc(gif, NR, NG), ALU.is_equal)
                link(dve.tensor_tensor(gexp, lg[:, :, 0:NG], bc(g8[:, :, 0:1], NR, NG), ALU.subtract))
                dve.sem_inc(s_gi, 1)
                link(dve.tensor_tensor(masked, lg[:, :, NG:NG + NE].rearrange("p i (g e) -> p i g e", e=EPG),
                                       bc(goh.unsqueeze(3), NR, NG, EPG), ALU.mult))
                link(dve.tensor_reduce(fine, masked.rearrange("p i g e -> p i e g"), AX, ALU.add))
                top_of(fine, e8, ei8)
                link(dve.tensor_copy(eif, ei8[:, :, 0:2].bitcast(U32)))
                for k in range(2):
                    link(dve.tensor_tensor(oh[k], bc(iota.unsqueeze(1), NR, EPG),
                                           bc(eif[:, :, k:k + 1], NR, EPG), ALU.is_equal))
                    for g in range(NG):
                        last = dve.tensor_tensor(full[k][:, :, g * EPG:g * EPG + EPG], oh[k],
                                                 bc(goh[:, :, g:g + 1], NR, EPG), ALU.mult)
                    link(last)
                link(dve.tensor_tensor(both, full[0], full[1], ALU.add))
                dve.sem_inc(s_rl, 2)
                link(dve.tensor_tensor(p2, e8[:, :, 1], e8[:, :, 0], ALU.subtract))
                dve.sem_inc(s_pe2o, 1)
                dve.wait_ge(s_ge, 1)
                link(dve.tensor_reduce(gsum, gexp, AX, ALU.add))
                dve.wait_ge(s_pe2, 1)
                link(dve.scalar_tensor_tensor(mx[:, 0:NR], p2, 1.0, gsum, ALU.add, ALU.mult))
                link(dve.reciprocal(wcol[:, 0, :], mx[:, 0:NR]))
                link(dve.tensor_tensor(wcol[:, 1, :], wcol[:, 0, :], p2, ALU.mult))
                dve.wait_ge(s_rank, 1)
                dve.tensor_scalar(slotm[:, 0:4, :], psum[:, 7, 0:4 * NE].rearrange("p (a b) -> p a b", b=NE),
                                  -1.0, float(NE), ALU.add, ALU.mult)
                dve.tensor_scalar(slotm[0:NEW, 4, :], psum[0:NEW, 7, 4 * NE:5 * NE], -1.0, float(NE),
                                  ALU.add, ALU.mult)
                link(dve.tensor_reduce(mx[:, 0:1], psum[:, 7, NR * NE:(NR + 1) * NE], AX, ALU.max))
                link(dve.tensor_tensor(slotm, slotm, bc(const("iota32").unsqueeze(1), NR, NE), ALU.add))
                for k in range(2):
                    link(dve.tensor_tensor(tmp32, slotm, full[k], ALU.mult))
                    link(dve.tensor_reduce(slotf[:, k, :], tmp32, AX, ALU.add))
                dve.tensor_copy(slot_i, slotf)
                link(dve.tensor_scalar(mx[:, 1:2], mx[:, 0:1], float(CAP), 1.0, ALU.is_gt, ALU.add))
                for j in range(2, NR):
                    link(dve.scalar_tensor_tensor(mx[:, j:j + 1], mx[:, 0:1], float(CAP * j),
                                                  mx[:, j - 1:j], ALU.is_gt, ALU.add))
                link(dve.tensor_copy(rounds_i, mx[:, NR - 1:NR]))
                link(dve.tensor_copy(value_i, const("row_values").rearrange("p (a b) -> p a b", b=NR)))
                dve.sem_inc(s_slot, 1)

            @block.sync
            def _(sp):
                for i in range(NR):
                    m = P if i < 4 else NEW
                    sp.wait_ge(s_row_sb, i + 1)
                    sp.dma_start(h2_rows[i * P:i * P + m, :], rows11[0:m, i % 2, :]).then_inc(s_h2w[i % 2], 16)
                sp.wait_ge(s_h2w[0], 16 * 3)
                sp.wait_ge(s_h2w[1], 16 * 2)

            @block.gpsimd
            def _(pool):
                pool.wait_ge(s_tabinit, 1)
                pool.dma_start(table.rearrange("(p n) o -> p (n o)", p=P), none_i).then_inc(s_tabw, 16)
                pool.wait_ge(s_hp11, DC)
                pool.wait_ge(s_hs11, DC)
                pool.memset(xg, 0.0).then_inc(s_rows, 1)
                pool.wait_ge(s_slot, 1)
                pool.wait_ge(s_tabw, 16)
                for k in range(2):
                    for i in range(NR):
                        m = P if i < 4 else NEW
                        pool.indirect_dma_start(
                            out=table, out_offset=bass.IndirectOffsetOnAxis(slot_i[0:m, k, i:i + 1], 0),
                            in_=value_i[0:m, k, i:i + 1], in_offset=None).then_inc(s_tabw, 16)
                pool.wait_ge(s_tabw, 16 * (1 + 2 * NR))

            def rounds(eng):
                eng.wait_ge(s_slot, 1)
                return eng.value_load(rounds_i[0:1, 0:1], min_val=1, max_val=NR)

            @block.sync
            def _(sp):
                def gate_up_in(r, e2, k):
                    sp.wait_ge(s_gu, r * NE + e2 * 2 + (k + 1))
                    sp.dma_start(w_gu[:, k, :], ins["w_gu"][bass.ds(e2 * 2 + k, 1)].rearrange(
                        "a p n -> (a p) n")).then_inc(wgu_full[k], 16)

                def down_in(r, e2, k):
                    sp.wait_ge(s_dn, r * NE + e2 * 2 + (k + 1))
                    sp.dma_start(w_dn[:, k, :], ins["w_down"][bass.ds(e2 * 2 + k, 1)].rearrange(
                        "a p n -> (a p) n")).then_inc(wdn_full[k], 16)

                with sp.Fori(0, rounds(sp)) as r:
                    gate_up_in(r, 0, 0)
                    gate_up_in(r, 0, 1)
                    with sp.Fori(1, NE // 2) as e2:
                        down_in(r, e2 - 1, 0)
                        gate_up_in(r, e2, 0)
                        down_in(r, e2 - 1, 1)
                        gate_up_in(r, e2, 1)
                    down_in(r, NE // 2 - 1, 0)
                    down_in(r, NE // 2 - 1, 1)

            @block.gpsimd
            def _(pool):
                pool.sem_inc(s_xps, 2)
                for k, n in ((0, 3), (1, 2)):
                    pool.wait_ge(s_h2w[k], 16 * n)
                last_token, last_row = pool.to_reg(NT - 1), pool.to_reg(2 * NT - 1)
                with pool.Fori(0, rounds(pool)) as r:
                    pool.dma_start(tab_i, table[bass.ds(r * (CAP * NE), CAP * NE), :].rearrange(
                        "(p n) o -> p (n o)", p=P)).then_inc(s_tab, 16)
                    pool.wait_ge(s_idx, r + 1)
                    pool.wait_ge(s_rows, 1)
                    for e in range(NE + 3):
                        k = e % 2
                        if e < NE:
                            pool.wait_ge(s_xps, r * NE + (e + 1))
                            pool.sem_inc(s_passed, 1)
                            pool.indirect_dma_start(
                                out=xg[:, k, :], out_offset=None, in_=h2_rows,
                                in_offset=bass.IndirectOffsetOnAxis(gat_i[:, e:e + 1], 0),
                                bounds_check=last_token, oob_is_err=False).then_inc(gath[k], 16)
                        if e >= 3:
                            k = (e - 3) % 2
                            pool.wait_ge(s_yo, r * NE + (e - 1))
                            pool.sem_inc(s_passed, 1)
                            pool.indirect_dma_start(
                                out=y_rows, out_offset=bass.IndirectOffsetOnAxis(tab_i[:, e - 3:e - 2], 0),
                                in_=yst[:, k, :], in_offset=None,
                                bounds_check=last_row, oob_is_err=False).then_inc(scat[k], 16)
                    pool.wait_ge(scat[0], r * (8 * NE) + 8 * NE)
                    pool.wait_ge(scat[1], r * (8 * NE) + 8 * NE)
                    pool.sem_inc(s_passed, 1)

            @block.tensor
            def _(pe):
                def at(r, e2, k):
                    return r * NE + e2 * 2 + k, r * (8 * NE) + e2 * 16 + 16

                def turn_x(r, e2, k):
                    n, half = at(r, e2, k)
                    pe.wait_ge(gath[k], half)
                    pe.wait_ge(s_xsb, n + 1)
                    for c in range(DC):
                        mm = pe.transpose(psum[:, c // 4, (c % 4) * P:(c % 4) * P + P],
                                          xg[:, k, c * P:c * P + P], const("ident"))
                    mm.then_inc(s_xps, 1)

                def gate_up(r, e2, k):
                    n, half = at(r, e2, k)
                    pe.wait_ge(s_xsb, n + 2)
                    pe.wait_ge(wgu_full[k], half)
                    pe.wait_ge(s_act, n + 1)
                    wv = w_gu[:, k, :].rearrange("p (o c f) -> p c o f", o=2, c=DC)
                    for c in range(DC):
                        mm = pe.matmul(psum[:, 2 + k, :].rearrange("p (o f) -> p o f", o=2),
                                       lhsT=xgT[:, k, c * P:c * P + P], rhs=wv[:, c],
                                       start=(c == 0), stop=(c == DC - 1))
                    mm.then_inc(s_gu, 1)

                def turn_act(r, e2, k):
                    n, _ = at(r, e2, k)
                    pe.wait_ge(s_act, n + 3)
                    for f in range(2):
                        mm = pe.transpose(psum[:, 6, f * P:f * P + P], actb[:, k, f * P:f * P + P],
                                          const("ident"))
                    mm.then_inc(s_aps, 1)

                def down(r, e2, k):
                    n, half = at(r, e2, k)
                    pe.wait_ge(s_asb, n + 1)
                    pe.wait_ge(wdn_full[k], half)
                    pe.wait_ge(s_yo, n + 1)
                    for h in range(2):
                        for f in range(2):
                            mm = pe.matmul(psum[:, 4 + h, :], lhsT=actT[:, k, f * P:f * P + P],
                                           rhs=w_dn[:, k, f * D + h * 512:f * D + h * 512 + 512],
                                           start=(f == 0), stop=(f == 1))
                    mm.then_inc(s_dn, 1)

                def two_experts(r, e2, first=False, last=False):
                    gate_up(r, e2, 0)
                    turn_x(r, e2, 1)
                    if not first:
                        down(r, e2 - 1, 1)
                    turn_act(r, e2, 0)
                    gate_up(r, e2, 1)
                    if not last:
                        turn_x(r, e2 + 1, 0)
                    down(r, e2, 0)
                    turn_act(r, e2, 1)

                with pe.Fori(0, rounds(pe)) as r:
                    turn_x(r, 0, 0)
                    two_experts(r, 0, first=True)
                    with pe.Fori(1, NE // 2 - 1) as e2:
                        two_experts(r, e2)
                    two_experts(r, NE // 2 - 1, last=True)
                    down(r, NE // 2 - 1, 1)

            @block.scalar
            def _(act):
                def x_out(r, e2, k):
                    act.wait_ge(s_xps, r * NE + e2 * 2 + k + 3)
                    act.activation(xgT[:, k, :].rearrange("p (a n) -> p a n", n=512), psum[:, 0:2, :],
                                   ACT.Copy).then_inc(s_xsb, 1)

                def two_experts(r, e2, last=False):
                    for k in range(2):
                        n = r * NE + e2 * 2 + k
                        act.wait_ge(s_gu, n + 3)
                        act.activation(sil[:, k, :], psum[:, 2 + k, 0:FF], ACT.Silu).then_inc(s_silu12, 1)
                        if k == 0:
                            x_out(r, e2, 1)
                        elif not last:
                            x_out(r, e2 + 1, 0)
                        act.wait_ge(s_aps, n + 1)
                        act.activation(actT[:, k, :], psum[:, 6, 0:2 * P], ACT.Copy).then_inc(s_asb, 1)

                act.sem_inc(s_xsb, 1)
                with act.Fori(0, rounds(act)) as r:
                    x_out(r, 0, 0)
                    with act.Fori(0, NE // 2 - 1) as e2:
                        two_experts(r, e2)
                    two_experts(r, NE // 2 - 1, last=True)

            @block.vector
            def _(dve):
                def mix(r, e2, k):
                    n = r * NE + e2 * 2 + k
                    dve.wait_ge(s_silu12, n + 1)
                    dve.tensor_tensor(actb[:, k, :], sil[:, k, :], psum[:, 2 + k, FF:2 * FF],
                                      ALU.mult).then_inc(s_act, 1)

                def y_out(r, e2, k, first=False):
                    dve.wait_ge(s_dn, r * NE + e2 * 2 + k + 3)
                    if not first:
                        dve.wait_ge(scat[k], r * (8 * NE) + e2 * 16)
                    dve.tensor_copy(yst[:, k, :].rearrange("p (a n) -> p a n", n=512),
                                    psum[:, 4:6, :]).then_inc(s_yo, 1)

                dve.sem_inc(s_act, 2)
                dve.sem_inc(s_yo, 1)
                with dve.Fori(0, rounds(dve)) as r:
                    dve.wait_ge(s_tab, r * 16 + 16)
                    dve.tensor_scalar(gat_i, tab_i, 1, None, ALU.logical_shift_right).then_inc(s_idx, 1)
                    mix(r, 0, 0)
                    mix(r, 0, 1)
                    y_out(r, 0, 0, first=True)
                    mix(r, 1, 0)
                    y_out(r, 0, 1, first=True)
                    mix(r, 1, 1)
                    y_out(r, 1, 0)
                    with dve.Fori(2, NE // 2) as e2:
                        mix(r, e2, 0)
                        y_out(r, e2 - 1, 1)
                        mix(r, e2, 1)
                        y_out(r, e2, 0)
                    y_out(r, NE // 2 - 1, 1)

        s_yr, s_yc, s_yt, s_yres, s_sq13, s_ss13, s_std13, s_y13 = (sem(n) for n in (
            "y_row_weighted", "y_rows_added", "y_rows_turned", "y_residual", "squares3", "square_sums3",
            "std3", "y_ready"))
        v_link13 = sem("dve_link13")
        s_yrs = [sem(f"y_rows_loaded{i}") for i in range(NR)]
        yr = A.at(a_q, NR, 2 * D)
        sq13 = A.at(a_q + NR * 2 * D, DC, NT)
        rstd13 = A.at(a_q + NR * 2 * D + DC * NT, NT)
        tmp13 = A.at(a_q + NR * 2 * D + DC * NT + NT, NEW)

        with nc.Block() as block:
            @block.sync
            def _(sp):
                for i in range(NR):
                    m = P if i < 4 else NEW
                    sp.dma_start(yr[0:m, i, :], y_rows[2 * i * P:2 * i * P + 2 * m, :].rearrange(
                        "(p w) n -> p (w n)", w=2)).then_inc(s_yrs[i], 16)
                for c in range(DC):
                    sp.wait_ge(s_y13, c + 1)
                    write(sp, outs["y"][:, c, :], sq13[:, c, :])
                sp.wait_ge(s_out, outs_written[0])

            @block.tensor
            def _(pe):
                for i in range(NR):
                    m = P if i < 4 else NEW
                    pe.wait_ge(s_yc, i + 1)
                    if i >= 2:
                        pe.wait_ge(s_yres, i - 1)
                    for c in range(DC):
                        mm = pe.transpose(psum[:, 2 * (i % 2) + c // 4, (c % 4) * P:(c % 4) * P + m],
                                          yr[0:m, i, c * P:c * P + P], const("ident", m)[:, 0:m])
                    mm.then_inc(s_yt, 1)
                for c in range(DC):
                    pe.wait_ge(s_sq13, c + 1)
                    for h in range(2):
                        mm = pe.matmul(pair[2][:, h, :], lhsT=const("ones"),
                                       rhs=sq13[:, c, h * HALF:(h + 1) * HALF],
                                       start=(c == 0), stop=(c == DC - 1))
                mm.then_inc(s_ss13, 1)

            @block.scalar
            def _(act):
                for i in range(NR):
                    m = P if i < 4 else NEW
                    act.wait_ge(s_yrs[i], 16)
                    act.activation(yr[0:m, i, 0:D], yr[0:m, i, 0:D], ACT.Copy,
                                   scale=wcol[0:m, 0, i:i + 1]).then_inc(s_yr, 1)
                act.wait_ge(s_yres, NR)
                for c in range(DC):
                    act.activation(sq13[:, c, :], xT[:, c, :], ACT.Square).then_inc(s_sq13, 1)
                act.wait_ge(s_ss13, 1)
                act.activation(halves(rstd13), pair[2], ACT.Sqrt, bias=eps_col[:, 0:1],
                               scale=1.0 / D).then_inc(s_std13, 1)

            @block.vector
            def _(dve):
                link = Link(dve, v_link13)
                for i in range(NR):
                    m = P if i < 4 else NEW
                    dve.wait_ge(s_yr, i + 1)
                    a, b = yr[0:m, i, 0:D], yr[0:m, i, D:2 * D]
                    dve.scalar_tensor_tensor(a, b, wcol[0:m, 1, i:i + 1], a, ALU.mult,
                                             ALU.add).then_inc(s_yc, 1)
                for i in range(NR):
                    dve.wait_ge(s_yt, i + 1)
                    for c in range(DC):
                        ps = psum[:, 2 * (i % 2) + c // 4, (c % 4) * P:(c % 4) * P + (P if i < 4 else NEW)]
                        if i < 4:
                            dst = xT[:, c, i * P:i * P + P]
                            last = dve.scalar_tensor_tensor(dst, ps, mods[:, 40 + c, 0:1], dst, ALU.mult, ALU.add)
                        else:
                            link(dve.tensor_tensor(by_seq(tmp13), by_seq(ps), per_seq(mods[:, 40 + c, :]),
                                                   ALU.mult))
                            last = dve.tensor_tensor(xT[:, c, SEQ:NT], xT[:, c, SEQ:NT], tmp13, ALU.add)
                            link(last)
                    if i < 4:
                        last.then_inc(s_yres, 1)
                    else:
                        dve.sem_inc(s_yres, 1)
                dve.wait_ge(s_std13, 1)
                link(dve.reciprocal(rstd13, rstd13))
                for c in range(DC):
                    dve.scalar_tensor_tensor(sq13[:, c, :], xT[:, c, :], param("final")[:, c:c + 1], rstd13,
                                             ALU.mult, ALU.mult).then_inc(s_y13, 1)



def inputs_of(x_prompt, x_sample, c_prompt, c_sample, cache_k, cache_v, cache_kidx, state_ssm, state_ssm_conv,
              state_sc_conv, page_table, ada_w, ada_b, norm1_w, norm2_w, w_in, ssm_conv_w, ssm_conv_b,
              ssm_dt_bias, ssm_a_log, ssm_d, ssm_norm_w, sc_conv_w, rel_bias, w_out_ssm, w_out_att, w_out_sc,
              w_o, router_group_w, router_expert_w, exp_w_gate, exp_w_up, exp_w_down, final_norm_w):
    f = lambda a: np.asarray(a)

    def cols(v):
        v = f(v)
        return v.reshape(-1, P).T

    def tiles(w):
        w = f(w)
        return w.reshape(DC, P, -1, P).transpose(2, 1, 0, 3).reshape(-1, P, DC * P)

    wi = f(w_in)[0]

    def cut(at, n):
        return tiles(wi[:, at:at + n])

    ki = wi[:, O_KI:O_KI + D_IDX]
    narrow = np.concatenate([wi[:, O_DT:O_DT + H_SSD], wi[:, O_WI:O_WI + H_IDX],
                             np.zeros((D, P - 24), wi.dtype)], 1)
    c_, h_, b_ = cut(O_GC, D), cut(O_HV, D), cut(O_GB, D)
    gates = [cut(O_GATE + i * D, D) for i in range(3)]
    projections = [tiles(f(w)[0]) for w in (w_out_ssm, w_out_att, w_out_sc)]
    ada = tiles(f(ada_w)[0])
    stream = [ada[:T_KI], tiles(np.concatenate([ki, ki], 1)), cut(O_QI, 512), tiles(narrow),
              cut(O_K, 256), cut(O_V, 256), cut(O_Q, D), cut(O_Z, D), cut(O_XBC, 2048),
              np.stack([c_, h_, b_], 1).reshape(24, P, D), ada[T_KI:],
              np.stack([projections[2], gates[2]], 1).reshape(16, P, D),
              np.stack([projections[1], gates[1]], 1).reshape(16, P, D),
              np.stack([projections[0], gates[0]], 1).reshape(16, P, D),
              tiles(f(w_o)[0])]
    weights = np.concatenate(stream, 0)
    assert weights.shape[0] == T_END

    def feat(a):
        return f(a).reshape(-1, DC, P).transpose(2, 1, 0)

    x = np.concatenate([f(x_prompt).reshape(SEQ, D), f(x_sample).reshape(NEW, D)], 0)
    c = np.concatenate([f(c_prompt), f(c_sample)], 0)
    router = np.concatenate([f(router_group_w)[0], f(router_expert_w)[0]], 1)
    rel = np.zeros((P, H_ATT), np.float32)
    rel[:32] = f(rel_bias)
    part = {
        "ada_b": cols(f(ada_b)[0]), "norm1": cols(f(norm1_w)[0]), "norm2": cols(f(norm2_w)[0]),
        "final": cols(final_norm_w),
        "conv_w": f(ssm_conv_w)[0].reshape(K_SSD, XBC, P).transpose(2, 1, 0).reshape(P, -1),
        "conv_b": cols(f(ssm_conv_b)[0]),
        "sc_w": f(sc_conv_w)[0].reshape(K_SC, 8, P).transpose(2, 1, 0).reshape(P, -1),
        "dt_bias": np.broadcast_to(f(ssm_dt_bias), (P, H_SSD)), "a_log": np.broadcast_to(f(ssm_a_log), (P, H_SSD)),
        "d_skip": cols(np.repeat(f(ssm_d)[0], P_SSD)), "ssm_norm": cols(f(ssm_norm_w)[0]), "rel_bias": rel,
        "c": feat(c).reshape(P, -1), "router": router.reshape(DC, P, 36).transpose(1, 0, 2).reshape(P, -1),
        "conv_prev": f(state_ssm_conv)[0].reshape(NB, 3, XBC, P).transpose(3, 2, 0, 1).reshape(P, -1),
        "sc_prev": f(state_sc_conv)[0].reshape(NB, 2, 8, P).transpose(3, 2, 0, 1).reshape(P, -1),
    }
    params = np.concatenate([part[n] for n in PARAM_AT], 1)
    assert params.shape == (P, PARAM_W)
    ck, cv, ci = f(cache_k)[0], f(cache_v)[0], f(cache_kidx)[0]
    pages_k = ck.transpose(0, 3, 2, 1).reshape(POOL, P, KV * PAGE)
    pages_v = cv.reshape(POOL, PAGE, KV * DH)
    pages_i = ci.transpose(0, 2, 1)
    state = f(state_ssm)[0].transpose(3, 0, 1, 2).reshape(N_SSD, NB * D)
    w_gu = np.stack([f(exp_w_gate)[0], f(exp_w_up)[0]], 1)
    w_gu = w_gu.reshape(NE, 2, DC, P, FF).transpose(0, 3, 1, 2, 4).reshape(NE, P, 2 * DC * FF)
    w_down = f(exp_w_down)[0].reshape(NE, 2, P, D).transpose(0, 2, 1, 3).reshape(NE, P, 2 * D)
    arrays = {"weights": weights, "params": params, "consts": np.concatenate(list(shape_constants().values()), 1),
              "x": feat(x), "pages_k": pages_k, "pages_v": pages_v, "pages_i": pages_i, "state": state,
              "page_table": f(page_table).reshape(1, -1), "w_gu": w_gu, "w_down": w_down}
    return {k: np.ascontiguousarray(v) for k, v in arrays.items()}


OUTS = {"y": (P, DC, NT), "k": (P, 2, NT), "v": (P, 5, 256), "ki": (D_IDX, NT), "ssm_p": (N_SSD, D),
        "conv": (P, XBC, 27), "sc_conv": (P, 8, 18), "ssm_s": (N_SSD, NB * D)}


def launch(nc, arrays):
    ins = {k: nc.dram_tensor(f"in_{k}", a.shape, mybir.dt.from_np(a.dtype), kind="ExternalInput").ap()
           for k, a in arrays.items()}
    outs = {k: nc.dram_tensor(f"out_{k}", s, F32, kind="ExternalOutput").ap() for k, s in OUTS.items()}
    build(nc, ins, outs)


def kernel(**inputs):
    import concourse.bacc as _bacc
    from concourse.bass_utils import run_bass_kernel_spmd as _run

    arrays = inputs_of(**inputs)
    nc = _bacc.Bacc("TRN2", target_bir_lowering=False, num_devices=1)
    launch(nc, arrays)
    r = _run(nc, [{f"in_{k}": a for k, a in arrays.items()}], core_ids=[0]).results[0]
    o = {k: r[f"out_{k}"] for k in OUTS}
    y = o["y"].transpose(2, 1, 0).reshape(NT, D)
    k = o["k"].transpose(2, 1, 0)
    ki = o["ki"].T
    v = o["v"].transpose(1, 0, 2).reshape(5 * P, KV, DH)
    ssm_p = o["ssm_p"].reshape(N_SSD, H_SSD, P_SSD).transpose(1, 2, 0)
    ssm_s = o["ssm_s"].reshape(N_SSD, NB, H_SSD, P_SSD).transpose(1, 2, 3, 0)
    conv = o["conv"].transpose(2, 1, 0).reshape(27, XBC * P)
    sc = o["sc_conv"].transpose(2, 1, 0).reshape(18, D)
    c = np.ascontiguousarray
    return (c(y[:SEQ].reshape(1, SEQ, D)), c(y[SEQ:].reshape(NB, NS, D)),
            c(k[:SEQ].reshape(1, 1, SEQ, KV, DH)), c(v[:SEQ].reshape(1, 1, SEQ, KV, DH)),
            c(ki[:SEQ].reshape(1, 1, SEQ, D_IDX)), c(ssm_p[None, None]), c(conv[:3][None, None]),
            c(sc[:2][None, None]), c(k[SEQ:].reshape(1, NB, NS, KV, DH)),
            c(v[SEQ:SEQ + NEW].reshape(1, NB, NS, KV, DH)), c(ki[SEQ:].reshape(1, NB, NS, D_IDX)),
            c(ssm_s[None]), c(conv[3:].reshape(1, NB, 3, XBC * P)), c(sc[2:].reshape(1, NB, 2, D)))
```
